# Optimizing a Trainium2 kernel written in Bass

```python
import math
import jax, jax.numpy as jnp
from jax import lax
import numpy as np

D_MODEL = 1024
BATCH = 1
SEQ = 2048
DEPTH = 1

MEM_LEN = 256
EPS = 1e-6
D_MIX = D_MODEL
RET_W = D_MIX // 4
RET_HEADS = 4
RET_HEAD_DIM = RET_W // RET_HEADS
RET_CHUNK = 128
ROPE_BASE = 10000.0
SSD_W = D_MIX // 2
SSD_HEAD_DIM = 64
SSD_HEADS = SSD_W // SSD_HEAD_DIM
SSD_GROUPS = 2
SSD_STATE = 128
SSD_CONV = 4
SSD_CHUNK = 128
SSD_XBC_W = SSD_W + 2 * SSD_GROUPS * SSD_STATE
S5_W = D_MIX - RET_W - SSD_W
S5_GROUP = 16
S5_GROUPS = S5_W // S5_GROUP
S5_STATE = 64
IN_SIZES = (RET_W, RET_W, RET_W, RET_W, SSD_W, SSD_XBC_W, SSD_HEADS, S5_W)
IN_COLS = RET_W * 4 + SSD_W + SSD_XBC_W + SSD_HEADS + S5_W
CROSS_HEADS = 4
CROSS_HEAD_DIM = D_MODEL // CROSS_HEADS
MOE_GROUPS = 4
EXPERTS_PER_GROUP = 8
N_EXPERTS = MOE_GROUPS * EXPERTS_PER_GROUP
TOP_K_INNER = 2
D_EXPERT = D_MODEL // 2
MOE_BLOCK = 128

kernel_name = "hybrid_ret_ssd_s5_hmoe"

F32 = jnp.float32

def rmsnorm(x, g):
    xf = x.astype(F32)
    y = xf * lax.rsqrt(jnp.mean(xf * xf, axis=-1, keepdims=True) + EPS)
    return (y * g.astype(F32)).astype(x.dtype)

def rotary(t):
    L, d = t.shape[1], t.shape[-1]
    inv = ROPE_BASE ** (-jnp.arange(0, d, 2, dtype=F32) / d)
    ang = jnp.arange(L, dtype=F32)[:, None] * inv[None, :]
    cos = jnp.cos(ang)[None, :, None, :]
    sin = jnp.sin(ang)[None, :, None, :]
    t1, t2 = t[..., : d // 2].astype(F32), t[..., d // 2:].astype(F32)
    return jnp.concatenate([t1 * cos - t2 * sin, t1 * sin + t2 * cos], axis=-1)

def retention(q, k, v):
    b, L, H, dh = q.shape
    C = RET_CHUNK
    nc = L // C
    lg = jnp.log1p(-(2.0 ** (-5.0 - jnp.arange(H, dtype=F32))))
    q = rotary(q)
    k = rotary(k) * (dh ** -0.5)

    def chunks(t):
        return t.reshape(b, nc, C, H, dh).transpose(0, 3, 1, 2, 4)

    qc, kc, vc = chunks(q), chunks(k), chunks(v.astype(F32))
    i = jnp.arange(C, dtype=F32)
    rel = i[:, None] - i[None, :]
    decay = jnp.where(rel[None] >= 0, jnp.exp(lg[:, None, None] * jnp.maximum(rel, 0.0)[None]), 0.0)
    s = jnp.einsum('bhcid,bhcjd->bhcij', qc, kc) * decay[None, :, None]
    y_in = jnp.einsum('bhcij,bhcjd->bhcid', s, vc)
    k_dec = kc * jnp.exp(lg[:, None] * (C - 1.0 - i)[None])[None, :, None, :, None]
    kv = jnp.einsum('bhcjd,bhcje->bhcde', k_dec, vc)
    chunk_decay = jnp.exp(lg * C)[None, :, None, None]

    def step(S, kv_c):
        return S * chunk_decay + kv_c, S

    _, S_prev = lax.scan(step, jnp.zeros_like(kv[:, :, 0]), kv.transpose(2, 0, 1, 3, 4))
    S_prev = S_prev.transpose(1, 2, 0, 3, 4)
    q_dec = qc * jnp.exp(lg[:, None] * (i + 1.0)[None])[None, :, None, :, None]
    y_x = jnp.einsum('bhcid,bhcde->bhcie', q_dec, S_prev)
    return (y_in + y_x).transpose(0, 2, 3, 1, 4).reshape(b, L, H, dh)

def ssd_mixer(z, xbc, dt_raw, conv_w, conv_b, dt_bias, A_log, D, norm_g):
    b, L, _ = xbc.shape
    xpad = jnp.pad(xbc, ((0, 0), (SSD_CONV - 1, 0), (0, 0)))
    conv = conv_b
    for j in range(SSD_CONV):
        conv = conv + xpad[:, j:j + L] * conv_w[j]
    xbc = jax.nn.silu(conv)
    xs = xbc[..., :SSD_W]
    Bm = xbc[..., SSD_W:SSD_W + SSD_GROUPS * SSD_STATE]
    Cm = xbc[..., SSD_W + SSD_GROUPS * SSD_STATE:]
    G, R, P, N = SSD_GROUPS, SSD_HEADS // SSD_GROUPS, SSD_HEAD_DIM, SSD_STATE
    C = SSD_CHUNK
    nc = L // C
    x = xs.astype(F32).reshape(b, nc, C, G, R, P)
    Bc = Bm.astype(F32).reshape(b, nc, C, G, N)
    Cc = Cm.astype(F32).reshape(b, nc, C, G, N)
    dt = jax.nn.softplus((dt_raw + dt_bias).astype(F32)).reshape(b, nc, C, G, R)
    A = -jnp.exp(A_log.astype(F32)).reshape(G, R)
    A_cum = jnp.cumsum(dt * A, axis=2)
    Acum_t = A_cum.transpose(0, 1, 3, 4, 2)
    diff = Acum_t[..., :, None] - Acum_t[..., None, :]
    causal = jnp.tril(jnp.ones((C, C), dtype=bool))
    Lmat = jnp.exp(jnp.where(causal, diff, -jnp.inf))
    CB = jnp.einsum('bclgn,bcsgn->bcgls', Cc, Bc)
    xdt = x * dt[..., None]
    y_diag = jnp.einsum('bcgrls,bcsgrp->bclgrp', CB[:, :, :, None] * Lmat, xdt)
    decay_states = jnp.exp(A_cum[:, :, -1:] - A_cum)
    states = jnp.einsum('bclgn,bclgrp->bcgrpn', Bc, xdt * decay_states[..., None])
    chunk_decay = jnp.exp(A_cum[:, :, -1])

    def step(S, inp):
        st, dc = inp
        return S * dc[..., None, None] + st, S

    _, S_prev = lax.scan(step, jnp.zeros((b, G, R, P, N), F32),
                         (states.transpose(1, 0, 2, 3, 4, 5), chunk_decay.transpose(1, 0, 2, 3)))
    S_prev = S_prev.transpose(1, 0, 2, 3, 4, 5)
    y_off = jnp.einsum('bclgn,bcgrpn->bclgrp', Cc, S_prev) * jnp.exp(A_cum)[..., None]
    y = y_diag + y_off + x * D.astype(F32).reshape(G, R)[..., None]
    y = y.reshape(b, L, SSD_W)
    return rmsnorm(y * jax.nn.silu(z.astype(F32)), norm_g)

def _complex_affine_combine(e1, e2):
    a1r, a1i, b1r, b1i = e1
    a2r, a2i, b2r, b2i = e2
    return (a2r * a1r - a2i * a1i,
            a2r * a1i + a2i * a1r,
            a2r * b1r - a2i * b1i + b2r,
            a2r * b1i + a2i * b1r + b2i)

def s5_mixer(u, A_re, A_im, B_re, B_im, C_re, C_im, log_step, D, w_glu, b_glu):
    b, L, _ = u.shape
    ug = u.astype(F32).reshape(b, L, S5_GROUPS, S5_GROUP)
    delta = jnp.exp(log_step.astype(F32))[:, None]
    ar, ai = A_re.astype(F32), A_im.astype(F32)
    mag = jnp.exp(ar * delta)
    ang = ai * delta
    lr, li = mag * jnp.cos(ang), mag * jnp.sin(ang)
    den = ar * ar + ai * ai
    nr, ni = lr - 1.0, li
    cr = (nr * ar + ni * ai) / den
    ci = (ni * ar - nr * ai) / den
    br, bi = B_re.astype(F32), B_im.astype(F32)
    Bbr = cr[..., None] * br - ci[..., None] * bi
    Bbi = cr[..., None] * bi + ci[..., None] * br
    bu_r = jnp.einsum('blgc,gpc->blgp', ug, Bbr)
    bu_i = jnp.einsum('blgc,gpc->blgp', ug, Bbi)
    a_r = jnp.broadcast_to(lr, bu_r.shape)
    a_i = jnp.broadcast_to(li, bu_r.shape)
    _, _, xr, xi = lax.associative_scan(_complex_affine_combine, (a_r, a_i, bu_r, bu_i), axis=1)
    y = (jnp.einsum('gcp,blgp->blgc', C_re.astype(F32), xr)
         - jnp.einsum('gcp,blgp->blgc', C_im.astype(F32), xi))
    y = y.reshape(b, L, S5_W) + D.astype(F32) * u.astype(F32)
    g = jax.nn.gelu(y)
    return g * jax.nn.sigmoid(g @ w_glu.astype(F32) + b_glu.astype(F32))

def hybrid_mixer(hn, w_in, ret_gn_g, ssd_conv_w, ssd_conv_b, ssd_dt_bias, ssd_A_log, ssd_D, ssd_norm_g,
                 s5_A_re, s5_A_im, s5_B_re, s5_B_im, s5_C_re, s5_C_im, s5_log_step, s5_D, s5_w_glu, s5_b_glu,
                 w_out):
    b, L, _ = hn.shape
    proj = hn @ w_in
    splits = [int(s) for s in np.cumsum(IN_SIZES)[:-1]]
    q, k, v, g, z, xbc, dt_raw, u = jnp.split(proj, splits, axis=-1)
    shp = (b, L, RET_HEADS, RET_HEAD_DIM)
    yr = retention(q.reshape(shp), k.reshape(shp), v.reshape(shp))
    yr = yr * lax.rsqrt(jnp.mean(yr * yr, axis=-1, keepdims=True) + EPS)
    out_r = jax.nn.silu(g.astype(F32)) * (yr.reshape(b, L, RET_W) * ret_gn_g.astype(F32))
    out_m = ssd_mixer(z, xbc, dt_raw, ssd_conv_w, ssd_conv_b, ssd_dt_bias, ssd_A_log, ssd_D, ssd_norm_g)
    out_s = s5_mixer(u, s5_A_re, s5_A_im, s5_B_re, s5_B_im, s5_C_re, s5_C_im, s5_log_step, s5_D,
                     s5_w_glu, s5_b_glu)
    cat = jnp.concatenate([out_r, out_m.astype(F32), out_s], axis=-1).astype(hn.dtype)
    return cat @ w_out

def cross_attend(hn, mn, wq, wk, wv, wo):
    b, L, _ = hn.shape
    q = (hn @ wq).reshape(b, L, CROSS_HEADS, CROSS_HEAD_DIM)
    k = (mn @ wk).reshape(b, MEM_LEN, CROSS_HEADS, CROSS_HEAD_DIM)
    v = (mn @ wv).reshape(b, MEM_LEN, CROSS_HEADS, CROSS_HEAD_DIM)
    s = jnp.einsum('blhd,bmhd->bhlm', q, k).astype(F32) * (CROSS_HEAD_DIM ** -0.5)
    p = jax.nn.softmax(s, axis=-1).astype(v.dtype)
    o = jnp.einsum('bhlm,bmhd->blhd', p, v).reshape(b, L, D_MODEL)
    return o @ wo

def hier_moe(xn, w_rg, b_rg, w_re, b_re, w_gate, w_up, w_down):
    T, d = xn.shape
    glog = (xn @ w_rg + b_rg).astype(F32)
    gsel = jnp.argmax(glog, axis=-1)
    pg = jnp.take_along_axis(jax.nn.softmax(glog, axis=-1), gsel[:, None], axis=-1)
    elog = (xn @ w_re + b_re).astype(F32).reshape(T, MOE_GROUPS, EXPERTS_PER_GROUP)
    elog = jnp.take_along_axis(elog, gsel[:, None, None], axis=1)[:, 0]
    top_p, top_i = lax.top_k(jax.nn.softmax(elog, axis=-1), TOP_K_INNER)
    gate = pg * top_p / jnp.sum(top_p, axis=-1, keepdims=True)
    expert = gsel[:, None] * EXPERTS_PER_GROUP + top_i
    flat_e = expert.reshape(-1)
    flat_t = jnp.repeat(jnp.arange(T), TOP_K_INNER)
    flat_w = gate.reshape(-1)
    M = T * TOP_K_INNER
    order = jnp.argsort(flat_e)
    se, st, sw = flat_e[order], flat_t[order], flat_w[order]
    counts = jnp.bincount(flat_e, length=N_EXPERTS)
    starts = jnp.cumsum(counts) - counts
    padded = (counts + MOE_BLOCK - 1) // MOE_BLOCK * MOE_BLOCK
    pends = jnp.cumsum(padded)
    pstarts = pends - padded
    dest = pstarts[se] + jnp.arange(M) - starts[se]
    nb = -(-M // MOE_BLOCK) + N_EXPERTS
    buf = jnp.zeros((nb * MOE_BLOCK, d), xn.dtype).at[dest].set(xn[st])
    block_e = jnp.minimum(jnp.searchsorted(pends, jnp.arange(nb) * MOE_BLOCK, side='right'), N_EXPERTS - 1)

    def expert_block(args):
        xb, e = args
        h = jax.nn.silu(xb @ w_gate[e]) * (xb @ w_up[e])
        return h @ w_down[e]

    ybuf = lax.map(expert_block, (buf.reshape(nb, MOE_BLOCK, d), block_e)).reshape(nb * MOE_BLOCK, d)
    y = ybuf[dest].astype(F32) * sw[:, None]
    return jax.ops.segment_sum(y, st, num_segments=T).astype(xn.dtype)

def setup_inputs(seed: int = 0) -> dict:
    key = jax.random.key(seed)
    ks = iter(jax.random.split(key, 48))

    def nrm(shape, scale):
        return jax.random.normal(next(ks), shape, F32) * scale

    def unif(shape, lo, hi):
        return jax.random.uniform(next(ks), shape, F32, lo, hi)

    def gain(shape):
        return 1.0 + nrm(shape, 0.02)

    x = nrm((BATCH, SEQ, D_MODEL), 1.0)
    mem = nrm((BATCH, MEM_LEN, D_MODEL), 1.0)
    dt0 = jnp.exp(unif((DEPTH, SSD_HEADS), math.log(1e-3), math.log(1e-1)))
    n_idx = jnp.arange(S5_STATE, dtype=F32)
    return {
        'x': x,
        'mem': mem,
        'norm_mix_g': gain((DEPTH, D_MODEL)),
        'w_in': nrm((DEPTH, D_MODEL, IN_COLS), D_MODEL ** -0.5),
        'ret_gn_g': gain((DEPTH, RET_W)),
        'ssd_conv_w': nrm((DEPTH, SSD_CONV, SSD_XBC_W), SSD_CONV ** -0.5),
        'ssd_conv_b': nrm((DEPTH, SSD_XBC_W), 0.02),
        'ssd_dt_bias': dt0 + jnp.log(-jnp.expm1(-dt0)),
        'ssd_A_log': jnp.log(unif((DEPTH, SSD_HEADS), 1.0, 16.0)),
        'ssd_D': gain((DEPTH, SSD_HEADS)),
        'ssd_norm_g': gain((DEPTH, SSD_W)),
        's5_A_re': -0.5 + nrm((DEPTH, S5_GROUPS, S5_STATE), 0.01),
        's5_A_im': math.pi * n_idx + nrm((DEPTH, S5_GROUPS, S5_STATE), 0.01),
        's5_B_re': nrm((DEPTH, S5_GROUPS, S5_STATE, S5_GROUP), (2 * S5_GROUP) ** -0.5),
        's5_B_im': nrm((DEPTH, S5_GROUPS, S5_STATE, S5_GROUP), (2 * S5_GROUP) ** -0.5),
        's5_C_re': nrm((DEPTH, S5_GROUPS, S5_GROUP, S5_STATE), (2 * S5_STATE) ** -0.5),
        's5_C_im': nrm((DEPTH, S5_GROUPS, S5_GROUP, S5_STATE), (2 * S5_STATE) ** -0.5),
        's5_log_step': unif((DEPTH, S5_GROUPS), math.log(1e-3), math.log(1e-1)),
        's5_D': nrm((DEPTH, S5_W), 0.5),
        's5_w_glu': nrm((DEPTH, S5_W, S5_W), S5_W ** -0.5),
        's5_b_glu': nrm((DEPTH, S5_W), 0.02),
        'w_out': nrm((DEPTH, D_MIX, D_MODEL), D_MIX ** -0.5),
        'norm_cross_g': gain((DEPTH, D_MODEL)),
        'mem_norm_g': gain((D_MODEL,)),
        'w_cq': nrm((DEPTH, D_MODEL, D_MODEL), D_MODEL ** -0.5),
        'w_ck': nrm((DEPTH, D_MODEL, D_MODEL), D_MODEL ** -0.5),
        'w_cv': nrm((DEPTH, D_MODEL, D_MODEL), D_MODEL ** -0.5),
        'w_co': nrm((DEPTH, D_MODEL, D_MODEL), D_MODEL ** -0.5),
        'norm_ffn_g': gain((DEPTH, D_MODEL)),
        'w_route_group': nrm((DEPTH, D_MODEL, MOE_GROUPS), D_MODEL ** -0.5),
        'b_route_group': nrm((DEPTH, MOE_GROUPS), 0.01),
        'w_route_expert': nrm((DEPTH, D_MODEL, N_EXPERTS), D_MODEL ** -0.5),
        'b_route_expert': nrm((DEPTH, N_EXPERTS), 0.01),
        'w_gate': nrm((DEPTH, N_EXPERTS, D_MODEL, D_EXPERT), D_MODEL ** -0.5),
        'w_up': nrm((DEPTH, N_EXPERTS, D_MODEL, D_EXPERT), D_MODEL ** -0.5),
        'w_down': nrm((DEPTH, N_EXPERTS, D_EXPERT, D_MODEL), D_EXPERT ** -0.5),
        'norm_final_g': gain((D_MODEL,)),
    }

def reference(x, mem, norm_mix_g, w_in, ret_gn_g, ssd_conv_w, ssd_conv_b, ssd_dt_bias, ssd_A_log, ssd_D,
              ssd_norm_g, s5_A_re, s5_A_im, s5_B_re, s5_B_im, s5_C_re, s5_C_im, s5_log_step, s5_D, s5_w_glu,
              s5_b_glu, w_out, norm_cross_g, mem_norm_g, w_cq, w_ck, w_cv, w_co, norm_ffn_g, w_route_group,
              b_route_group, w_route_expert, b_route_expert, w_gate, w_up, w_down, norm_final_g):
    b, L, d = x.shape
    h = x
    mn = rmsnorm(mem, mem_norm_g)
    for i in range(DEPTH):
        hn = rmsnorm(h, norm_mix_g[i])
        h = h + hybrid_mixer(hn, w_in[i], ret_gn_g[i], ssd_conv_w[i], ssd_conv_b[i], ssd_dt_bias[i],
                             ssd_A_log[i], ssd_D[i], ssd_norm_g[i], s5_A_re[i], s5_A_im[i], s5_B_re[i],
                             s5_B_im[i], s5_C_re[i], s5_C_im[i], s5_log_step[i], s5_D[i], s5_w_glu[i],
                             s5_b_glu[i], w_out[i]).astype(h.dtype)
        hn = rmsnorm(h, norm_cross_g[i])
        h = h + cross_attend(hn, mn, w_cq[i], w_ck[i], w_cv[i], w_co[i]).astype(h.dtype)
        hn = rmsnorm(h, norm_ffn_g[i]).reshape(b * L, d)
        h = h + hier_moe(hn, w_route_group[i], b_route_group[i], w_route_expert[i], b_route_expert[i],
                         w_gate[i], w_up[i], w_down[i]).reshape(b, L, d).astype(h.dtype)
    return rmsnorm(h, norm_final_g)


_drawn_inputs = setup_inputs


def setup_inputs(seed=0):
    import zlib

    import numpy as np

    out = dict(_drawn_inputs(seed))
    spreads = {}
    factors = {'ret_gn_g': 4.782,
     'ssd_D': 3.704,
     'ssd_norm_g': 2.714,
     's5_A_re': 64.0,
     's5_A_im': 27.104,
     's5_B_re': 32.528,
     's5_B_im': 37.48,
     's5_C_re': 31.512,
     's5_C_im': 31.984,
     's5_log_step': 27.84,
     's5_w_glu': 3.061,
     's5_b_glu': 34.108,
     'norm_cross_g': 8.0,
     'mem_norm_g': 6.017,
     'b_route_group': 34.712,
     'b_route_expert': 41.856,
     'norm_final_g': 7.201,
     'norm_ffn_g': 8.0}
    for name, (base, spread) in spreads.items():
        noise = np.random.default_rng([zlib.crc32(name.encode()), seed]).standard_normal(out[name].shape)
        drawn = base * np.exp(spread * noise) if base else spread * noise
        out[name] = __import__('jax').numpy.asarray(drawn.astype(out[name].dtype))
    for name, factor in factors.items():
        out[name] = (out[name] * factor).astype(out[name].dtype)
    return out
```

```python
from contextlib import ExitStack

import concourse.bass as bass
from concourse import mybir
import numpy as np

F32 = mybir.dt.float32
F16 = mybir.dt.float16
I32 = mybir.dt.int32
U32 = mybir.dt.uint32
ALU = mybir.AluOpType
ACT = mybir.ActivationFunctionType
AX = mybir.AxisListType

P = 128
D = 1024
KT = D // P
T = 2048
NCH = T // P
GC = 4
NG = NCH // GC
GT = GC * P
EPS = 1e-6
RH, RD = 4, 64
RW = RH * RD
SH, SP_, SN = 8, 64, 128
SW = SH * SP_
XBC = SW + 4 * SN
S5G, S5C, S5P = 16, 16, 64
S5W = S5G * S5C
COLS = 4 * RW + SW + XBC + SH + S5W
C_VG, C_Z, C_XBC, C_DT = 2 * RW, 4 * RW, 4 * RW + SW, 4 * RW + SW + XBC
MEM = 256
NE, NGR, EPG, DE = 32, 4, 8, 512
NB = 2 * T // P + NE
USED_MIN = 2 * T // P

W_SCALE, N_SCALE = 2.0 ** 9, 2.0 ** 5
UNSCALE = 1.0 / (W_SCALE * N_SCALE)

K_ID, K_LE, K_GT, K_ONE, K_LT, K_IOTA = 0, 128, 256, 384, 512, 640
K_TOK = K_IOTA + P
K_GAM = K_TOK + NCH
K_HALF = K_GAM + 2 * RD
K_END = K_HALF + 64


def constants():
    c = np.zeros((P, K_END), np.float32)
    i = np.arange(P)
    c[:, K_ID:K_ID + P] = np.eye(P)
    c[:, K_LE:K_LE + P] = i[:, None] <= i[None, :]
    c[:, K_GT:K_GT + P] = i[:, None] > i[None, :]
    c[:, K_ONE:K_ONE + P] = 1
    c[:, K_LT:K_LT + P] = i[:, None] < i[None, :]
    c[:, K_IOTA:K_IOTA + P] = i
    c[:, K_TOK:K_TOK + NCH] = np.arange(NCH)[None, :] * P + i[:, None]
    gamma = 1.0 - 2.0 ** (-5.0 - np.arange(RH))
    for j in range(RH // 2):
        for half in range(2):
            c[half * 64:half * 64 + 64, K_GAM + j * RD:K_GAM + (j + 1) * RD] = gamma[2 * j + half] ** P
    c[:, K_HALF:K_HALF + 64] = -0.5
    half = RD // 2
    inv = (np.float32(10000.0) ** (-np.arange(0, RD, 2, dtype=np.float32) / np.float32(RD))).astype(np.float32)
    ang = (np.arange(T, dtype=np.float32)[:, None] * inv[None, :]).astype(np.float32).astype(np.float64)
    pos = (np.arange(T) % P + 1.0)[:, None]
    fold = np.concatenate([gamma[None, :] ** pos, gamma[None, :] ** -pos * RD ** -0.5], 1)
    rope = np.stack([fold[:, :, None] * np.cos(ang)[:, None, :], fold[:, :, None] * np.sin(ang)[:, None, :]], 1)
    rope *= UNSCALE
    return c, rope.reshape(T, 2 * 2 * RH * half).astype(np.float32)


def bc(ap, axis, n):
    a = ap.unsqueeze(axis)
    s = list(a.shape)
    s[axis] = n
    return a.to_broadcast(s)


def halves(t):
    a, b = list(t[:, :, :].shape)[1:]
    v = t[:, :, :].bitcast(F16).rearrange("p a b -> p (a b)").rearrange("p (h a b) -> p h a b", h=2, a=a)
    return v[:, 0], v[:, 1]


def products(pe, o, a, b, start=True, stop=True):
    n = len(a[0])
    for k in range(n):
        for j, (x, y) in enumerate(((0, 0), (0, 1), (1, 0))):
            ins = pe.matmul(o, a[x][k], b[y][k], start=start and k == 0 and j == 0, stop=stop and k == n - 1 and j == 2)
    return ins


class Chain:

    def __init__(self, eng, sem, turn=0, per=0):
        self.eng, self.sem, self.turn, self.per, self.n = eng, sem, turn, per, 0

    def post(self, ins):
        ins.then_inc(self.sem, 1)
        self.n += 1

    def wait(self, n=None):
        k = self.n if n is None else n
        self.eng.wait_ge(self.sem, self.turn * self.per + k if self.per else k)


def mixer_projections(nc, env, dram):
    x, w_in, cat, u_scr = dram["x"], dram["w_in"][0], dram["cat"], dram["u_scr"]
    BIG = 2 * KT + 3 * GC
    SML = 12
    DVE_TURN = env["dve_a"]
    with ExitStack() as ctx:
        def sb(name, shape, dt=F32):
            return ctx.enter_context(nc.sbuf_tensor(name, shape, dt))

        held = []

        def sem(name):
            held.append(nc.alloc_semaphore(name))
            return held[-1]

        wi = sb("wi", [P, 2, KT, COLS], F16)
        cst = sb("cst_a", [P, K_IOTA])
        gam = sb("gam", [P, 2 * RD])
        nhalf = sb("nhalf", [P, 64])
        gmix = sb("gmix", [P, KT])
        gn_bc = sb("gn_bc", [P, RW])
        ng_bc = sb("ng_bc", [P, SW])
        dtb_bc = sb("dtb_bc", [P, SH])
        a_bc = sb("a_bc", [P, SH])
        d_bc = sb("d_bc", [P, SH])
        cw = sb("cw", [P, 4, KT])
        cb = sb("cb", [P, KT])
        xg = sb("xg", [P, GC, D])
        ss = sb("ss_a", [P, GC])
        ms = sb("ms_a", [P, GC])
        rstd = sb("rstd_a", [P, GC])
        hnT = sb("hnT", [P, KT, GT])
        hn_s = halves(hnT)
        gmix_s = sb("gmix_s", [P, KT])
        junk = hnT[:, 6:8, :].rearrange("p a b -> p (a b)")
        PT = hnT[:, 0, :].rearrange("p (a b) -> p a b", a=RH)
        kT = hnT[:, 1, 0:2 * P].rearrange("p (a b) -> p a b", a=2)
        xdt = hnT[:, 2, :].rearrange("p (a b) -> p a b", a=SH)
        xtok = hnT[:, 3, :].rearrange("p (a b) -> p a b", a=SH)
        xbcT = sb("xbcT", [P, 2, GT + 3])
        hist = sb("hist", [P, KT, 3])
        xc = sb("xc", [P, KT, GT])
        vb = sb("vb", [P, GC, RW])
        gs = sb("gs", [P, GC, RW])
        dtu = sb("dtu", [P, GC, SH + S5W])
        qr = sb("qr", [P, GC, 2 * RW])
        rope = sb("rope_t", [P, GC, 2 * RW])
        Y = sb("Y", [P, GC, RW + SW])
        HC, ROOMS = COLS // 2, 4
        stage = [t[:, :, :].rearrange("p a b -> p (a b)")[:, h * HC:(h + 1) * HC] for t in (Y, xc) for h in range(2)]
        pieces = [(kt, slice(h * HC, (h + 1) * HC), (2 * kt + h) % ROOMS, (2 * kt + h) // ROOMS) for kt in range(KT) for h in range(2)]
        dts = sb("dts", [P, 8, GC, SH])
        qz = sb("qz", [P, 2, 2, P])
        btok = sb("btok", [P, 2, SN])
        dec = sb("dec", [P, 3, SH])
        E = sb("E", [P, SH, P])
        AB = E[:, :, :].rearrange("p (a h) l -> p a (h l)", a=2)
        segin = sb("segin", [P, SH, P])
        sg2 = segin[:, :, :].rearrange("p (a h) l -> p a (h l)", a=2)
        yo, xdec = sg2[:, 0, :], sg2[:, 1, :]
        cbm = sb("cbm", [P, 2, P])
        S_r = sb("S_r", [P, 2, RD])
        S_m = sb("S_m", [P, SH, SP_])
        sso = sb("sso", [P, 5 * GC])
        mso = sb("mso", [P, 5 * GC])
        rso = sb("rso", [P, 5 * GC])
        bank = [ctx.enter_context(nc.psum_tensor(f"bankA{i}", [P, 512], F32)) for i in range(8)]
        ident, le, gt, ones = (cst[:, k:k + P] for k in (K_ID, K_LE, K_GT, K_ONE))
        dt_, dtA = dts[:, 6, :, :], dts[:, 7, :, :]

        w_ld = [sem(f"w_in_loaded{i}") for i in range(ROOMS)]
        w_hi, w_lo, hn_lo = sem("w_in_nearest"), sem("w_in_rest"), sem("hn_rest")
        c_ld, x_ld, r_ld = sem("consts_a_loaded"), sem("x_loaded"), sem("rope_loaded")
        a_set, s_set = sem("ssd_A_set"), sem("states_zeroed")
        sq_done, ms_done, rs_done, xs_done = sem("squares_a"), sem("mean_a"), sem("rstd_a_ready"), sem("xs_ready")
        big, taken, qk_done, qk_free = sem("big_done"), sem("big_taken"), sem("qk_done"), sem("rope_done")
        conv_done, silu_done, hist_done = sem("conv_done"), sem("conv_silu"), sem("history_kept")
        small, s_act, s_dve = sem("small_done"), sem("small_taken_act"), sem("small_taken_dve")
        dt_ready, ax_ready, e_ready, w_ready, ln_ready = (sem("dt_ready"), sem("dt_abs"), sem("dt_exp"),
                                                          sem("dt_exp1"), sem("dt_ln"))
        seg_ready = sem("segin_ready")
        ch_done, mo_done, ro_done, out_done = sem("chunk_done"), sem("mean_out"), sem("rstd_out"), sem("out_ready")
        u_ready, u_st, cat_st = sem("u_ready"), sem("u_stored"), sem("cat_stored")
        dve_s = sem("dve_steps_a")

        BY = ["act", "act", "act", "act", "act", "dve", "dve", "dve", "dve", "dve", "dve", "dve"]
        N_ACT, N_DVE = BY.count("act"), BY.count("dve")
        SB0 = 5

        ctx.enter_context(nc.allow_non_contiguous_dma(reason="gains by rows, loaded once"))
        block = ctx.enter_context(nc.Block())

        @block.sync
        def _(sp):
            xv = x[0].rearrange("(g c p) d -> g p c d", c=GC, p=P)
            rv = dram["rope"].rearrange("(g c p) d -> g p c d", c=GC, p=P)
            catv = cat.rearrange("(g c p) d -> g p c d", c=GC, p=P)
            uv = u_scr.rearrange("(g c p) d -> g p c d", c=GC, p=P)
            sp.dma_start(xg[:, :, :], xv[0]).then_inc(x_ld, 16)
            sp.dma_start(cst[:, :], dram["cst"][:, 0:K_IOTA]).then_inc(c_ld, 16)
            sp.dma_start(gam[:, :], dram["cst"][:, K_GAM:K_GAM + 2 * RD]).then_inc(c_ld, 16)
            sp.dma_start(nhalf[:, :], dram["cst"][:, K_HALF:K_HALF + 64]).then_inc(c_ld, 16)
            sp.dma_start(gmix[:, :], dram["norm_mix_g"][0].rearrange("(k p) -> p k", p=P)).then_inc(c_ld, 16)
            sp.dma_start(gn_bc[:, :], dram["ret_gn_g"][0].partition_broadcast(P)).then_inc(c_ld, 16)
            sp.dma_start(ng_bc[:, :], dram["ssd_norm_g"][0].partition_broadcast(P)).then_inc(c_ld, 16)
            sp.dma_start(dtb_bc[:, :], dram["ssd_dt_bias"][0].partition_broadcast(P)).then_inc(c_ld, 16)
            sp.dma_start(a_bc[:, :], dram["ssd_A_log"][0].partition_broadcast(P)).then_inc(c_ld, 16)
            sp.dma_start(d_bc[:, :], dram["ssd_D"][0].partition_broadcast(P)).then_inc(c_ld, 16)
            for j in range(4):
                sp.dma_start(cw[:, j, :], dram["ssd_conv_w"][0, j].rearrange("(k p) -> p k", p=P)).then_inc(c_ld, 16)
            sp.dma_start(cb[:, :], dram["ssd_conv_b"][0].rearrange("(k p) -> p k", p=P)).then_inc(c_ld, 16)
            for n, (kt, cols, room, before) in enumerate(pieces):
                if before:
                    sp.wait_ge(w_hi, n - ROOMS + 1)
                    sp.wait_ge(w_lo, n - ROOMS + 1)
                sp.dma_start(stage[room], w_in[kt * P:(kt + 1) * P, cols]).then_inc(w_ld[room], 16)
            sp.dma_start(rope[:, :, :], rv[0]).then_inc(r_ld, 16)

            def stores(g, at):
                sp.wait_ge(u_ready, g * GC + GC)
                sp.dma_start(uv[at], dtu[:, :, SH:]).then_inc(u_st, 16)
                sp.wait_ge(out_done, g * 2 + 2)
                sp.dma_start(catv[at][:, :, 0:RW + SW], Y[:, :, :]).then_inc(cat_st, 16)

            with sp.Fori(0, NG - 1) as g:
                sp.wait_ge(big, g * BIG + KT)
                sp.dma_start(xg[:, :, :], xv[bass.ds(g + 1, 1)].squeeze(0)).then_inc(x_ld, 16)
                sp.wait_ge(qk_free, g * GC + GC)
                sp.dma_start(rope[:, :, :], rv[bass.ds(g + 1, 1)].squeeze(0)).then_inc(r_ld, 16)
                sp.wait_ge(u_ready, g * GC + GC)
                sp.dma_start(uv[bass.ds(g, 1)].squeeze(0), dtu[:, :, SH:]).then_inc(u_st, 16)
                sp.wait_ge(out_done, g * 2 + 2)
                sp.dma_start(catv[bass.ds(g, 1)].squeeze(0)[:, :, 0:RW + SW], Y[:, :, :]).then_inc(cat_st, 16)
            stores(NG - 1, NG - 1)
            sp.wait_ge(u_st, 16 * NG)
            sp.wait_ge(cat_st, 16 * NG)

        @block.gpsimd
        def _(pool):
            pool.memset(S_r[:, :, :], 0.0).then_inc(s_set, 1)
            pool.memset(S_m[:, :, :], 0.0).then_inc(s_set, 1)
            pool.memset(hist[:, :, :], 0.0).then_inc(s_set, 1)
            pool.memset(qz[:, :, :, :], 0.0).then_inc(s_set, 1)
            pool.wait_ge(c_ld, 16 * 14)
            with pool.Fori(0, NG) as g:
                pool.wait_ge(ms_done, g + 1)
                pool.tensor_tensor(rstd[:, :], ms[:, :], nhalf[:, 0:GC], ALU.pow).then_inc(rs_done, 1)
                pool.wait_ge(mo_done, g * 2 + 2)
                pool.tensor_tensor(rso[:, :], mso[:, :], nhalf[:, 0:5 * GC], ALU.pow).then_inc(ro_done, 1)

        @block.scalar
        def _(act):
            act.wait_ge(c_ld, 16 * 14)
            act.wait_ge(s_set, 4)
            act.activation(a_bc[:, :], a_bc[:, :], ACT.Exp).then_inc(a_set, 1)
            for kt, cols, room, before in pieces:
                act.wait_ge(w_ld[room], before * 16 + 16)
                act.activation(wi[:, 0, kt, cols], stage[room], ACT.Copy, scale=W_SCALE).then_inc(w_hi, 1)
            act.wait_ge(w_lo, len(pieces))
            act.wait_ge(a_set, 3)
            with act.Fori(0, NG) as g:
                act.wait_ge(x_ld, g * 16 + 16)
                for c in range(GC):
                    if c == 0:
                        act.wait_ge(ms_done, g)
                    act.wait_ge(sq_done, g * GC + c)
                    act.activation(junk, xg[:, c, :], ACT.Square, accum_out=ss[:, c:c + 1]).then_inc(sq_done, 1)
                n = 0
                for kt in range(KT):
                    act.wait_ge(big, g * BIG + n + 1)
                    act.activation(hn_s[0][:, kt, :], bank[n % 4][:, :], ACT.Copy, scale=gmix_s[:, kt:kt + 1]).then_inc(taken, 1)
                    n += 1
                for ct in range(KT):
                    if ct == 0:
                        act.wait_ge(hist_done, g * KT)
                    if ct >= 2:
                        act.wait_ge(hist_done, g * KT + ct - 1)
                    act.wait_ge(big, g * BIG + n + 1)
                    act.activation(xbcT[:, ct % 2, 3:], bank[n % 4][:, :], ACT.Copy, scale=UNSCALE).then_inc(taken, 1)
                    n += 1
                for ct in range(KT):
                    act.wait_ge(conv_done, g * KT + ct + 1)
                    act.activation(xc[:, ct, :], xc[:, ct, :], ACT.Silu).then_inc(silu_done, 1)
                for c in range(GC):
                    if c == 0:
                        act.wait_ge(out_done, g * 2)
                    act.wait_ge(big, g * BIG + n + 1)
                    act.activation(gs[:, c, :], bank[n % 4][:, RW:], ACT.Silu, scale=UNSCALE)
                    act.activation(vb[:, c, :], bank[n % 4][:, 0:RW], ACT.Copy, scale=UNSCALE).then_inc(taken, 1)
                    n += 1
                    if c == 0:
                        act.wait_ge(cat_st, g * 16)
                    act.wait_ge(big, g * BIG + n + 1)
                    act.activation(Y[:, c, RW:], bank[n % 4][:, :], ACT.Silu, scale=UNSCALE).then_inc(taken, 1)
                    n += 1
                    if c == 0:
                        act.wait_ge(u_st, g * 16)
                    act.wait_ge(big, g * BIG + n + 1)
                    act.activation(dtu[:, c, SH:], bank[n % 4][:, SH:SH + S5W], ACT.Copy, scale=UNSCALE).then_inc(u_ready, 1)
                    act.activation(dtu[:, c, 0:SH], bank[n % 4][:, 0:SH], ACT.Copy, scale=UNSCALE).then_inc(taken, 1)
                    n += 1
                act.wait_ge(ax_ready, g + 1)
                act.activation(dts[:, 2, :, :], dts[:, 1, :, :], ACT.Exp, scale=-1.0).then_inc(e_ready, 1)
                act.wait_ge(w_ready, g + 1)
                act.activation(dts[:, 4, :, :], dts[:, 3, :, :], ACT.Ln).then_inc(ln_ready, 1)
                for c in range(GC):
                    s0 = g * GC * SML + c * SML
                    act.wait_ge(small, s0 + 1)
                    qk = bank[SB0][:, :].rearrange("p (a b) -> p a b", a=4)
                    act.activation(qz[0:RD, :, 0, :], qk[0:RD, 0:2, :], ACT.Copy)
                    act.activation(qz[RD:, :, 1, :], qk[RD:, 0:2, :], ACT.Copy)
                    act.activation(kT, qk[:, 2:4, :], ACT.Copy).then_inc(s_act, 1)
                    if c == 0:
                        act.wait_ge(ch_done, g * GC)
                    else:
                        act.wait_ge(ch_done, g * GC + c)
                    act.wait_ge(small, s0 + 2)
                    act.activation(xtok[:, :, :], bank[SB0 + 1][:, :].rearrange("p (a b) -> p a b", a=SH), ACT.Copy).then_inc(s_act, 1)
                    act.wait_ge(small, s0 + 3)
                    act.activation(dec[:, :, :], bank[SB0 + 2][:, 2 * SN:2 * SN + 3 * SH].rearrange("p (a b) -> p a b", a=3), ACT.Exp)
                    act.activation(btok[:, :, :], bank[SB0 + 2][:, 0:2 * SN].rearrange("p (a b) -> p a b", a=2), ACT.Copy).then_inc(s_act, 1)
                    for h in range(2):
                        act.wait_ge(small, s0 + 4 + h)
                        act.activation(AB[:, h, :], bank[SB0 + h][:, :], ACT.Exp).then_inc(s_act, 1)

        @block.vector
        def _(dve):
            for n, (kt, cols, room, before) in enumerate(pieces):
                dve.wait_ge(w_hi, n + 1)
                dve.scalar_tensor_tensor(wi[:, 1, kt, cols], stage[room], W_SCALE, wi[:, 0, kt, cols], ALU.mult, ALU.subtract).then_inc(w_lo, 1)
            dve.wait_ge(a_set, 1)
            dve.wait_ge(c_ld, 16 * 14)
            dve.tensor_scalar(a_bc[:, :], a_bc[:, :], -1.0, None, ALU.mult).then_inc(a_set, 1)
            dve.tensor_scalar(gmix_s[:, :], gmix[:, :], N_SCALE, None, ALU.mult).then_inc(a_set, 1)
            dve.wait_ge(a_set, 3)
            dve.wait_ge(w_lo, len(pieces))
            dve.wait_ge(s_set, 4)
            with dve.Fori(0, NG) as g:
                ch = Chain(dve, dve_s, g, DVE_TURN)
                dve.wait_ge(sq_done, g * GC + GC)
                dve.tensor_scalar(ms[:, :], ss[:, :], 1.0 / D, EPS, ALU.mult, ALU.add).then_inc(ms_done, 1)
                dve.wait_ge(rs_done, g + 1)
                for c in range(GC):
                    dve.tensor_scalar(xg[:, c, :], xg[:, c, :], rstd[:, c:c + 1], None, ALU.mult).then_inc(xs_done, 1)
                for kt in range(KT):
                    dve.wait_ge(taken, g * BIG + kt + 1)
                    dve.scalar_tensor_tensor(hn_s[1][:, kt, :], bank[kt % 4][:, :], gmix_s[:, kt:kt + 1], hn_s[0][:, kt, :], ALU.mult, ALU.subtract).then_inc(hn_lo, 1)
                for ct in range(KT):
                    b = xbcT[:, ct % 2, :]
                    ch.post(dve.tensor_copy(b[:, 0:3], hist[:, ct, :]))
                    ch.wait()
                    dve.wait_ge(taken, g * BIG + KT + ct + 1)
                    ch.post(dve.tensor_scalar(xc[:, ct, :], b[:, 0:GT], cw[:, 0, ct:ct + 1], cb[:, ct:ct + 1], ALU.mult, ALU.add))
                    for j in range(1, 4):
                        ch.wait()
                        ins = dve.scalar_tensor_tensor(xc[:, ct, :], b[:, j:GT + j], cw[:, j, ct:ct + 1], xc[:, ct, :], ALU.mult, ALU.add)
                        if j < 3:
                            ch.post(ins)
                        else:
                            ins.then_inc(conv_done, 1)
                    dve.tensor_copy(hist[:, ct, :], b[:, GT:]).then_inc(hist_done, 1)
                dve.wait_ge(r_ld, g * 16 + 16)
                for c in range(GC):
                    dve.wait_ge(qk_done, g * GC + c + 1)
                    t = bank[4][:, :].rearrange("p (h a r) -> p h a r", a=2, r=RD // 2)
                    for j in range(2):
                        tab = rope[:, c, j * RW:(j + 1) * RW].rearrange("p (h r) -> p h r", r=RD // 2)
                        o = AB[:, j, :].rearrange("p (h a r) -> p h a r", a=2, r=RD // 2)
                        ch.post(dve.tensor_tensor(o, t, bc(tab, 2, 2), ALU.mult))
                    ch.wait()
                    A = AB[:, 0, :].rearrange("p (h a r) -> p h a r", a=2, r=RD // 2)
                    B = AB[:, 1, :].rearrange("p (h a r) -> p h a r", a=2, r=RD // 2)
                    o = qr[:, c, :].rearrange("p (h a r) -> p h a r", a=2, r=RD // 2)
                    ch.post(dve.tensor_tensor(o[:, :, 0, :], A[:, :, 0, :], B[:, :, 1, :], ALU.subtract))
                    dve.tensor_tensor(o[:, :, 1, :], A[:, :, 1, :], B[:, :, 0, :], ALU.add).then_inc(qk_free, 1)
                dve.wait_ge(taken, g * BIG + BIG)
                ch.post(dve.tensor_tensor(dts[:, 0, :, :], dtu[:, :, 0:SH], bc(dtb_bc[:, :], 1, GC), ALU.add))
                ch.wait()
                ch.post(dve.tensor_scalar(dts[:, 5, :, :], dts[:, 0, :, :], -1.0, None, ALU.mult))
                ch.wait()
                dve.tensor_tensor(dts[:, 1, :, :], dts[:, 0, :, :], dts[:, 5, :, :], ALU.max).then_inc(ax_ready, 1)
                dve.wait_ge(e_ready, g + 1)
                dve.tensor_scalar(dts[:, 3, :, :], dts[:, 2, :, :], 1.0, None, ALU.add).then_inc(w_ready, 1)
                dve.wait_ge(w_ready, g + 1)
                ch.post(dve.tensor_scalar(dts[:, 5, :, :], dts[:, 3, :, :], -1.0, 1e-30, ALU.add, ALU.add))
                ch.wait()
                ch.post(dve.reciprocal(dts[:, 5, :, :], dts[:, 5, :, :]))
                ch.wait()
                ch.post(dve.tensor_tensor(dts[:, 5, :, :], dts[:, 5, :, :], dts[:, 2, :, :], ALU.mult))
                ch.wait()
                dve.wait_ge(ln_ready, g + 1)
                ch.post(dve.scalar_tensor_tensor(dts[:, 5, :, :], dts[:, 4, :, :], 1e-30, dts[:, 5, :, :], ALU.add, ALU.mult))
                ch.wait()
                ch.post(dve.scalar_tensor_tensor(dt_, dts[:, 0, :, :], 0.0, dts[:, 5, :, :], ALU.max, ALU.add))
                ch.wait()
                dve.tensor_tensor(dtA, dt_, bc(a_bc[:, :], 1, GC), ALU.mult).then_inc(dt_ready, 1)
                dve.wait_ge(dt_ready, g + 1)
                for c in range(GC):
                    s0 = g * GC * SML + c * SML
                    a0 = g * GC * N_ACT + c * N_ACT
                    if c:
                        dve.wait_ge(small, s0)
                        dve.wait_ge(ch_done, g * GC + c)
                    dve.tensor_tensor(segin[:, :, :], bc(le, 1, SH), bc(dtA[:, c, :], 2, P), ALU.mult).then_inc(seg_ready, 1)
                    dve.wait_ge(s_act, a0 + 2)
                    ch.post(dve.tensor_tensor(xdt[:, :, :], xtok[:, :, :], bc(dt_[:, c, :], 2, SP_), ALU.mult))
                    ch.wait()
                    dve.wait_ge(s_act, a0 + 5)
                    ch.post(dve.tensor_tensor(xdec.rearrange("p (h e) -> p h e", h=SH), xdt[:, :, :], bc(dec[:, 1, :], 2, SP_), ALU.mult))
                    ch.wait()
                    dve.wait_ge(small, s0 + 6)
                    dve.tensor_tensor(cbm[:, :, :], bank[SB0 + 2][:, 0:2 * P].rearrange("p (a b) -> p a b", a=2), bc(le, 1, 2), ALU.mult).then_inc(s_dve, 1)
                    dve.wait_ge(s_dve, (g * GC + c) * N_DVE + 1)
                    Ev = E[:, :, :].rearrange("p (a h) l -> p a h l", a=2)
                    ch.post(dve.tensor_tensor(Ev, Ev, bc(cbm[:, :, :], 2, SH // 2), ALU.mult))
                    ch.wait()
                    dve.wait_ge(small, s0 + 7)
                    dve.tensor_tensor(PT[:, :, :], bank[SB0][:, :].rearrange("p (a b) -> p a b", a=RH), bc(le, 1, RH), ALU.mult).then_inc(s_dve, 1)
                    dve.wait_ge(s_dve, (g * GC + c) * N_DVE + 2)
                    dve.wait_ge(small, s0 + 8)
                    dve.tensor_tensor(yo.rearrange("p (h e) -> p h e", h=SH), bank[SB0 + 1][:, :].rearrange("p (h e) -> p h e", h=SH),
                                      bc(dec[:, 0, :], 2, SP_), ALU.mult).then_inc(s_dve, 1)
                    dve.wait_ge(small, s0 + 9)
                    ch.post(dve.tensor_tensor(S_m[:, :, :], S_m[:, :, :], bc(dec[:, 2, :], 2, SP_), ALU.mult))
                    ch.wait()
                    dve.tensor_tensor(S_m[:, :, :], S_m[:, :, :], bank[SB0 + 2][:, :].rearrange("p (h e) -> p h e", h=SH), ALU.add).then_inc(s_dve, 1)
                    dve.wait_ge(small, s0 + 10)
                    dve.tensor_copy(Y[:, c, 0:RW], bank[SB0][:, 0:RW]).then_inc(s_dve, 1)
                    dve.wait_ge(small, s0 + 11)
                    ch.post(dve.tensor_tensor(S_r[:, :, :], S_r[:, :, :], bank[SB0 + 1][:, 0:2 * RD].rearrange("p (a b) -> p a b", a=2), ALU.add))
                    ch.wait()
                    dve.tensor_tensor(S_r[:, :, :], S_r[:, :, :], gam[:, :].rearrange("p (a b) -> p a b", a=2), ALU.mult).then_inc(s_dve, 1)
                    dve.wait_ge(small, s0 + 12)
                    ch.post(dve.tensor_tensor(yo, yo, bank[SB0 + 2][:, :], ALU.add))
                    ch.post(dve.tensor_tensor(xdt[:, :, :], xtok[:, :, :], bc(d_bc[:, :], 2, SP_), ALU.mult))
                    ch.wait()
                    ch.post(dve.tensor_tensor(yo, yo, xdt[:, :, :].rearrange("p h e -> p (h e)"), ALU.add))
                    ch.wait()
                    dve.tensor_tensor(Y[:, c, RW:], yo, Y[:, c, RW:], ALU.mult).then_inc(s_dve, 1)
                    dve.wait_ge(s_dve, (g * GC + c) * N_DVE + N_DVE)
                    ch.post(dve.scalar_tensor_tensor(xdt[:, :, :].rearrange("p h e -> p (h e)"), Y[:, c, RW:], 1.0, Y[:, c, RW:], ALU.mult, ALU.mult, accum_out=sso[:, c:c + 1]))
                    ch.post(dve.tensor_tensor(yo[:, 0:RW], Y[:, c, 0:RW], Y[:, c, 0:RW], ALU.mult))
                    ch.wait()
                    dve.tensor_reduce(sso[:, GC + 4 * c:GC + 4 * c + 4], yo[:, 0:RW].rearrange("p (h e) -> p h e", h=RH), AX.X, ALU.add).then_inc(ch_done, 1)
                dve.wait_ge(ch_done, g * GC + GC)
                dve.tensor_scalar(mso[:, 0:GC], sso[:, 0:GC], 1.0 / SW, EPS, ALU.mult, ALU.add).then_inc(mo_done, 1)
                dve.tensor_scalar(mso[:, GC:], sso[:, GC:], 1.0 / RD, EPS, ALU.mult, ALU.add).then_inc(mo_done, 1)
                dve.wait_ge(ro_done, g + 1)
                for c in range(GC):
                    ins = dve.scalar_tensor_tensor(Y[:, c, RW:], Y[:, c, RW:], rso[:, c:c + 1], ng_bc[:, :], ALU.mult, ALU.mult)
                ins.then_inc(out_done, 1)
                for c in range(GC):
                    yh = Y[:, c, 0:RW].rearrange("p (h e) -> p h e", h=RH)
                    ch.post(dve.tensor_tensor(yh, yh, bc(rso[:, GC + 4 * c:GC + 4 * c + 4], 2, RD), ALU.mult))
                ch.wait()
                ch.post(dve.tensor_tensor(Y[:, :, 0:RW], Y[:, :, 0:RW], bc(gn_bc[:, :], 1, GC), ALU.mult))
                ch.wait()
                dve.tensor_tensor(Y[:, :, 0:RW], Y[:, :, 0:RW], gs[:, :, :], ALU.mult).then_inc(out_done, 1)
                assert ch.n == DVE_TURN, ch.n

        @block.tensor
        def _(pe):
            pe.wait_ge(c_ld, 16 * 14)
            with pe.Fori(0, NG) as g:
                n = 0

                def slot(n):
                    pe.wait_ge(taken, g * BIG + max(0, n - 3))
                    if 4 <= n < KT + 4:
                        pe.wait_ge(hn_lo, g * KT + n - 3)
                    return bank[n % 4]

                for kt in range(KT):
                    o = slot(n)
                    if kt == 0:
                        pe.wait_ge(xs_done, g * GC + GC)
                    for c in range(GC):
                        ins = pe.transpose(o[:, c * P:(c + 1) * P], xg[:, c, kt * P:(kt + 1) * P], ident)
                    ins.then_inc(big, 1)
                    n += 1
                pe.wait_ge(w_lo, len(pieces))
                pe.wait_ge(taken, g * BIG + KT)
                pe.wait_ge(hn_lo, g * KT + KT)
                for ct in range(KT):
                    o = slot(n)
                    w = [[wi[:, h, kt, C_XBC + ct * P:C_XBC + (ct + 1) * P] for kt in range(KT)] for h in range(2)]
                    hn = [[hn_s[h][:, kt, :] for kt in range(KT)] for h in range(2)]
                    products(pe, o[:, :], w, hn).then_inc(big, 1)
                    n += 1
                for c in range(GC):
                    def project(o, a, w):
                        return products(pe, o[:, 0:w], [[hn_s[h][:, kt, c * P:(c + 1) * P] for kt in range(KT)] for h in range(2)],
                                        [[wi[:, h, kt, a:a + w] for kt in range(KT)] for h in range(2)])

                    pe.wait_ge(qk_free, g * GC + c)
                    project(bank[4], 0, 2 * RW).then_inc(qk_done, 1)
                    project(slot(n), C_VG, 2 * RW).then_inc(big, 1)
                    project(slot(n + 1), C_Z, SW).then_inc(big, 1)
                    project(slot(n + 2), C_DT, SH + S5W).then_inc(big, 1)
                    n += 3
                assert n == BIG
                pe.wait_ge(taken, g * BIG + BIG)
                pe.wait_ge(silu_done, g * KT + KT)
                pe.wait_ge(qk_free, g * GC + GC)
                pe.wait_ge(dt_ready, g + 1)
                for c in range(GC):
                    tok = slice(c * P, (c + 1) * P)

                    def room(j):
                        t = j - 3
                        if t < 0:
                            pe.wait_ge(s_dve, (g * GC + c) * N_DVE)
                        elif BY[t] == "act":
                            pe.wait_ge(s_act, (g * GC + c) * N_ACT + BY[:t + 1].count("act"))
                        else:
                            pe.wait_ge(s_dve, (g * GC + c) * N_DVE + BY[:t + 1].count("dve"))
                        return bank[SB0 + j % 3]

                    o = room(0)
                    for k in range(4):
                        ins = pe.transpose(o[:, k * P:(k + 1) * P], qr[:, c, k * P:(k + 1) * P], ident)
                    ins.then_inc(small, 1)
                    o = room(1)
                    for k in range(4):
                        ins = pe.transpose(o[:, k * P:(k + 1) * P], xc[:, k, tok], ident)
                    ins.then_inc(small, 1)
                    o = room(2)
                    for k in range(2):
                        pe.transpose(o[:, k * P:(k + 1) * P], xc[:, 4 + k, tok], ident)
                    for k, m in enumerate((le, gt, ones)):
                        ins = pe.matmul(o[:, 2 * P + k * SH:2 * P + (k + 1) * SH], m, dtA[:, c, :], start=True, stop=True)
                    ins.then_inc(small, 1)
                    pe.wait_ge(seg_ready, g * GC + c + 1)
                    for h in range(2):
                        pe.matmul(room(3 + h)[:, :], gt, sg2[:, h, :], start=True, stop=True).then_inc(small, 1)
                    o = room(5)
                    for k in range(2):
                        ins = pe.matmul(o[:, k * P:(k + 1) * P], xc[:, 4 + k, tok], xc[:, 6 + k, tok], start=True, stop=True)
                    ins.then_inc(small, 1)
                    pe.wait_ge(s_act, (g * GC + c) * N_ACT + 1)
                    o = room(6)
                    for h in range(RH):
                        ins = pe.matmul(o[:, h * P:(h + 1) * P], kT[:, h // 2, :], qz[:, h // 2, h % 2, :], start=True, stop=True)
                    ins.then_inc(small, 1)
                    o = room(7)
                    for k in range(2):
                        ins = pe.matmul(o[:, k * 256:(k + 1) * 256], xc[:, 6 + k, tok],
                                        S_m[:, 4 * k:4 * k + 4, :].rearrange("p h e -> p (h e)"), start=True, stop=True)
                    ins.then_inc(small, 1)
                    o = room(8)
                    pe.wait_ge(s_dve, (g * GC + c) * N_DVE + 1)
                    for k in range(2):
                        ins = pe.matmul(o[:, k * 256:(k + 1) * 256], btok[:, k, :], xdec[:, k * 256:(k + 1) * 256], start=True, stop=True)
                    ins.then_inc(small, 1)
                    pe.wait_ge(s_dve, (g * GC + c) * N_DVE + 2)
                    o = room(9)
                    for h in range(RH):
                        pe.matmul(o[:, h * RD:(h + 1) * RD], PT[:, h, :], vb[:, c, h * RD:(h + 1) * RD], start=True, stop=False)
                        ins = pe.matmul(o[:, h * RD:(h + 1) * RD], qz[:, h // 2, h % 2, :], S_r[:, h // 2, :], start=False, stop=True)
                    ins.then_inc(small, 1)
                    o = room(10)
                    for h in range(RH):
                        r = slice(h % 2 * RD, h % 2 * RD + RD)
                        ins = pe.matmul(o[r, h // 2 * RD:(h // 2 + 1) * RD], qr[:, c, RW + h * RD:RW + (h + 1) * RD],
                                        vb[:, c, h * RD:(h + 1) * RD], start=True, stop=True)
                    ins.then_inc(small, 1)
                    o = room(11)
                    for h in range(SH):
                        ins = pe.matmul(o[:, h * SP_:(h + 1) * SP_], E[:, h, :], xdt[:, h, :], start=True, stop=True)
                    ins.then_inc(small, 1)
    return held



SBL = 8
SBN = T // SBL
LK = SBL * S5C
GQ = 4
CODY = (6.28125, 0.0019350051879882812, 3.0199159819583e-07)


def s5_mixer(nc, env, dram, held):
    DT2 = env["s5_turn"]
    with ExitStack() as ctx:
        def sb(name, shape, dt=F32):
            return ctx.enter_context(nc.sbuf_tensor(name, shape, dt))

        def sem(name):
            return nc.alloc_semaphore(name)

        cst = sb("cst_b", [P, P])
        anat = sb("anat", [S5G, 2, 2, S5P])
        cnat = sb("cnat", [P, 2, 2, 2, S5P])
        bnat = sb("bnat", [P, 2, S5G, S5C])
        step = sb("step", [P, S5G])
        d_bc = sb("d5_bc", [P, S5W])
        b_bc = sb("b5_bc", [P, S5W])
        wglu = sb("wglu", [P, 2, S5W])
        w = sb("s5_work", [P, 16, S5G])
        pw = sb("powers", [P, 2, SBL + 1, S5G])
        pv = sb("powers_back", [P, 2, SBL, S5G])
        Ba, Bb, Bt = (sb(n, [P, S5G, S5C]) for n in ("Ba", "Bb", "Bt"))
        Ca, Cb, Cc, Cd = (sb(n, [P, S5G, S5C]) for n in ("Ca", "Cb", "Cc", "Cd"))
        Cr, Ci = sb("Cr", [P, S5G, S5C]), sb("Ci", [P, S5G, S5C])
        u8 = sb("u8", [P, 2, S5G])
        r8 = sb("r8", [P, S5G])
        TC, TS = sb("TC", [P, S5G, SBN + 1]), sb("TS", [P, S5G, SBN + 1])
        U = sb("U5", [P, 2, SBL, S5W])
        Y5 = sb("Y5", [P, 2, SBL, S5W])
        big = sb("s5_big", [P, 8 * 1024])
        tmp = [big[:, i * 2048:(i + 1) * 2048].rearrange("p (g b) -> p g b", g=S5G) for i in range(2)]
        Uc = big[:, 0:1024].rearrange("p (h g k) -> p h g k", h=2, g=GQ)
        UT = big[:, 1024:2048].rearrange("p (g b) -> p g b", g=GQ)
        z1 = big[:, 2048:3072].rearrange("p (g b) -> p g b", g=GQ)
        z2 = big[:, 3072:4096].rearrange("p (g b) -> p g b", g=GQ)
        W1 = big[:, 4096:5120].rearrange("p (g b) -> p g b", g=GQ)
        W2 = big[:, 5120:6144].rearrange("p (g b) -> p g b", g=GQ)
        z = big[:, 6144:7168].rearrange("p (g b) -> p g b", g=GQ)
        t5 = big[:, 7168:8192]
        MB = sb("MB", [P, GQ, LK])
        BmT = sb("BmT", [P, 2, GQ, P])
        BZ = sb("BZ", [P, GQ, (2 * SBL - 1) * S5C])
        CZ = sb("CZ", [P, GQ, 2 * SBL * S5C])
        CM = sb("CM", [P, GQ, LK])
        Tm = sb("Tm", [P, GQ, LK])
        bank = [ctx.enter_context(nc.psum_tensor(f"bankB{i}", [P, 512], F32)) for i in range(4)]
        vbank = ctx.enter_context(nc.psum_tensor("vbank", [P, GQ, 2, SBN], F32))
        ident = cst[:, :]
        no_rows = sb("no_rows", [P, D])

        ld, u_ld = sem("s5_params_loaded"), sem("s5_u_loaded")
        tr0, s1, s2, act0 = sem("s5_params_transposed"), sem("s5_setup_dve"), sem("s5_setup_act"), sem("s5_C_taken")
        dve_t = sem("s5_turn_dve")
        zeroed, uc_ready, mb_ready, z_ready, y_taken = (sem("s5_zeroed"), sem("s5_u_sorted"), sem("s5_matrices"),
                                                        sem("s5_states"), sem("s5_y_taken"))
        ut_done, mb_done, tm_done, v_done, y_done = (sem("s5_uT_done"), sem("s5_BT_done"), sem("s5_T_done"),
                                                     sem("s5_V_done"), sem("s5_y_done"))
        ut_taken, mb_taken, tm_taken = sem("s5_uT_taken"), sem("s5_BT_taken"), sem("s5_T_taken")
        pre, gelu, gt_done, gt_taken, glu_done, glu_b, sig, s5_out, st = (
            sem("s5_plus_Du"), sem("s5_gelu"), sem("s5_gT_done"), sem("s5_gT_taken"), sem("s5_glu_done"),
            sem("s5_glu_bias"), sem("s5_sigmoid"), sem("s5_out"), sem("s5_stored"))
        y_clear = sem("ybuf_cleared")
        block = ctx.enter_context(nc.Block())

        @block.sync
        def _(sp):
            for j in range(2):
                for r, a in enumerate(("s5_A_re", "s5_A_im")):
                    sp.dma_start(anat[:, r, j, :], dram[a][0]).then_inc(ld, 16)
                for r, a in enumerate(("s5_C_re", "s5_C_im")):
                    sp.dma_start(cnat[:, r, :, j, :], dram[a][0].rearrange("(a g) c p -> (g c) a p", a=2)).then_inc(ld, 16)
                for r, a in enumerate(("s5_B_re", "s5_B_im")):
                    sp.dma_start(bnat[j * S5P:(j + 1) * S5P, r, :, :], dram[a][0].rearrange("g p c -> p g c")).then_inc(ld, 16)
            sp.dma_start(step[:, :], dram["s5_log_step"][0].partition_broadcast(P)).then_inc(ld, 16)
            sp.dma_start(cst[:, :], dram["cst"][:, K_ID:K_ID + P]).then_inc(ld, 16)
            sp.dma_start(d_bc[:, :], dram["s5_D"][0].partition_broadcast(P)).then_inc(ld, 16)
            sp.dma_start(b_bc[:, :], dram["s5_b_glu"][0].partition_broadcast(P)).then_inc(ld, 16)
            sp.dma_start(wglu[:, :, :], dram["s5_w_glu"][0].rearrange("(k p) n -> p k n", p=P)).then_inc(ld, 16)
            for h in range(2):
                sp.dma_start(U[:, h, :, :], dram["u_scr"].rearrange("(h b t) c -> h b t c", h=2, t=SBL)[h]).then_inc(u_ld, 16)
            sp.wait_ge(zeroed, 3)
            spare = dram["ybuf"].rearrange("(b p) d -> p b d", p=P)[:, USED_MIN:, :]
            sp.dma_start(spare, bc(no_rows[:, :], 1, NB - USED_MIN)).then_inc(y_clear, 16)
            for h in range(2):
                sp.wait_ge(s5_out, 4 * h + 4)
                sp.dma_start(dram["cat"].rearrange("(h b t) d -> h b t d", h=2, t=SBL)[h, :, :, RW + SW:], Y5[:, h, :, :]).then_inc(st, 16)
            sp.wait_ge(st, 32)
            sp.wait_ge(y_clear, 16)

        @block.gpsimd
        def _(pool):
            for h in held:
                pool.sem_clear(h)
            pool.memset(no_rows[:, :], 0.0).then_inc(zeroed, 1)
            pool.memset(BZ[:, :, :], 0.0).then_inc(zeroed, 1)
            pool.memset(CZ[:, :, :], 0.0).then_inc(zeroed, 1)

        @block.vector
        def _(dve):
            ch = Chain(dve, s1)
            tt, ts, stt = dve.tensor_tensor, dve.tensor_scalar, dve.scalar_tensor_tensor

            def do(f, *a):
                ch.post(f(*a))
                ch.wait()

            def W(i):
                return w[:, i, :]

            DELTA, MAG, ANG, K_, SIN, COS, X, LR, LI, DEN, CR, CI, X2 = range(13)
            dve.wait_ge(ld, 16 * 17)
            dve.wait_ge(tr0, 1)
            AR, AI = w[:, 13, :], w[:, 14, :]
            do(dve.tensor_copy, AR, bank[0][:, 0:S5G])
            do(dve.tensor_copy, AI, bank[0][:, S5G:2 * S5G])
            dve.wait_ge(s2, 1)
            do(tt, W(MAG), AR, W(DELTA), ALU.mult)
            do(tt, W(ANG), AI, W(DELTA), ALU.mult)
            mag_at = ch.n
            do(ts, W(K_), W(ANG), 1.0 / (2 * np.pi), 12582912.0, ALU.mult, ALU.add)
            do(ts, W(K_), W(K_), -12582912.0, None, ALU.add)
            for c in CODY:
                do(stt, W(ANG), W(K_), -c, W(ANG), ALU.mult, ALU.add)
            do(ts, W(ANG), W(ANG), 3.1415925, -3.1415925, ALU.min, ALU.max)
            do(ts, W(X), W(ANG), -1.0, None, ALU.mult)
            do(tt, W(X), W(X), W(ANG), ALU.max)
            do(ts, W(X), W(X), -1.0, np.pi / 2, ALU.mult, ALU.add)
            ang_at = ch.n
            assert (mag_at, ang_at) == env["s5_marks"], (mag_at, ang_at)
            dve.wait_ge(s2, 5)
            do(tt, W(LR), W(MAG), W(COS), ALU.mult)
            do(tt, W(LI), W(MAG), W(SIN), ALU.mult)
            do(tt, W(DEN), AR, AR, ALU.mult)
            do(tt, W(X), AI, AI, ALU.mult)
            do(tt, W(DEN), W(DEN), W(X), ALU.add)
            do(dve.reciprocal, W(DEN), W(DEN))
            do(ts, W(K_), W(LR), -1.0, None, ALU.add)
            do(tt, W(CR), W(K_), AR, ALU.mult)
            do(tt, W(X), W(LI), AI, ALU.mult)
            do(tt, W(CR), W(CR), W(X), ALU.add)
            do(tt, W(CR), W(CR), W(DEN), ALU.mult)
            do(tt, W(CI), W(LI), AR, ALU.mult)
            do(tt, W(X), W(K_), AI, ALU.mult)
            do(tt, W(CI), W(CI), W(X), ALU.subtract)
            do(tt, W(CI), W(CI), W(DEN), ALU.mult)
            cr, ci = bc(W(CR), 2, S5C), bc(W(CI), 2, S5C)
            br, bi = bnat[:, 0, :, :], bnat[:, 1, :, :]
            lo, hi = slice(0, S5P), slice(S5P, P)
            do(tt, Ba[:, :, :], cr, br, ALU.mult)
            do(tt, Bt[:, :, :], ci, bi, ALU.mult)
            do(tt, Ba[:, :, :], Ba[:, :, :], Bt[:, :, :], ALU.subtract)
            do(tt, Bb[:, :, :], cr, bi, ALU.mult)
            do(tt, Bt[:, :, :], ci, br, ALU.mult)
            do(tt, Bb[:, :, :], Bb[:, :, :], Bt[:, :, :], ALU.add)
            do(dve.tensor_copy, Bt[hi], Ba[hi])
            do(dve.tensor_copy, Ba[hi], Bb[hi])
            do(dve.tensor_copy, Bb[hi], Bt[hi])
            do(ts, Bb[lo], Bb[lo], -1.0, None, ALU.mult)
            dve.wait_ge(act0, 2)
            do(dve.tensor_copy, Ca[lo], Cr[lo])
            do(ts, Ca[hi], Ci[hi], -1.0, None, ALU.mult)
            do(ts, Cb[lo], Ci[lo], -1.0, None, ALU.mult)
            do(ts, Cb[hi], Cr[hi], -1.0, None, ALU.mult)
            do(ts, Cc[lo], Ci[lo], -1.0, None, ALU.mult)
            do(dve.tensor_copy, Cc[hi], Cr[hi])
            do(ts, Cd[lo], Cr[lo], -1.0, None, ALU.mult)
            do(ts, Cd[hi], Ci[hi], -1.0, None, ALU.mult)

            def cmul(o_r, o_i, a_r, a_i, b_r, b_i, x, y):
                do(tt, x, a_r, b_r, ALU.mult)
                do(tt, y, a_i, b_i, ALU.mult)
                do(tt, o_r, x, y, ALU.subtract)
                do(tt, x, a_r, b_i, ALU.mult)
                do(tt, y, a_i, b_r, ALU.mult)
                do(tt, o_i, x, y, ALU.add)

            do(dve.memset, pw[:, 0, 0, :], 1.0)
            do(dve.memset, pw[:, 1, 0, :], 0.0)
            do(dve.tensor_copy, pw[:, 0, 1, :], W(LR))
            do(dve.tensor_copy, pw[:, 1, 1, :], W(LI))
            n = 1
            while n < SBL:
                a = [pw[:, r, 1:n + 1, :] for r in range(2)]
                b = [bc(pw[:, r, n, :], 1, n) for r in range(2)]
                x, y = (tmp[i][:, 0:n, 0:S5G] for i in range(2))
                cmul(pw[:, 0, n + 1:2 * n + 1, :], pw[:, 1, n + 1:2 * n + 1, :], a[0], a[1], b[0], b[1], x, y)
                n *= 2
            for s in range(SBL):
                do(dve.tensor_copy, pv[:, :, s, :], pw[:, :, SBL - 1 - s, :])
            do(dve.tensor_copy, u8[:, 0, :], W(COS))
            do(dve.tensor_copy, u8[:, 1, :], W(SIN))
            n = 1
            while n < SBL:
                do(tt, W(X), u8[:, 0, :], u8[:, 0, :], ALU.mult)
                do(tt, W(X2), u8[:, 1, :], u8[:, 1, :], ALU.mult)
                do(stt, W(K_), u8[:, 0, :], 2.0, u8[:, 1, :], ALU.mult, ALU.mult)
                do(tt, u8[:, 0, :], W(X), W(X2), ALU.subtract)
                do(dve.tensor_copy, u8[:, 1, :], W(K_))
                n *= 2
            do(dve.memset, TC[:, :, 0:1], 1.0)
            do(dve.memset, TS[:, :, 0:1], 0.0)
            do(dve.tensor_copy, TC[:, :, 1:2], u8[:, 0, :].unsqueeze(2))
            do(dve.tensor_copy, TS[:, :, 1:2], u8[:, 1, :].unsqueeze(2))
            n = 1
            while n < SBN:
                b_r, b_i = (bc(t[:, :, n], 2, n) for t in (TC, TS))
                x, y = (tmp[i][:, :, 0:n] for i in range(2))
                cmul(TC[:, :, n + 1:2 * n + 1], TS[:, :, n + 1:2 * n + 1], TC[:, :, 1:n + 1], TS[:, :, 1:n + 1], b_r, b_i, x, y)
                n *= 2
            do(ts, TS[hi], TS[hi], -1.0, None, ALU.mult)
            do(dve.memset, W1[:, :, 0:1], 0.0)
            do(dve.memset, W2[:, :, 0:1], 0.0)
            dve.wait_ge(zeroed, 3)
            dve.wait_ge(u_ld, 32)
            with dve.Fori(0, S5G // GQ) as q:
                c2 = Chain(dve, dve_t, q, DT2)
                gr = bass.ds(q * GQ, GQ)
                dve.wait_ge(y_done, q)
                for h in range(2):
                    src = U[:, h, :, bass.ds(q * GQ * S5C, GQ * S5C)].rearrange("p s (g c) -> p g s c", g=GQ)
                    ins = ts(Uc[:, h, :, :].rearrange("p g (s c) -> p g s c", s=SBL), src, 1.0, None, ALU.mult)
                    ins.then_inc(uc_ready, 1)

                def powers(o, pp, A, B, k):
                    oo = o.rearrange("p g (s c) -> p g s c", c=S5C)
                    for s, M in ((0, A), (1, B)):
                        dst = oo if s == 0 else t5[:, 0:GQ * k * S5C].rearrange("p (g s c) -> p g s c", g=GQ, s=k)
                        for gg in range(GQ):
                            mr = bc(M[:, bass.ds(q * GQ + gg, 1), :].squeeze(1), 1, k)
                            pr = bc(pp[:, s, :, bass.ds(q * GQ + gg, 1)].squeeze(2), 2, S5C)
                            c2.post(tt(dst[:, gg, :, :], pr, mr, ALU.mult))
                    c2.wait()
                    return tt(o, o, t5[:, 0:GQ * k * S5C].rearrange("p (g k) -> p g k", g=GQ), ALU.add)

                powers(MB[:, :, :], pv, Ba, Bb, SBL).then_inc(mb_ready, 1)
                dve.wait_ge(mb_ready, q * 4 + 1)
                ts(BZ[:, :, (SBL - 1) * S5C:SBL * S5C], Ba[:, gr, :], 1.0, None, ALU.mult).then_inc(mb_ready, 1)
                powers(CZ[:, :, (SBL - 1) * S5C:], pw, Ca, Cb, SBL + 1).then_inc(mb_ready, 1)
                dve.wait_ge(mb_ready, q * 4 + 3)
                powers(CM[:, :, :], pw[:, :, 1:, :], Cc, Cd, SBL).then_inc(mb_ready, 1)
                dve.wait_ge(v_done, q + 1)
                c2.post(tt(z1, TC[:, gr, 0:SBN], vbank[:, :, 0, :], ALU.mult))
                c2.post(tt(z2, TS[:, gr, 0:SBN], vbank[:, :, 1, :], ALU.mult))
                c2.wait()
                c2.post(tt(z1, z1, z2, ALU.add))
                c2.wait()
                for gg in range(GQ):
                    rr = bc(r8[:, bass.ds(q * GQ + gg, 1)].squeeze(1), 1, SBN)
                    c2.post(dve.tensor_tensor_scan(z[:, gg, :], rr, z1[:, gg, :], 0.0, ALU.mult, ALU.add))
                c2.wait()
                c2.post(tt(W1[:, :, 1:], TC[:, gr, 0:SBN - 1], z[:, :, 0:SBN - 1], ALU.mult))
                tt(W2[:, :, 1:], TS[:, gr, 0:SBN - 1], z[:, :, 0:SBN - 1], ALU.mult).then_inc(z_ready, 1)
                dve.wait_ge(y_done, q + 1)
                for h in range(2):
                    dst = Y5[:, h, :, bass.ds(q * GQ * S5C, GQ * S5C)].rearrange("p s (g c) -> p g s c", g=GQ)
                    ts(dst, bank[2 + h][:, :].rearrange("p (g s c) -> p g s c", g=GQ, s=SBL), 1.0, None, ALU.mult).then_inc(y_taken, 1)
                assert c2.n == DT2, c2.n
            dve.wait_ge(y_taken, 2 * (S5G // GQ))
            Uf, Yf = (t[:, :, :, :].rearrange("p h s c -> p (h s) c") for t in (U, Y5))
            for h in range(2):
                hh = slice(h * SBL, (h + 1) * SBL)
                tt(Uf[:, hh, :], Uf[:, hh, :], bc(d_bc[:, :], 1, SBL), ALU.mult).then_inc(pre, 1)
                dve.wait_ge(pre, 2 * h + 1)
                tt(Yf[:, hh, :], Yf[:, hh, :], Uf[:, hh, :], ALU.add).then_inc(pre, 1)
            for j in range(SBL):
                jj = slice(2 * j, 2 * j + 2)
                dve.wait_ge(glu_done, j + 1)
                tt(Uf[:, jj, :], bank[j % 2][:, :].rearrange("p (a n) -> p a n", a=2), bc(b_bc[:, :], 1, 2), ALU.add).then_inc(glu_b, 1)
                if j:
                    k = slice(2 * j - 2, 2 * j)
                    dve.wait_ge(sig, j)
                    tt(Yf[:, k, :], Yf[:, k, :], Uf[:, k, :], ALU.mult).then_inc(s5_out, 1)
            k = slice(2 * SBL - 2, 2 * SBL)
            dve.wait_ge(sig, SBL)
            tt(Yf[:, k, :], Yf[:, k, :], Uf[:, k, :], ALU.mult).then_inc(s5_out, 1)

        @block.scalar
        def _(act):
            act.wait_ge(ld, 16 * 17)
            act.activation(w[:, 0, :], step[:, :], ACT.Exp).then_inc(s2, 1)
            act.wait_ge(tr0, 2)
            for r, C in enumerate((Cr, Ci)):
                act.activation(C[:, :, :].rearrange("p g c -> p (g c)"), bank[1][:, r * 256:(r + 1) * 256], ACT.Copy).then_inc(act0, 1)
            act.wait_ge(s1, env["s5_marks"][0])
            act.activation(r8[:, :], w[:, 1, :], ACT.Exp, scale=float(SBL)).then_inc(s2, 1)
            act.wait_ge(s2, 2)
            act.activation(w[:, 1, :], w[:, 1, :], ACT.Exp).then_inc(s2, 1)
            act.wait_ge(s1, env["s5_marks"][1])
            act.activation(w[:, 4, :], w[:, 2, :], ACT.Sin).then_inc(s2, 1)
            act.activation(w[:, 5, :], w[:, 6, :], ACT.Sin).then_inc(s2, 1)
            with act.Fori(0, S5G // GQ) as q:
                for h in range(2):
                    act.wait_ge(ut_done, q * 2 + h + 1)
                    act.activation(UT[:, :, h * P:(h + 1) * P], bank[h][:, :].rearrange("p (g b) -> p g b", g=GQ), ACT.Copy).then_inc(ut_taken, 1)
                act.wait_ge(mb_done, q + 1)
                b = bank[2][:, :].rearrange("p (g a k) -> p g a k", g=GQ, a=2)
                o = BmT[:, :, :, :].rearrange("p s g (a k) -> p s g a k", a=2)
                act.activation(o[:, 0], b, ACT.Copy)
                act.activation(o[:, 1, :, 0, :], b[:, :, 1, :], ACT.Copy)
                act.activation(o[:, 1, :, 1, :], b[:, :, 0, :], ACT.Copy).then_inc(mb_taken, 1)
                act.wait_ge(tm_done, q + 1)
                act.activation(Tm[:, :, :], bank[3][:, :].rearrange("p (g k) -> p g k", g=GQ), ACT.Copy).then_inc(tm_taken, 1)
            Yf = Y5[:, :, :, :].rearrange("p h s c -> p (h s) c")
            Uf = U[:, :, :, :].rearrange("p h s c -> p (h s) c")
            for h in range(2):
                hh = slice(h * SBL, (h + 1) * SBL)
                act.wait_ge(pre, 2 * h + 2)
                act.activation(Yf[:, hh, :], Yf[:, hh, :], ACT.Gelu_apprx_tanh).then_inc(gelu, 1)
            for j in range(SBL + 1):
                if j < SBL:
                    act.wait_ge(gt_done, j + 1)
                    if j >= 2:
                        act.wait_ge(glu_done, j - 1)
                    act.activation(BmT[:, j % 2, :, :], bank[2 + j % 2][:, :].rearrange("p (a b) -> p a b", a=4), ACT.Copy).then_inc(gt_taken, 1)
                if j:
                    jj = slice(2 * j - 2, 2 * j)
                    act.wait_ge(glu_b, j)
                    act.activation(Uf[:, jj, :], Uf[:, jj, :], ACT.Sigmoid).then_inc(sig, 1)

        @block.tensor
        def _(pe):
            pe.wait_ge(ld, 16 * 17)
            for r in range(2):
                ins = pe.transpose(bank[0][:, r * S5G:(r + 1) * S5G], anat[:, r, :, :].rearrange("g a p -> g (a p)"), ident[0:S5G, 0:S5G])
            ins.then_inc(tr0, 1)
            for r in range(2):
                for a in range(2):
                    ins = pe.transpose(bank[1][:, (2 * r + a) * P:(2 * r + a + 1) * P], cnat[:, r, a, :, :].rearrange("q j p -> q (j p)"), ident)
            ins.then_inc(tr0, 1)
            pe.wait_ge(act0, 2)
            pe.wait_ge(s1, 2)
            with pe.Fori(0, S5G // GQ) as q:
                for h in range(2):
                    pe.wait_ge(uc_ready, q * 2 + h + 1)
                    for gg in range(GQ):
                        ins = pe.transpose(bank[h][:, gg * P:(gg + 1) * P], Uc[:, h, gg, :], ident)
                    ins.then_inc(ut_done, 1)
                pe.wait_ge(mb_ready, q * 4 + 1)
                pe.wait_ge(y_taken, q * 2)
                for gg in range(GQ):
                    ins = pe.transpose(bank[2][:, gg * P:(gg + 1) * P], MB[:, gg, :], ident)
                ins.then_inc(mb_done, 1)
                pe.wait_ge(mb_ready, q * 4 + 3)
                for gg in range(GQ):
                    for s in range(SBL):
                        a = (SBL - 1 - s) * S5C
                        ins = pe.matmul(bank[3][:, gg * P:(gg + 1) * P], BZ[:, gg, a:a + LK], CZ[:, gg, a:a + LK],
                                        start=(s == 0), stop=(s == SBL - 1))
                ins.then_inc(tm_done, 1)
                pe.wait_ge(ut_taken, q * 2 + 2)
                pe.wait_ge(mb_taken, q + 1)
                for gg in range(GQ):
                    for k in range(2):
                        ins = pe.matmul(vbank[:, gg, k, :], BmT[:, k, gg, :], UT[:, gg, :], start=True, stop=True)
                ins.then_inc(v_done, 1)
                pe.wait_ge(tm_taken, q + 1)
                pe.wait_ge(mb_ready, q * 4 + 4)
                pe.wait_ge(z_ready, q + 1)
                for h in range(2):
                    for gg in range(GQ):
                        o = bank[2 + h][:, gg * P:(gg + 1) * P]
                        b = slice(h * P, (h + 1) * P)
                        pe.matmul(o, UT[:, gg, b], Tm[:, gg, :], start=True, stop=False)
                        pe.matmul(o, W1[:, gg, b], CZ[:, gg, SBL * S5C:], start=False, stop=False)
                        ins = pe.matmul(o, W2[:, gg, b], CM[:, gg, :], start=False, stop=True)
                ins.then_inc(y_done, 1)
            Yf = Y5[:, :, :, :].rearrange("p h s c -> p (h s) c")
            pe.wait_ge(y_taken, 2 * (S5G // GQ))
            for j in range(SBL + 1):
                if j < SBL:
                    pe.wait_ge(gelu, j // 4 + 1)
                    if j >= 2:
                        pe.wait_ge(gt_taken, j - 1)
                    for a in range(2):
                        for k in range(2):
                            ins = pe.transpose(bank[2 + j % 2][:, (2 * a + k) * P:(2 * a + k + 1) * P], Yf[:, 2 * j + a, k * P:(k + 1) * P], ident)
                    ins.then_inc(gt_done, 1)
                if j:
                    i = j - 1
                    pe.wait_ge(gt_taken, i + 1)
                    if i >= 2:
                        pe.wait_ge(glu_b, i - 1)
                    for a in range(2):
                        for k in range(2):
                            ins = pe.matmul(bank[i % 2][:, a * S5W:(a + 1) * S5W], BmT[:, i % 2, 2 * a + k, :], wglu[:, k, :], start=(k == 0), stop=(k == 1))
                    ins.then_inc(glu_done, 1)



CH, CD = 4, 256
MT = MEM // P


def mem_keys_values(nc, env, dram, KT_, V_):
    with ExitStack() as ctx:
        def sb(name, shape, dt=F32):
            return ctx.enter_context(nc.sbuf_tensor(name, shape, dt))

        sem = nc.alloc_semaphore
        wk, wv = sb("wck", [P, KT, D]), sb("wcv", [P, KT, D])
        mem = sb("mem_t", [P, MT, D])
        junk = sb("junk_m", [P, MT, D])
        ident = sb("cst_m", [P, P])
        nhalf = sb("nhalf_m", [P, MT])
        gm = sb("gm", [P, KT])
        ss, ms, rs = sb("ss_m", [P, MT]), sb("ms_m", [P, MT]), sb("rs_m", [P, MT])
        mT = sb("mT", [P, KT, MEM])
        bank = [ctx.enter_context(nc.psum_tensor(f"bankM{i}", [P, 512], F32)) for i in range(4)]
        ld, w_ld = sem("mem_loaded"), sem("wck_wcv_loaded")
        sq, msd, rsd, xs, done, taken = (sem("mem_squares"), sem("mem_mean"), sem("mem_rstd"), sem("mem_scaled"),
                                         sem("mem_results"), sem("mem_results_taken"))
        ctx.enter_context(nc.allow_non_contiguous_dma(reason="gains by rows, loaded once"))
        block = ctx.enter_context(nc.Block())

        @block.sync
        def _(sp):
            sp.dma_start(mem[:, :, :], dram["mem"][0].rearrange("(m p) d -> p m d", p=P)).then_inc(ld, 16)
            sp.dma_start(ident[:, :], dram["cst"][:, K_ID:K_ID + P]).then_inc(ld, 16)
            sp.dma_start(nhalf[:, :], dram["cst"][:, K_HALF:K_HALF + MT]).then_inc(ld, 16)
            sp.dma_start(gm[:, :], dram["mem_norm_g"].rearrange("(k p) -> p k", p=P)).then_inc(ld, 16)
            for wt, src in ((wk, "w_ck"), (wv, "w_cv")):
                for h in range(2):
                    sp.dma_start(wt[:, 4 * h:4 * h + 4, :], dram[src][0].rearrange("(k p) n -> p k n", p=P)[:, 4 * h:4 * h + 4, :]).then_inc(w_ld, 16)

        @block.gpsimd
        def _(pool):
            pool.wait_ge(ld, 64)
            pool.wait_ge(msd, 1)
            pool.tensor_tensor(rs[:, :], ms[:, :], nhalf[:, :], ALU.pow).then_inc(rsd, 1)

        @block.vector
        def _(dve):
            dve.wait_ge(sq, MT)
            dve.tensor_scalar(ms[:, :], ss[:, :], 1.0 / D, EPS, ALU.mult, ALU.add).then_inc(msd, 1)
            dve.wait_ge(rsd, 1)
            for m in range(MT):
                dve.tensor_scalar(mem[:, m, :], mem[:, m, :], rs[:, m:m + 1], None, ALU.mult).then_inc(xs, 1)

        @block.scalar
        def _(act):
            act.wait_ge(ld, 64)
            for m in range(MT):
                act.activation(junk[:, m, :], mem[:, m, :], ACT.Square, accum_out=ss[:, m:m + 1]).then_inc(sq, 1)
            n = 0
            for kt in range(0, KT, 2):
                act.wait_ge(done, n + 1)
                for j in range(2):
                    ins = act.activation(mT[:, kt + j, :], bank[n % 4][:, j * MEM:(j + 1) * MEM], ACT.Copy, scale=gm[:, kt + j:kt + j + 1])
                ins.then_inc(taken, 1)
                n += 1
            for e in range(0, KT, 2):
                act.wait_ge(done, n + 1)
                act.activation(KT_[:, e:e + 2, :], bank[n % 4][:, :].rearrange("p (a b) -> p a b", a=2), ACT.Copy).then_inc(taken, 1)
                n += 1
            for m in range(MT):
                for h in range(2):
                    act.wait_ge(done, n + 1)
                    act.activation(V_[:, m, h * 512:(h + 1) * 512], bank[n % 4][:, :], ACT.Copy).then_inc(taken, 1)
                    n += 1

        @block.tensor
        def _(pe):
            n = 0

            def slot(n):
                if n >= 4:
                    pe.wait_ge(taken, n - 3)
                return bank[n % 4]

            pe.wait_ge(ld, 64)
            pe.wait_ge(xs, MT)
            for kt in range(0, KT, 2):
                o = slot(n)
                for j in range(2):
                    for m in range(MT):
                        ins = pe.transpose(o[:, j * MEM + m * P:j * MEM + (m + 1) * P], mem[:, m, (kt + j) * P:(kt + j + 1) * P], ident[:, :])
                ins.then_inc(done, 1)
                n += 1
            pe.wait_ge(taken, KT // 2)
            pe.wait_ge(w_ld, 64)
            for e in range(0, KT, 2):
                o = slot(n)
                for j in range(2):
                    for kt in range(KT):
                        ins = pe.matmul(o[:, j * MEM:(j + 1) * MEM], wk[:, kt, (e + j) * P:(e + j + 1) * P], mT[:, kt, :], start=(kt == 0), stop=(kt == KT - 1))
                ins.then_inc(done, 1)
                n += 1
            for m in range(MT):
                for h in range(2):
                    o = slot(n)
                    for kt in range(KT):
                        ins = pe.matmul(o[:, :], mT[:, kt, m * P:(m + 1) * P], wv[:, kt, h * 512:(h + 1) * 512], start=(kt == 0), stop=(kt == KT - 1))
                    ins.then_inc(done, 1)
                    n += 1


def cross_and_router(nc, env, dram, KT_, V_, logits):
    with ExitStack() as ctx:
        def sb(name, shape, dt=F32):
            return ctx.enter_context(nc.sbuf_tensor(name, shape, dt))

        sem = nc.alloc_semaphore
        wo_, wq, wc = sb("w_out_t", [P, KT, D]), sb("w_cq_t", [P, KT, D]), sb("w_co_t", [P, KT, D])
        wr = sb("w_route", [P, KT, NGR + NE])
        br = sb("b_route", [P, NGR + NE])
        ident = sb("cst_c", [P, P])
        nhalf = sb("nhalf_c", [P, GC])
        gc_, gf = sb("g_cross", [P, KT]), sb("g_ffn", [P, KT])
        X = sb("Xc", [P, GC, D])
        H = sb("Hc", [P, GC, D])
        A1 = sb("A1", [P, KT, GT])
        A2 = sb("A2", [P, KT, GT])
        Pm = sb("Pm", [P, 2, CH, MEM])
        ss, ms, rs = sb("ss_c", [P, 2, GC]), sb("ms_c", [P, 2, GC]), sb("rs_c", [P, 2, GC])
        mx, nm, sm, rc = (sb(n, [P, GC, CH]) for n in ("mx", "nm", "sm", "rc"))
        bank = [ctx.enter_context(nc.psum_tensor(f"bankC{i}", [P, 512], F32)) for i in range(8)]

        ld, w_ld, cat_ld, h_ld = sem("c_consts_loaded"), [sem(f"{w}_loaded") for w in ("w_out", "w_cq", "w_co")], sem("cat_loaded"), sem("x_res_loaded")
        tr, tr_taken = sem("transposes_done"), sem("transposes_taken")
        res, res_taken = sem("residual_products"), sem("residual_added")
        sq, msd, rsd, xs = sem("c_squares"), sem("c_mean"), sem("c_rstd"), sem("c_scaled")
        qd, q_taken = sem("q_done"), sem("q_taken")
        sc, p_exp, p_max, p_ready = sem("scores_done"), sem("scores_exp"), sem("scores_max"), sem("probs_ready")
        pt, pt_taken = sem("probsT_done"), sem("probsT_taken")
        od, o_taken = sem("o_done"), sem("o_taken")
        rt, rt_taken = sem("router_done"), sem("logits_taken")
        h_st, x_st = sem("h_stored"), sem("xn_stored")
        dve_c = sem("dve_steps_c")
        DVE_TURN = env["dve_c"]
        ctx.enter_context(nc.allow_non_contiguous_dma(reason="gains by rows, loaded once"))
        block = ctx.enter_context(nc.Block())

        @block.sync
        def _(sp):
            xv, cv, hv, nv = (dram[k].rearrange("(g c p) d -> g p c d", c=GC, p=P) if k != "x" else
                              dram[k][0].rearrange("(g c p) d -> g p c d", c=GC, p=P) for k in ("x", "cat", "h_scr", "xn_scr"))
            sp.dma_start(X[:, :, :], cv[0]).then_inc(cat_ld, 16)
            sp.dma_start(ident[:, :], dram["cst"][:, K_ID:K_ID + P]).then_inc(ld, 16)
            sp.dma_start(nhalf[:, :], dram["cst"][:, K_HALF:K_HALF + GC]).then_inc(ld, 16)
            sp.dma_start(gc_[:, :], dram["norm_cross_g"][0].rearrange("(k p) -> p k", p=P)).then_inc(ld, 16)
            sp.dma_start(gf[:, :], dram["norm_ffn_g"][0].rearrange("(k p) -> p k", p=P)).then_inc(ld, 16)
            sp.dma_start(wr[:, :, 0:NGR], dram["w_route_group"][0].rearrange("(k p) n -> p k n", p=P)).then_inc(ld, 16)
            sp.dma_start(wr[:, :, NGR:], dram["w_route_expert"][0].rearrange("(k p) n -> p k n", p=P)).then_inc(ld, 16)
            sp.dma_start(br[:, 0:NGR], dram["b_route_group"][0].partition_broadcast(P)).then_inc(ld, 16)
            sp.dma_start(br[:, NGR:], dram["b_route_expert"][0].partition_broadcast(P)).then_inc(ld, 16)
            for i, (wt, src) in enumerate(((wo_, "w_out"), (wq, "w_cq"), (wc, "w_co"))):
                for h in range(2):
                    sp.dma_start(wt[:, 4 * h:4 * h + 4, :], dram[src][0].rearrange("(k p) n -> p k n", p=P)[:, 4 * h:4 * h + 4, :]).then_inc(w_ld[i], 16)
                if i == 0:
                    sp.dma_start(H[:, :, :], xv[0]).then_inc(h_ld, 16)
            with sp.Fori(0, NG - 1) as g:
                sp.wait_ge(xs, g * 2 * GC + 2 * GC)
                sp.dma_start(nv[bass.ds(g, 1)].squeeze(0), X[:, :, :]).then_inc(x_st, 16)
                sp.dma_start(hv[bass.ds(g, 1)].squeeze(0), H[:, :, :]).then_inc(h_st, 16)
                sp.wait_ge(h_st, g * 16 + 16)
                sp.dma_start(H[:, :, :], xv[bass.ds(g + 1, 1)].squeeze(0)).then_inc(h_ld, 16)
                sp.wait_ge(x_st, g * 16 + 16)
                sp.wait_ge(tr, g * 3 * KT + 3 * KT)
                sp.dma_start(X[:, :, :], cv[bass.ds(g + 1, 1)].squeeze(0)).then_inc(cat_ld, 16)
            sp.wait_ge(xs, NG * 2 * GC)
            sp.dma_start(nv[NG - 1], X[:, :, :]).then_inc(x_st, 16)
            sp.dma_start(hv[NG - 1], H[:, :, :]).then_inc(h_st, 16)
            sp.wait_ge(x_st, 16 * NG)
            sp.wait_ge(h_st, 16 * NG)

        @block.gpsimd
        def _(pool):
            pool.wait_ge(ld, 16 * 8)
            with pool.Fori(0, NG) as g:
                for i in range(2):
                    for c in range(GC):
                        pool.wait_ge(msd, g * 2 * GC + i * GC + c + 1)
                        pool.tensor_tensor(rs[:, i, c:c + 1], ms[:, i, c:c + 1], nhalf[:, 0:1], ALU.pow).then_inc(rsd, 1)

        @block.scalar
        def _(act):
            act.wait_ge(ld, 16 * 8)
            with act.Fori(0, NG) as g:
                n = 0
                for kt in range(KT):
                    act.wait_ge(tr, g * 3 * KT + kt + 1)
                    act.activation(A1[:, kt, :], bank[n % 4][:, :], ACT.Copy).then_inc(tr_taken, 1)
                    n += 1
                for i, (A, gain) in enumerate(((A1, gc_), (A1, gf))):
                    for c in range(GC):
                        act.wait_ge(res_taken, g * 4 * GC + i * 2 * GC + 2 * c + 2)
                        if i == 0 and c == 0:
                            act.wait_ge(pt, g * 2 * GC)
                        act.wait_ge(sq, g * 2 * GC + i * GC + c)
                        act.activation(Pm[:, 0, :, :].rearrange("p h m -> p (h m)"), H[:, c, :], ACT.Square, accum_out=ss[:, i, c:c + 1]).then_inc(sq, 1)
                    for kt in range(KT):
                        act.wait_ge(tr, g * 3 * KT + (i + 1) * KT + kt + 1)
                        act.activation(A[:, kt, :], bank[n % 4][:, :], ACT.Copy, scale=gain[:, kt:kt + 1]).then_inc(tr_taken, 1)
                        n += 1
                    if i:
                        break
                    for e in range(KT):
                        act.wait_ge(qd, g * KT + e + 1)
                        act.activation(A2[:, e, :], bank[n % 4][:, :], ACT.Copy).then_inc(q_taken, 1)
                        n += 1
                    def take_pt(c):
                        for j in range(2):
                            act.wait_ge(pt, g * 2 * GC + 2 * c + j + 1)
                            act.activation(A1[:, 4 * j:4 * j + 4, c * P:(c + 1) * P], bank[6 + j][:, :].rearrange("p (a b) -> p a b", a=4), ACT.Copy).then_inc(pt_taken, 1)

                    for c in range(GC):
                        for j in range(2):
                            act.wait_ge(p_max, g * 2 * GC + 2 * c + j + 1)
                            if c >= 2:
                                act.wait_ge(pt, g * 2 * GC + 2 * (c - 2) + 2)
                            for k in range(2):
                                h = 2 * j + k
                                act.activation(Pm[:, c % 2, h, :], bank[4 + j][:, k * MEM:(k + 1) * MEM], ACT.Exp,
                                               bias=nm[:, c, h:h + 1], scale=CD ** -0.5, accum_out=sm[:, c, h:h + 1]).then_inc(p_exp, 1)
                        if c:
                            take_pt(c - 1)
                    take_pt(GC - 1)
                    for e in range(KT):
                        act.wait_ge(od, g * KT + e + 1)
                        act.activation(A2[:, e, :], bank[n % 4][:, :], ACT.Copy).then_inc(o_taken, 1)
                        n += 1

        @block.vector
        def _(dve):
            dve.wait_ge(ld, 16 * 8)
            with dve.Fori(0, NG) as g:
                ch = Chain(dve, dve_c, g, DVE_TURN)

                def residual(i):
                    for c in range(GC):
                        for j in range(2):
                            dve.wait_ge(res, g * 4 * GC + i * 2 * GC + 2 * c + j + 1)
                            hh = H[:, c, j * 512:(j + 1) * 512]
                            dve.tensor_tensor(hh, hh, bank[4 + j][:, :], ALU.add).then_inc(res_taken, 1)
                        if c:
                            scale(i, c - 1)
                    scale(i, GC - 1)

                def scale(i, c):
                    dve.wait_ge(sq, g * 2 * GC + i * GC + c + 1)
                    dve.tensor_scalar(ms[:, i, c:c + 1], ss[:, i, c:c + 1], 1.0 / D, EPS, ALU.mult, ALU.add).then_inc(msd, 1)
                    dve.wait_ge(rsd, g * 2 * GC + i * GC + c + 1)
                    dve.tensor_scalar(X[:, c, :], H[:, c, :], rs[:, i, c:c + 1], None, ALU.mult).then_inc(xs, 1)

                dve.wait_ge(h_ld, g * 16 + 16)
                dve.wait_ge(tr, g * 3 * KT + KT)
                residual(0)

                def probs(c):
                    dve.wait_ge(p_exp, g * CH * GC + CH * c + CH)
                    ch.post(dve.reciprocal(rc[:, c, :], sm[:, c, :]))
                    ch.wait()
                    dve.tensor_tensor(Pm[:, c % 2, :, :], Pm[:, c % 2, :, :], bc(rc[:, c, :], 2, MEM), ALU.mult).then_inc(p_ready, 1)

                for c in range(GC):
                    for j in range(2):
                        dve.wait_ge(sc, g * 2 * GC + 2 * c + j + 1)
                        hh = slice(2 * j, 2 * j + 2)
                        ch.post(dve.tensor_reduce(mx[:, c, hh], bank[4 + j][:, :].rearrange("p (a b) -> p a b", a=2), AX.X, ALU.max))
                        ch.wait()
                        dve.tensor_scalar(nm[:, c, hh], mx[:, c, hh], -CD ** -0.5, None, ALU.mult).then_inc(p_max, 1)
                    if c:
                        probs(c - 1)
                probs(GC - 1)
                residual(1)
                dve.wait_ge(rt, g + 1)
                o = logits[:, bass.ds(g * GC, GC), :]
                dve.tensor_tensor(o, bank[6][:, 0:GC * (NGR + NE)].rearrange("p (c n) -> p c n", c=GC), bc(br[:, :], 1, GC), ALU.add).then_inc(rt_taken, 1)
                assert ch.n == DVE_TURN, ch.n

        @block.tensor
        def _(pe):
            pe.wait_ge(ld, 16 * 8)
            with pe.Fori(0, NG) as g:
                def transposes(i, n0, before):
                    for kt in range(KT):
                        n = n0 + kt
                        before(kt)
                        for c in range(GC):
                            ins = pe.transpose(bank[n % 4][:, c * P:(c + 1) * P], X[:, c, kt * P:(kt + 1) * P], ident[:, :])
                        ins.then_inc(tr, 1)

                def add_products(i, A, w):
                    for c in range(GC):
                        for j in range(2):
                            if c == 0:
                                if i == 0:
                                    pe.wait_ge(res_taken, g * 4 * GC)
                                else:
                                    pe.wait_ge(p_exp, g * CH * GC + CH * GC)
                            else:
                                pe.wait_ge(res_taken, g * 4 * GC + i * 2 * GC + 2 * c + j - 1)
                            for kt in range(KT):
                                ins = pe.matmul(bank[4 + j][:, :], A[:, kt, c * P:(c + 1) * P], w[:, kt, j * 512:(j + 1) * 512], start=(kt == 0), stop=(kt == KT - 1))
                            ins.then_inc(res, 1)

                pe.wait_ge(cat_ld, g * 16 + 16)
                transposes(0, 0, lambda kt: pe.wait_ge(tr_taken, g * 3 * KT + max(kt - 3, 0)))
                pe.wait_ge(tr_taken, g * 3 * KT + KT)
                pe.wait_ge(w_ld[0], 32)
                pe.wait_ge(rt_taken, g)
                add_products(0, A1, wo_)
                pe.wait_ge(xs, g * 2 * GC + GC)
                transposes(1, KT, lambda kt: pe.wait_ge(tr_taken, g * 3 * KT + KT + kt - 3))
                pe.wait_ge(tr_taken, g * 3 * KT + 2 * KT)
                pe.wait_ge(w_ld[1], 32)
                for e in range(KT):
                    if e >= 4:
                        pe.wait_ge(q_taken, g * KT + e - 3)
                    for kt in range(KT):
                        ins = pe.matmul(bank[e % 4][:, :], wq[:, kt, e * P:(e + 1) * P], A1[:, kt, :], start=(kt == 0), stop=(kt == KT - 1))
                    ins.then_inc(qd, 1)
                pe.wait_ge(q_taken, g * KT + KT)

                def turn_probs(c):
                    pe.wait_ge(p_ready, g * GC + c + 1)
                    for j in range(2):
                        if c:
                            pe.wait_ge(pt_taken, g * 2 * GC + 2 * (c - 1) + j + 1)
                        for k in range(4):
                            h, m = 2 * j + k // 2, k % 2
                            ins = pe.transpose(bank[6 + j][:, k * P:(k + 1) * P], Pm[:, c % 2, h, m * P:(m + 1) * P], ident[:, :])
                        ins.then_inc(pt, 1)

                for c in range(GC):
                    for j in range(2):
                        if c:
                            pe.wait_ge(p_exp, g * CH * GC + CH * (c - 1) + 2 * j + 2)
                        for k in range(2):
                            h = 2 * j + k
                            for e in range(2):
                                ins = pe.matmul(bank[4 + j][:, k * MEM:(k + 1) * MEM], A2[:, 2 * h + e, c * P:(c + 1) * P], KT_[:, 2 * h + e, :], start=(e == 0), stop=(e == 1))
                        ins.then_inc(sc, 1)
                    if c:
                        turn_probs(c - 1)
                turn_probs(GC - 1)
                pe.wait_ge(pt_taken, g * 2 * GC + 2 * GC)
                for e in range(KT):
                    if e >= 4:
                        pe.wait_ge(o_taken, g * KT + e - 3)
                    h = e // 2
                    for m in range(MT):
                        ins = pe.matmul(bank[e % 4][:, :], V_[:, m, e * P:(e + 1) * P], A1[:, 2 * h + m, :], start=(m == 0), stop=(m == MT - 1))
                    ins.then_inc(od, 1)
                pe.wait_ge(o_taken, g * KT + KT)
                pe.wait_ge(w_ld[2], 32)
                add_products(1, A2, wc)
                pe.wait_ge(xs, g * 2 * GC + 2 * GC)
                transposes(2, 2 * KT, lambda kt: pe.wait_ge(tr_taken, g * 3 * KT + 2 * KT + max(kt - 3, 0)))
                pe.wait_ge(tr_taken, g * 3 * KT + 3 * KT)
                for c in range(GC):
                    for kt in range(KT):
                        a = c * (NGR + NE)
                        ins = pe.matmul(bank[6][:, a:a + NGR + NE], A1[:, kt, c * P:(c + 1) * P], wr[:, kt, :], start=(kt == 0), stop=(kt == KT - 1))
                ins.then_inc(rt, 1)



HB = 2
SLOTS = 3
ROWS = NB * P
WHOLE = 12582912.0
MAX_TURNS = NB // HB - 1
MIN_TURNS = (USED_MIN - 1) // HB
PL_BLOCK, PL_EXPERT, PL_FREE, PL_TURNS, PL_USED, PL_END = np.cumsum([0, NB, NE, NE, 1, 1]).tolist()


def route(nc, env, dram, logits, gates, dest, destf, plan):
    with ExitStack() as ctx:
        def sb(name, shape, dt=F32):
            return ctx.enter_context(nc.sbuf_tensor(name, shape, dt))

        sem = nc.alloc_semaphore
        cst = sb("cst_r", [P, K_GAM])
        G4, O4 = sb("G4", [P, NCH, NGR]), sb("O4", [P, NCH, NGR])
        t4 = sb("t4", [P, NCH, NGR])
        e32 = sb("e32", [P, NCH, NGR, EPG])
        E8, t8, m8, O8 = (sb(n, [P, NCH, EPG]) for n in ("E8", "t8", "m8", "O8"))
        c1 = sb("c1", [P, 8, NCH])
        oh = sb("oh", [P, 2, NCH, NE])
        pos = sb("pos", [P, NCH, NE])
        both, before, cum, again = (sb(n, [P, NE, NCH]) for n in ("both", "before", "cum", "again"))
        nblk, start, end, used, rank, eq, t32 = (sb(n, [P, NE]) for n in ("nblk", "start", "end", "used", "rank", "eq", "t32"))
        cols, turns = sb("cols", [P, 4]), sb("turns_f", [P, 1])
        bank = [ctx.enter_context(nc.psum_tensor(f"bankR{i}", [P, 512], F32)) for i in range(2)]
        ld, s, a_s, cnt, marks = sem("r_consts"), sem("route_steps"), sem("route_exp"), sem("counts_done"), sem("pairs_marked_r")
        ready = sem("again_ready")
        lt, ones, one = cst[:, K_LT:K_LT + P], cst[:, K_ONE:K_ONE + P], cst[:, K_ONE:K_ONE + NE]

        def flat(t):
            return t[:, :, :].rearrange("p e c -> p (e c)")

        def by_c(t):
            return t[:, :, :].rearrange("p e c -> p c e")

        block = ctx.enter_context(nc.Block())

        @block.sync
        def _(sp):
            sp.dma_start(cst[:, :], dram["cst"][:, 0:K_GAM]).then_inc(ld, 16)

        @block.scalar
        def _(act):
            act.wait_ge(s, env["r_marks"][0])
            act.activation(t4[:, :, :], G4[:, :, :], ACT.Exp).then_inc(a_s, 1)
            act.wait_ge(s, env["r_marks"][1])
            act.activation(E8[:, :, :], t8[:, :, :], ACT.Exp).then_inc(a_s, 1)

        @block.vector
        def _(dve):
            ch = Chain(dve, s)
            tt, ts, stt, red = dve.tensor_tensor, dve.tensor_scalar, dve.scalar_tensor_tensor, dve.tensor_reduce
            seen = []
            dve.memset(again[:, :, :], 1.0).then_inc(ready, 1)
            dve.wait_ge(ready, 1)
            dve.memset(again[:, :, 0:1], 0.0).then_inc(ready, 1)
            dve.wait_ge(ready, 2)

            def do(f, *a):
                ch.post(f(*a))
                ch.wait()

            def first(o, x, m, n, idx, t):
                iota = bc(cst[:, K_IOTA:K_IOTA + n], 1, NCH)
                do(tt, t, x, bc(m, 2, n), ALU.is_lt)
                do(stt, t, t, 1000.0, iota, ALU.mult, ALU.add)
                do(red, idx, t, AX.X, ALU.min)
                do(tt, o, iota, bc(idx, 2, n), ALU.is_equal)

            GM, GS, GI, M1, I1, M2, I2, X = (c1[:, i, :] for i in range(8))
            gl = logits[:, :, 0:NGR]
            dve.wait_ge(ld, 16)
            do(red, GM, gl, AX.X, ALU.max)
            first(O4[:, :, :], gl, GM, NGR, GI, t4[:, :, :])
            do(tt, G4[:, :, :], gl, bc(GM, 2, NGR), ALU.subtract)
            seen.append(ch.n)
            el = logits[:, :, NGR:].rearrange("p c (g e) -> p c g e", g=NGR)
            for g in range(NGR):
                ch.post(tt(e32[:, :, g, :], el[:, :, g, :], bc(O4[:, :, g], 2, EPG), ALU.mult))
            ch.wait()
            do(red, m8[:, :, :], e32[:, :, :, :].rearrange("p c g e -> p c e g"), AX.X, ALU.add)
            do(red, M1, m8[:, :, :], AX.X, ALU.max)
            do(tt, t8[:, :, :], m8[:, :, :], bc(M1, 2, EPG), ALU.subtract)
            seen.append(ch.n)
            dve.wait_ge(a_s, 2)
            do(red, GS, t4[:, :, :], AX.X, ALU.add)
            do(red, M1, E8[:, :, :], AX.X, ALU.max)
            first(O8[:, :, :], E8[:, :, :], M1, EPG, I1, t8[:, :, :])
            do(stt, m8[:, :, :], O8[:, :, :], -4.0, E8[:, :, :], ALU.mult, ALU.add)
            do(red, M2, m8[:, :, :], AX.X, ALU.max)
            first(O8[:, :, :], m8[:, :, :], M2, EPG, I2, t8[:, :, :])
            do(tt, X, M1, M2, ALU.add)
            do(tt, X, X, GS, ALU.mult)
            do(dve.reciprocal, X, X)
            do(tt, gates[:, 0, :], M1, X, ALU.mult)
            do(tt, gates[:, 1, :], M2, X, ALU.mult)
            iota = bc(cst[:, K_IOTA:K_IOTA + NE], 1, NCH)
            for k, I in enumerate((I1, I2)):
                do(stt, I, GI, float(EPG), I, ALU.mult, ALU.add)
                do(tt, oh[:, k, :, :], iota, bc(I, 2, NE), ALU.is_equal)
            tt(by_c(both), oh[:, 0, :, :], oh[:, 1, :, :], ALU.add).then_inc(marks, 1)
            dve.wait_ge(marks, 1)
            do(dve.tensor_tensor_scan, flat(cum), flat(again), flat(both), 0.0, ALU.mult, ALU.add)
            tt(before[:, :, :], cum[:, :, :], both[:, :, :], ALU.subtract).then_inc(marks, 1)
            dve.wait_ge(cnt, 1)
            do(ts, nblk[:, :], bank[1][:, 0:NE], 1.0 / P, 0.5 - 0.5 / P, ALU.mult, ALU.add)
            do(ts, nblk[:, :], nblk[:, :], WHOLE, None, ALU.add)
            do(ts, nblk[:, :], nblk[:, :], -WHOLE, None, ALU.add)
            do(dve.tensor_tensor_scan, end[:, :], one, nblk[:, :], 0.0, ALU.mult, ALU.add)
            do(ts, used[:, :], nblk[:, :], 0.0, None, ALU.is_gt)
            do(dve.tensor_tensor_scan, rank[:, :], one, used[:, :], 0.0, ALU.mult, ALU.add)
            here = cst[:, K_TOK:K_TOK + 1]
            do(ts, eq[:, :], rank[:, :], -1.0, here, ALU.add, ALU.is_equal)
            do(tt, eq[:, :], eq[:, :], used[:, :], ALU.mult)
            do(tt, t32[:, :], eq[:, :], cst[:, K_IOTA:K_IOTA + NE], ALU.mult)
            do(red, cols[:, 0:1], t32[:, :], AX.X, ALU.add)
            do(tt, t32[:, :], eq[:, :], end[:, :], ALU.mult)
            do(red, cols[:, 1:2], t32[:, :], AX.X, ALU.add)
            do(stt, t32[:, :], end[:, :], here, used[:, :], ALU.is_le, ALU.mult)
            do(red, cols[:, 3:4], t32[:, :], AX.X, ALU.add)
            do(ts, cols[:, 2:3], rank[:, NE - 1:NE], -1.0, None, ALU.add)
            tt(cols[:, 2:3], cols[:, 2:3], cols[:, 3:4], ALU.min).then_inc(marks, 1)
            do(ts, turns[:, :], end[:, NE - 1:NE], 1.0 / HB, -0.5 - 0.25, ALU.mult, ALU.add)
            do(ts, turns[:, :], turns[:, :], WHOLE, None, ALU.add)
            do(ts, turns[:, :], turns[:, :], -WHOLE, float(MAX_TURNS), ALU.add, ALU.min)
            do(dve.tensor_copy, plan[:, PL_TURNS:PL_TURNS + 1], turns[0:1, :])
            do(dve.tensor_copy, plan[:, PL_USED:PL_USED + 1], rank[0:1, NE - 1:NE])
            dve.wait_ge(cnt, 2)
            do(dve.memset, plan[:, PL_FREE:PL_FREE + SLOTS], 0)
            do(dve.tensor_copy, plan[:, 0:PL_FREE], bank[1][0:1, 2 * NE:2 * NE + PL_FREE])
            do(dve.tensor_copy, plan[:, PL_FREE + SLOTS:PL_TURNS], bank[1][0:1, 2 * NE + PL_FREE:2 * NE + PL_TURNS - SLOTS])
            tt(start[:, :], end[:, :], nblk[:, :], ALU.subtract).then_inc(marks, 1)
            dve.wait_ge(marks, 4)
            do(ts, start[:, :], start[:, :], float(P), None, ALU.mult)
            do(tt, pos[:, :, :], bank[0][:, :].rearrange("p (e c) -> p c e", c=NCH), bc(start[:, :], 1, NCH), ALU.add)
            for k in range(2):
                do(tt, oh[:, k, :, :], pos[:, :, :], oh[:, k, :, :], ALU.mult)
                do(red, destf[:, k, :], oh[:, k, :, :], AX.X, ALU.add)
            do(dve.tensor_copy, dest[:, :, :], destf[:, :, :])
            assert tuple(seen) == env["r_marks"], seen

        @block.tensor
        def _(pe):
            pe.wait_ge(ld, 16)
            pe.wait_ge(marks, 1)
            pe.matmul(bank[0][:, :], lt, flat(both), start=True, stop=False)
            pe.wait_ge(marks, 2)
            pe.matmul(bank[0][:, :], ones, flat(before), start=False, stop=True)
            pe.matmul(bank[1][:, 0:NE], ones, cum[:, :, NCH - 1], start=True, stop=True).then_inc(cnt, 1)
            pe.wait_ge(marks, 3)
            for c, n, at in ((2, NB, 0), (0, NE, PL_EXPERT), (1, NE, PL_FREE)):
                ins = pe.transpose(bank[1][0:1, 2 * NE + at:2 * NE + at + n], cols[0:n, c:c + 1], cst[0:n, K_ID:K_ID + n])
            ins.then_inc(cnt, 1)


def experts(nc, env, dram, destf, plan):
    FT = DE // P
    with ExitStack() as ctx:
        def sb(name, shape, dt=F32):
            return ctx.enter_context(nc.sbuf_tensor(name, shape, dt))

        sem = nc.alloc_semaphore
        wg, wu, wd = sb("wg", [P, SLOTS, KT, DE]), sb("wu", [P, SLOTS, KT, DE]), sb("wd", [P, SLOTS, FT, D])
        xr = [sb(f"xr{i}", [P, D]) for i in range(HB)]
        xT = [sb(f"xT{i}", [P, KT, P]) for i in range(HB)]
        sg = [sb(f"sg{i}", [P, DE]) for i in range(HB)]
        hT = [sb(f"hT{i}", [P, FT, P]) for i in range(HB)]
        y = [sb(f"y{i}", [P, D]) for i in range(HB)]
        ident, iota, tok = sb("cst_e", [P, P]), sb("iota_e", [P, P]), sb("tok_e", [P, NCH])
        in_blk, at_row = sb("in_block", [P, 2 * NCH, NB]), sb("at_row", [P, 2 * NCH, P])
        blk, off = sb("blk", [P, 2 * NCH]), sb("off", [P, 2 * NCH])
        rows_of = sb("rows_of", [P, NB], U32)
        gf = sb("g_ffn_e", [P, KT])
        bank = [ctx.enter_context(nc.psum_tensor(f"bankE{i}", [P, 512], F32)) for i in range(8)]
        ld = sem("e_consts")
        first_ld = [sem(f"first_{n}_loaded") for n in ("wg", "wu", "wd")]
        w_ld = [sem(f"weights_loaded{j}") for j in range(SLOTS)]
        x_ld = [sem(f"rows_gathered{i}") for i in range(HB)]
        lists, marked, listed, rows_ok = sem("list_steps"), sem("pairs_marked"), sem("rows_listed"), sem("rows_known")
        xt, xt_t, gd, ud, sil, hr, ht, ht_t, yd, y_t = (sem(n) for n in (
            "xT_done", "xT_taken", "gate_done", "up_done", "silu_done_e", "h_ready", "hT_done", "hT_taken", "down_done", "y_taken"))
        y_st = [sem(f"y_stored{i}") for i in range(HB)]
        y_end = sem("last_y_stored")
        NT = NB // HB
        ctx.enter_context(nc.allow_non_contiguous_dma(reason="gains by rows, loaded once"))
        block = ctx.enter_context(nc.Block())

        def turns_used(eng):
            return eng.value_load(plan[0:1, PL_TURNS:PL_TURNS + 1], min_val=MIN_TURNS, max_val=MAX_TURNS)

        @block.sync
        def _(sp):
            sp.dma_start(ident[:, :], dram["cst"][:, K_ID:K_ID + P]).then_inc(ld, 16)
            wv = [dram[n][0].rearrange("e (k p) f -> e p k f", p=P) for n in ("w_gate", "w_up", "w_down")]
            here = (wg, wu, wd)

            def expert(u):
                return sp.value_load(plan[0:1, bass.ds(PL_EXPERT + u, 1)], min_val=0, max_val=NE - 1)

            def weights(u, j):
                e = expert(u)
                free = sp.value_load(plan[0:1, bass.ds(PL_FREE + u, 1)], min_val=0, max_val=NB)
                for w, src, used in zip(here, wv, (gd, ud, yd)):
                    sp.wait_ge(used, free * 2 if used is yd else free)
                    sp.dma_start(w[:, j, :, :], src[bass.ds(e, 1)].squeeze(0)).then_inc(w_ld[j], 16)

            e0 = expert(0)
            for w, src, loaded in zip(here, wv, first_ld):
                sp.dma_start(w[:, 0, :, :], src[bass.ds(e0, 1)].squeeze(0)).then_inc(loaded, 16)
            sp.dma_start(iota[:, :], dram["cst"][:, K_IOTA:K_IOTA + P]).then_inc(ld, 16)
            sp.dma_start(tok[:, :], dram["cst"][:, K_TOK:K_TOK + NCH]).then_inc(ld, 16)
            sp.dma_start(gf[:, :], dram["norm_ffn_g"][0].rearrange("(k p) -> p k", p=P)).then_inc(ld, 16)
            e1 = expert(1)
            for w, src in zip(here, wv):
                sp.dma_start(w[:, 1, :, :], src[bass.ds(e1, 1)].squeeze(0)).then_inc(w_ld[1], 16)
            n_used = sp.value_load(plan[0:1, PL_USED:PL_USED + 1], min_val=2, max_val=NE)
            with sp.Fori(0, NE // SLOTS) as t:
                for i in range(SLOTS):
                    u = t * SLOTS + 2 + i
                    with sp.If(u < n_used):
                        weights(u, (2 + i) % SLOTS)

        @block.gpsimd
        def _(pool):
            used = turns_used(pool)
            pool.wait_ge(rows_ok, 1)

            def gather(b):
                if b >= HB:
                    pool.wait_ge(xt, 2 * (b - HB) + 2)
                pool.indirect_dma_start(xr[b % HB][:, :], None, dram["xn_scr"], bass.IndirectOffsetOnAxis(ap=rows_of[:, b:b + 1], axis=0)).then_inc(x_ld[b % HB], 16)

            for b in range(USED_MIN):
                gather(b)
            for t in range(USED_MIN // HB, NT):
                with pool.If(used + 1 > t):
                    for i in range(HB):
                        gather(HB * t + i)

        def steps(eng, first, step, last):
            used = turns_used(eng)
            first()
            with eng.Fori(0, MAX_TURNS) as t, eng.If(t < used):
                step(t * HB + 1, 1, t)
                step(t * HB + 2, 0, t + 1)
            last(used * HB + 1, used)

        @block.scalar
        def _(act):
            act.wait_ge(ld, 64)
            yb = dram["ybuf"].rearrange("(b p) d -> b p d", p=P)

            def silu(b, i):
                act.wait_ge(hr, b)
                act.wait_ge(gd, b + 1)
                act.activation(sg[i][:, :], bank[2][:, :], ACT.Silu).then_inc(sil, 1)

            def outputs(b, i, k, stored=None):
                act.wait_ge(ht, b + 1)
                act.activation(hT[i][:, :, :], bank[4][:, :].rearrange("p (k n) -> p k n", k=FT), ACT.Copy).then_inc(ht_t, 1)
                act.wait_ge(y_st[i], k * 16)
                for j in range(2):
                    act.wait_ge(yd, b * 2 + j + 1)
                    act.activation(y[i][:, j * 512:(j + 1) * 512], bank[5 + j][:, :], ACT.Copy).then_inc(y_t, 1)
                dst = yb[b] if isinstance(b, int) else yb[bass.ds(b, 1)].squeeze(0)
                act.wait_ge(y_t, b * 2 + 2)
                act.dma_start(dst, y[i][:, :]).then_inc(stored or y_st[i], 16)

            def step(b, i, k):
                silu(b, i)
                outputs(b - 1, 1 - i, k if i else k - 1)

            def last(b, k):
                silu(b, 1)
                outputs(b - 1, 0, k, y_end)
                outputs(b, 1, k, y_end)
                act.wait_ge(y_end, 32)

            steps(act, lambda: silu(0, 0), step, last)

        @block.vector
        def _(dve):
            dve.wait_ge(ld, 64)
            ch = Chain(dve, lists)

            def do(f, *a):
                ch.post(f(*a))
                ch.wait()

            places = destf[:, :, :].rearrange("p k c -> p (k c)")
            pairs = 2 * NCH
            do(dve.tensor_scalar, blk[:, :], places, 1.0 / P, 0.5 / P - 0.5, ALU.mult, ALU.add)
            do(dve.tensor_scalar, blk[:, :], blk[:, :], WHOLE, None, ALU.add)
            do(dve.tensor_scalar, blk[:, :], blk[:, :], -WHOLE, None, ALU.add)
            do(dve.scalar_tensor_tensor, off[:, :], blk[:, :], -float(P), places, ALU.mult, ALU.add)
            do(dve.tensor_tensor, in_blk[:, :, :], bc(iota[:, 0:NB], 1, pairs), bc(blk[:, :], 2, NB), ALU.is_equal)
            for k in range(2):
                kk = slice(k * NCH, (k + 1) * NCH)
                do(dve.tensor_tensor, in_blk[:, kk, :], in_blk[:, kk, :], bc(tok[:, :], 2, NB), ALU.mult)
            for q in range(0, pairs, 8):
                dve.tensor_tensor(at_row[:, q:q + 8, :], bc(iota[:, :], 1, 8), bc(off[:, q:q + 8], 2, P), ALU.is_equal).then_inc(marked, 1)
            dve.wait_ge(listed, 1)
            dve.tensor_copy(rows_of[:, :], bank[7][:, 0:NB]).then_inc(rows_ok, 1)

            def product(b, i):
                dve.wait_ge(sil, b + 1)
                dve.wait_ge(ud, b + 1)
                dve.tensor_tensor(sg[i][:, :], sg[i][:, :], bank[3][:, :], ALU.mult).then_inc(hr, 1)

            def turn_x(b, i):
                for j in range(2):
                    dve.wait_ge(xt, b * 2 + j + 1)
                    dve.tensor_tensor(xT[i][:, 4 * j:4 * j + 4, :], bank[j][:, :].rearrange("p (k n) -> p k n", k=4),
                                      bc(gf[:, 4 * j:4 * j + 4], 2, P), ALU.mult).then_inc(xt_t, 1)

            def step(b, i, k):
                product(b, i)
                turn_x(b + 1, 1 - i)

            def first():
                turn_x(0, 0)
                step(0, 0, 0)

            steps(dve, first, step, lambda b, k: product(b, 1))

        @block.tensor
        def _(pe):
            pe.wait_ge(ld, 64)
            for q in range(2 * NCH):
                if q % 8 == 0:
                    pe.wait_ge(marked, q // 8 + 1)
                ins = pe.matmul(bank[7][:, 0:NB], at_row[:, q, :], in_blk[:, q, :], start=(q == 0), stop=(q == 2 * NCH - 1))
            ins.then_inc(listed, 1)

            def turn_x(b, i, k):
                pe.wait_ge(x_ld[i], k * 16 + 16)
                pe.wait_ge(xt_t, b * 2)
                for j in range(2):
                    for n in range(4):
                        kt = 4 * j + n
                        ins = pe.transpose(bank[j][:, n * P:(n + 1) * P], xr[i][:, kt * P:(kt + 1) * P], ident[:, :])
                    ins.then_inc(xt, 1)

            def expert_of(b):
                u = pe.value_load(plan[0:1, bass.ds(b, 1)], min_val=0, max_val=NE - 1)
                for j in range(SLOTS):
                    pe.wait_ge(w_ld[j], (u + (SLOTS - j) % SLOTS) // SLOTS * 48)
                return u % SLOTS

            def gate_up(b, i):
                pe.wait_ge(xt_t, b * 2 + 2)
                at = expert_of(b)
                for w, used, o, done in ((wg, sil, 2, gd), (wu, hr, 3, ud)):
                    pe.wait_ge(used, b)
                    for kt in range(KT):
                        ins = pe.matmul(bank[o][:, :], xT[i][:, kt, :], w[:, bass.ds(at, 1), kt, :].squeeze(1), start=(kt == 0), stop=(kt == KT - 1))
                    ins.then_inc(done, 1)

            def turn_h(b, i):
                pe.wait_ge(hr, b + 1)
                pe.wait_ge(ht_t, b)
                for n in range(FT):
                    ins = pe.transpose(bank[4][:, n * P:(n + 1) * P], sg[i][:, n * P:(n + 1) * P], ident[:, :])
                ins.then_inc(ht, 1)

            def down(b, i, at):
                pe.wait_ge(ht_t, b + 1)
                pe.wait_ge(y_t, b * 2)
                for j in range(2):
                    for n in range(FT):
                        ins = pe.matmul(bank[5 + j][:, :], hT[i][:, n, :], wd[:, bass.ds(at, 1), n, j * 512:(j + 1) * 512].squeeze(1), start=(n == 0), stop=(n == FT - 1))
                    ins.then_inc(yd, 1)

            def slot_of(b):
                return pe.value_load(plan[0:1, bass.ds(b, 1)], min_val=0, max_val=NE - 1) % SLOTS

            def step(b, i, k):
                gate_up(b, i)
                turn_h(b - 1, 1 - i)
                turn_x(b + 1, 1 - i, k + 1 if i else k)
                down(b - 1, 1 - i, slot_of(b - 1))

            def first():
                turn_x(0, 0, 0)
                pe.wait_ge(xt_t, 2)
                for w, loaded, o, done in ((wg, first_ld[0], 2, gd), (wu, first_ld[1], 3, ud)):
                    pe.wait_ge(loaded, 16)
                    for kt in range(KT):
                        ins = pe.matmul(bank[o][:, :], xT[0][:, kt, :], w[:, 0, kt, :], start=(kt == 0), stop=(kt == KT - 1))
                    ins.then_inc(done, 1)
                turn_x(1, 1, 0)
                pe.wait_ge(first_ld[2], 16)

            def last(b, k):
                gate_up(b, 1)
                turn_h(b - 1, 0)
                down(b - 1, 0, slot_of(b - 1))
                turn_h(b, 1)
                down(b, 1, slot_of(b))

            steps(pe, first, step, last)


def combine(nc, env, dram, gates, dest):
    with ExitStack() as ctx:
        def sb(name, shape, dt=F32):
            return ctx.enter_context(nc.sbuf_tensor(name, shape, dt))

        sem = nc.alloc_semaphore
        R = 4
        NTR = NCH // R
        H = [sb(f"hf{i}", [P, D]) for i in range(R)]
        Y = [[sb(f"yf{k}{i}", [P, D]) for i in range(R)] for k in range(2)]
        junk = sb("junk_f", [P, D])
        gb = sb("g_final", [P, D])
        nhalf = sb("nhalf_f", [P, 2])
        ss, ms, rs = (sb(n, [P, R]) for n in ("ss_f", "ms_f", "rs_f"))
        ld = sem("f_consts")
        h_ld, y_ld, st = ([sem(f"{n}{i}") for i in range(R)] for n in ("h_in", "y_in", "out_stored"))
        add1, add2, sq, msd, rsd, fin = (sem(n) for n in ("added_one", "added_two", "f_squares", "f_mean", "f_rstd", "f_ready"))
        block = ctx.enter_context(nc.Block())

        @block.sync
        def _(sp):
            hv = dram["h_scr"].rearrange("(t i p) d -> t i p d", i=R, p=P)
            ov = dram["out"][0].rearrange("(t i p) d -> t i p d", i=R, p=P)
            sp.dma_start(nhalf[:, :], dram["cst"][:, K_HALF:K_HALF + 2]).then_inc(ld, 16)
            sp.dma_start(gb[:, :], dram["norm_final_g"].partition_broadcast(P)).then_inc(ld, 16)
            for i in range(R):
                sp.dma_start(H[i][:, :], hv[0, i]).then_inc(h_ld[i], 16)
            with sp.Fori(0, NTR - 1) as t:
                for i in range(R):
                    sp.wait_ge(fin, t * R + i + 1)
                    sp.dma_start(ov[bass.ds(t, 1)].squeeze(0)[i], H[i][:, :]).then_inc(st[i], 16)
                for i in range(R):
                    sp.wait_ge(st[i], t * 16 + 16)
                    sp.dma_start(H[i][:, :], hv[bass.ds(t + 1, 1)].squeeze(0)[i]).then_inc(h_ld[i], 16)
            for i in range(R):
                sp.wait_ge(fin, (NTR - 1) * R + i + 1)
                sp.dma_start(ov[NTR - 1, i], H[i][:, :]).then_inc(st[i], 16)
            for i in range(R):
                sp.wait_ge(st[i], 16 * NTR)

        @block.gpsimd
        def _(pool):
            pool.wait_ge(ld, 32)

            def rstd(c):
                pool.wait_ge(msd, c + 1)
                pool.tensor_tensor(rs[:, c % R:c % R + 1], ms[:, c % R:c % R + 1], nhalf[:, 0:1], ALU.pow).then_inc(rsd, 1)

            for c in range(NCH):
                if c >= R:
                    rstd(c - R)
                    pool.wait_ge(add2, c - R + 1)
                for k in range(2):
                    pool.indirect_dma_start(Y[k][c % R][:, :], None, dram["ybuf"], bass.IndirectOffsetOnAxis(ap=dest[:, k, c:c + 1], axis=0)).then_inc(y_ld[c % R], 16)
            for c in range(NCH - R, NCH):
                rstd(c)

        @block.scalar
        def _(act):
            with act.Fori(0, NTR) as t:
                for i in range(R):
                    act.wait_ge(add2, t * R + i + 1)
                    act.wait_ge(sq, t * R + i)
                    act.activation(junk[:, :], H[i][:, :], ACT.Square, accum_out=ss[:, i:i + 1]).then_inc(sq, 1)

        @block.vector
        def _(dve):
            dve.wait_ge(ld, 32)
            with dve.Fori(0, NTR) as t:
                def norm(i):
                    dve.wait_ge(sq, t * R + i + 1)
                    dve.tensor_scalar(ms[:, i:i + 1], ss[:, i:i + 1], 1.0 / D, EPS, ALU.mult, ALU.add).then_inc(msd, 1)
                    dve.wait_ge(rsd, t * R + i + 1)
                    dve.scalar_tensor_tensor(H[i][:, :], H[i][:, :], rs[:, i:i + 1], gb[:, :], ALU.mult, ALU.mult).then_inc(fin, 1)

                for i in range(R):
                    dve.wait_ge(h_ld[i], t * 16 + 16)
                    dve.wait_ge(y_ld[i], t * 32 + 32)
                    g = [gates[:, k, bass.ds(t * R + i, 1)] for k in range(2)]
                    dve.scalar_tensor_tensor(H[i][:, :], Y[0][i][:, :], g[0], H[i][:, :], ALU.mult, ALU.add).then_inc(add1, 1)
                    dve.wait_ge(add1, t * R + i + 1)
                    dve.scalar_tensor_tensor(H[i][:, :], Y[1][i][:, :], g[1], H[i][:, :], ALU.mult, ALU.add).then_inc(add2, 1)
                    if i:
                        norm(i - 1)
                norm(R - 1)


def program(nc, dram):
    env = {"dve_a": 96, "s5_turn": 32, "s5_marks": (4, 13), "dve_c": 12, "r_marks": (6, 13)}
    held = mixer_projections(nc, env, dram)
    s5_mixer(nc, env, dram, held)
    nc.extend_free_semaphores([s.num for s in held])
    with ExitStack() as ctx:
        def sb(name, shape, dt=F32):
            return ctx.enter_context(nc.sbuf_tensor(name, shape, dt))

        logits, gates = sb("logits", [P, NCH, NGR + NE]), sb("gates", [P, 2, NCH])
        dest, destf = sb("dest", [P, 2, NCH], U32), sb("destf", [P, 2, NCH])
        plan = sb("plan", [1, PL_END], I32)
        with ExitStack() as kv:
            keys_t = kv.enter_context(nc.sbuf_tensor("keysT", [P, KT, MEM], F32))
            values = kv.enter_context(nc.sbuf_tensor("values", [P, MT, D], F32))
            mem_keys_values(nc, env, dram, keys_t, values)
            cross_and_router(nc, env, dram, keys_t, values, logits)
        route(nc, env, dram, logits, gates, dest, destf, plan)
        experts(nc, env, dram, destf, plan)
        combine(nc, env, dram, gates, dest)


_INS = ["x", "mem", "norm_mix_g", "w_in", "ret_gn_g", "ssd_conv_w", "ssd_conv_b", "ssd_dt_bias", "ssd_A_log", "ssd_D",
        "ssd_norm_g", "s5_A_re", "s5_A_im", "s5_B_re", "s5_B_im", "s5_C_re", "s5_C_im", "s5_log_step", "s5_D", "s5_w_glu",
        "s5_b_glu", "w_out", "norm_cross_g", "mem_norm_g", "w_cq", "w_ck", "w_cv", "w_co", "norm_ffn_g", "w_route_group",
        "b_route_group", "w_route_expert", "b_route_expert", "w_gate", "w_up", "w_down", "norm_final_g"]
_SCRATCH = {"cat": (T, D), "u_scr": (T, S5W), "h_scr": (T, D), "xn_scr": (T, D), "ybuf": (ROWS, D)}


def kernel(**inputs):
    import concourse.bacc as _bacc
    from concourse.bass_utils import run_bass_kernel_spmd as _run

    nc = _bacc.Bacc("TRN2", target_bir_lowering=False, num_devices=1)
    table, rope = constants()
    sent = {name: inputs[name] for name in _INS} | {"cst": table, "rope": rope}
    arrays, dram = {}, {}
    for name, a in sent.items():
        a = np.ascontiguousarray(a)
        arrays[f"in_{name}"] = a
        dram[name] = nc.dram_tensor(f"in_{name}", a.shape, mybir.dt.from_np(a.dtype), kind="ExternalInput").ap()
    for name, shape in _SCRATCH.items():
        dram[name] = nc.dram_tensor(f"scratch_{name}", shape, F32, kind="Internal").ap()
    dram["out"] = nc.dram_tensor("out_0", (1, T, D), F32, kind="ExternalOutput").ap()
    program(nc, dram)
    r = _run(nc, [arrays], core_ids=[0])
    return r.results[0]["out_0"]
```

```python
from contextlib import ExitStack

import concourse.bass as bass
from concourse import mybir
import numpy as np

F32 = mybir.dt.float32
F16 = mybir.dt.float16
I32 = mybir.dt.int32
U32 = mybir.dt.uint32
ALU = mybir.AluOpType
ACT = mybir.ActivationFunctionType
AX = mybir.AxisListType

P = 128
D = 1024
KT = D // P
T = 2048
NCH = T // P
GC = 4
NG = NCH // GC
GT = GC * P
EPS = 1e-6
RH, RD = 4, 64
RW = RH * RD
SH, SP_, SN = 8, 64, 128
SW = SH * SP_
XBC = SW + 4 * SN
S5G, S5C, S5P = 16, 16, 64
S5W = S5G * S5C
COLS = 4 * RW + SW + XBC + SH + S5W
C_VG, C_Z, C_XBC, C_DT = 2 * RW, 4 * RW, 4 * RW + SW, 4 * RW + SW + XBC
MEM = 256
NE, NGR, EPG, DE = 32, 4, 8, 512
NB = 2 * T // P + NE
USED_MIN = 2 * T // P

W_SCALE, N_SCALE = 2.0 ** 9, 2.0 ** 5
UNSCALE = 1.0 / (W_SCALE * N_SCALE)

K_ID, K_LE, K_GT, K_ONE, K_LT, K_IOTA = 0, 128, 256, 384, 512, 640
K_TOK = K_IOTA + P
K_GAM = K_TOK + NCH
K_HALF = K_GAM + 2 * RD
K_END = K_HALF + 64


def constants():
    c = np.zeros((P, K_END), np.float32)
    i = np.arange(P)
    c[:, K_ID:K_ID + P] = np.eye(P)
    c[:, K_LE:K_LE + P] = i[:, None] <= i[None, :]
    c[:, K_GT:K_GT + P] = i[:, None] > i[None, :]
    c[:, K_ONE:K_ONE + P] = 1
    c[:, K_LT:K_LT + P] = i[:, None] < i[None, :]
    c[:, K_IOTA:K_IOTA + P] = i
    c[:, K_TOK:K_TOK + NCH] = np.arange(NCH)[None, :] * P + i[:, None]
    gamma = 1.0 - 2.0 ** (-5.0 - np.arange(RH))
    for j in range(RH // 2):
        for half in range(2):
            c[half * 64:half * 64 + 64, K_GAM + j * RD:K_GAM + (j + 1) * RD] = gamma[2 * j + half] ** P
    c[:, K_HALF:K_HALF + 64] = -0.5
    half = RD // 2
    inv = (np.float32(10000.0) ** (-np.arange(0, RD, 2, dtype=np.float32) / np.float32(RD))).astype(np.float32)
    ang = (np.arange(T, dtype=np.float32)[:, None] * inv[None, :]).astype(np.float32).astype(np.float64)
    pos = (np.arange(T) % P + 1.0)[:, None]
    fold = np.concatenate([gamma[None, :] ** pos, gamma[None, :] ** -pos * RD ** -0.5], 1)
    rope = np.stack([fold[:, :, None] * np.cos(ang)[:, None, :], fold[:, :, None] * np.sin(ang)[:, None, :]], 1)
    rope *= UNSCALE
    return c, rope.reshape(T, 2 * 2 * RH * half).astype(np.float32)


def bc(ap, axis, n):
    a = ap.unsqueeze(axis)
    s = list(a.shape)
    s[axis] = n
    return a.to_broadcast(s)


def halves(t):
    a, b = list(t[:, :, :].shape)[1:]
    v = t[:, :, :].bitcast(F16).rearrange("p a b -> p (a b)").rearrange("p (h a b) -> p h a b", h=2, a=a)
    return v[:, 0], v[:, 1]


def products(pe, o, a, b, start=True, stop=True):
    n = len(a[0])
    for k in range(n):
        for j, (x, y) in enumerate(((0, 0), (0, 1), (1, 0))):
            ins = pe.matmul(o, a[x][k], b[y][k], start=start and k == 0 and j == 0, stop=stop and k == n - 1 and j == 2)
    return ins


class Chain:

    def __init__(self, eng, sem, turn=0, per=0):
        self.eng, self.sem, self.turn, self.per, self.n = eng, sem, turn, per, 0

    def post(self, ins):
        ins.then_inc(self.sem, 1)
        self.n += 1

    def wait(self, n=None):
        k = self.n if n is None else n
        self.eng.wait_ge(self.sem, self.turn * self.per + k if self.per else k)


def mixer_projections(nc, env, dram):
    x, w_in, cat, u_scr = dram["x"], dram["w_in"][0], dram["cat"], dram["u_scr"]
    BIG = 2 * KT + 3 * GC
    SML = 12
    DVE_TURN = env["dve_a"]
    with ExitStack() as ctx:
        def sb(name, shape, dt=F32):
            return ctx.enter_context(nc.sbuf_tensor(name, shape, dt))

        held = []

        def sem(name):
            held.append(nc.alloc_semaphore(name))
            return held[-1]

        wi = sb("wi", [P, 2, KT, COLS], F16)
        cst = sb("cst_a", [P, K_IOTA])
        gam = sb("gam", [P, 2 * RD])
        nhalf = sb("nhalf", [P, 64])
        gmix = sb("gmix", [P, KT])
        gn_bc = sb("gn_bc", [P, RW])
        ng_bc = sb("ng_bc", [P, SW])
        dtb_bc = sb("dtb_bc", [P, SH])
        a_bc = sb("a_bc", [P, SH])
        d_bc = sb("d_bc", [P, SH])
        cw = sb("cw", [P, 4, KT])
        cb = sb("cb", [P, KT])
        xg = sb("xg", [P, GC, D])
        ss = sb("ss_a", [P, GC])
        ms = sb("ms_a", [P, GC])
        rstd = sb("rstd_a", [P, GC])
        hnT = sb("hnT", [P, KT, GT])
        hn_s = halves(hnT)
        gmix_s = sb("gmix_s", [P, KT])
        PT = hnT[:, 0, :].rearrange("p (a b) -> p a b", a=RH)
        kT = hnT[:, 1, 0:2 * P].rearrange("p (a b) -> p a b", a=2)
        xdt = hnT[:, 2, :].rearrange("p (a b) -> p a b", a=SH)
        xtok = hnT[:, 3, :].rearrange("p (a b) -> p a b", a=SH)
        xbcT = sb("xbcT", [P, 2, GT + 3])
        hist = sb("hist", [P, KT, 3])
        xc = sb("xc", [P, KT, GT])
        vb = sb("vb", [P, GC, RW])
        gs = sb("gs", [P, GC, RW])
        dtu = sb("dtu", [P, GC, SH + S5W])
        qr = sb("qr", [P, GC, 2 * RW])
        rope = sb("rope_t", [P, GC, 2 * RW])
        Y = sb("Y", [P, GC, RW + SW])
        HC, ROOMS = COLS // 2, 4
        stage = [t[:, :, :].rearrange("p a b -> p (a b)")[:, h * HC:(h + 1) * HC] for t in (Y, xc) for h in range(2)]
        pieces = [(kt, slice(h * HC, (h + 1) * HC), (2 * kt + h) % ROOMS, (2 * kt + h) // ROOMS) for kt in range(KT) for h in range(2)]
        dts = sb("dts", [P, 8, GC, SH])
        qz = sb("qz", [P, 2, 2, P])
        btok = sb("btok", [P, 2, SN])
        dec = sb("dec", [P, 3, SH])
        E = sb("E", [P, SH, P])
        AB = E[:, :, :].rearrange("p (a h) l -> p a (h l)", a=2)
        segin = sb("segin", [P, SH, P])
        sg2 = segin[:, :, :].rearrange("p (a h) l -> p a (h l)", a=2)
        yo, xdec = sg2[:, 0, :], sg2[:, 1, :]
        junk = segin[:, :, :].rearrange("p h l -> p (h l)")
        cbm = sb("cbm", [P, 2, P])
        S_r = sb("S_r", [P, 2, RD])
        S_m = sb("S_m", [P, SH, SP_])
        sso = sb("sso", [P, 5 * GC])
        eps = sb("eps", [P, 5])
        mso = sb("mso", [P, 5 * GC])
        rso = sb("rso", [P, 5 * GC])
        bank = [ctx.enter_context(nc.psum_tensor(f"bankA{i}", [P, 512], F32)) for i in range(8)]
        ident, le, gt, ones = (cst[:, k:k + P] for k in (K_ID, K_LE, K_GT, K_ONE))
        dt_, dtA = dts[:, 6, :, :], dts[:, 7, :, :]

        w_ld = [sem(f"w_in_loaded{i}") for i in range(ROOMS)]
        w_hi, w_lo, hn_lo = sem("w_in_nearest"), sem("w_in_rest"), sem("hn_rest")
        c_ld, x_ld, r_ld = sem("consts_a_loaded"), sem("x_loaded"), sem("rope_loaded")
        a_set, s_set = sem("ssd_A_set"), sem("states_zeroed")
        sq_done, ms_done, rs_done, xs_done = sem("squares_a"), sem("mean_a"), sem("rstd_a_ready"), sem("xs_ready")
        big, taken, qk_done, qk_free = sem("big_done"), sem("big_taken"), sem("qk_done"), sem("rope_done")
        conv_done, silu_done, hist_done = sem("conv_done"), sem("conv_silu"), sem("history_kept")
        small, s_act, s_dve = sem("small_done"), sem("small_taken_act"), sem("small_taken_dve")
        dt_ready, ax_ready, e_ready, w_ready, ln_ready = (sem("dt_ready"), sem("dt_abs"), sem("dt_exp"),
                                                          sem("dt_exp1"), sem("dt_ln"))
        seg_ready = sem("segin_ready")
        ch_done, ro_done, out_done = sem("chunk_done"), sem("rstd_out"), sem("out_ready")
        u_ready, u_st, cat_st = sem("u_ready"), sem("u_stored"), sem("cat_stored")
        dve_s, pool_s = sem("dve_steps_a"), sem("pool_steps_a")

        BY = ["act", "act", "act", "act", "act", "dve", "dve", "dve", "dve", "dve", "dve", "dve"]
        N_ACT, N_DVE = BY.count("act"), BY.count("dve")
        SB0 = 5

        ctx.enter_context(nc.allow_non_contiguous_dma(reason="gains by rows, loaded once"))
        block = ctx.enter_context(nc.Block())

        @block.sync
        def _(sp):
            xv = x[0].rearrange("(g c p) d -> g p c d", c=GC, p=P)
            rv = dram["rope"].rearrange("(g c p) d -> g p c d", c=GC, p=P)
            catv = cat.rearrange("(g c p) d -> g p c d", c=GC, p=P)
            uv = u_scr.rearrange("(g c p) d -> g p c d", c=GC, p=P)
            sp.dma_start(xg[:, :, :], xv[0]).then_inc(x_ld, 16)
            sp.dma_start(cst[:, :], dram["cst"][:, 0:K_IOTA]).then_inc(c_ld, 16)
            sp.dma_start(gam[:, :], dram["cst"][:, K_GAM:K_GAM + 2 * RD]).then_inc(c_ld, 16)
            sp.dma_start(nhalf[:, :], dram["cst"][:, K_HALF:K_HALF + 64]).then_inc(c_ld, 16)
            sp.dma_start(gmix[:, :], dram["norm_mix_g"][0].rearrange("(k p) -> p k", p=P)).then_inc(c_ld, 16)
            sp.dma_start(gn_bc[:, :], dram["ret_gn_g"][0].partition_broadcast(P)).then_inc(c_ld, 16)
            sp.dma_start(ng_bc[:, :], dram["ssd_norm_g"][0].partition_broadcast(P)).then_inc(c_ld, 16)
            sp.dma_start(dtb_bc[:, :], dram["ssd_dt_bias"][0].partition_broadcast(P)).then_inc(c_ld, 16)
            sp.dma_start(a_bc[:, :], dram["ssd_A_log"][0].partition_broadcast(P)).then_inc(c_ld, 16)
            sp.dma_start(d_bc[:, :], dram["ssd_D"][0].partition_broadcast(P)).then_inc(c_ld, 16)
            for j in range(4):
                sp.dma_start(cw[:, j, :], dram["ssd_conv_w"][0, j].rearrange("(k p) -> p k", p=P)).then_inc(c_ld, 16)
            sp.dma_start(cb[:, :], dram["ssd_conv_b"][0].rearrange("(k p) -> p k", p=P)).then_inc(c_ld, 16)
            for n, (kt, cols, room, before) in enumerate(pieces):
                if before:
                    sp.wait_ge(w_hi, n - ROOMS + 1)
                    sp.wait_ge(w_lo, n - ROOMS + 1)
                sp.dma_start(stage[room], w_in[kt * P:(kt + 1) * P, cols]).then_inc(w_ld[room], 16)
            sp.dma_start(rope[:, :, :], rv[0]).then_inc(r_ld, 16)

            def stores(g, at):
                sp.wait_ge(u_ready, g * GC + GC)
                sp.dma_start(uv[at], dtu[:, :, SH:]).then_inc(u_st, 16)
                sp.wait_ge(out_done, g * GC + GC)
                sp.dma_start(catv[at][:, :, 0:RW + SW], Y[:, :, :]).then_inc(cat_st, 16)

            with sp.Fori(0, NG - 1) as g:
                sp.wait_ge(big, g * BIG + KT)
                sp.dma_start(xg[:, :, :], xv[bass.ds(g + 1, 1)].squeeze(0)).then_inc(x_ld, 16)
                sp.wait_ge(qk_free, g * GC + GC)
                sp.dma_start(rope[:, :, :], rv[bass.ds(g + 1, 1)].squeeze(0)).then_inc(r_ld, 16)
                sp.wait_ge(u_ready, g * GC + GC)
                sp.dma_start(uv[bass.ds(g, 1)].squeeze(0), dtu[:, :, SH:]).then_inc(u_st, 16)
                sp.wait_ge(out_done, g * GC + GC)
                sp.dma_start(catv[bass.ds(g, 1)].squeeze(0)[:, :, 0:RW + SW], Y[:, :, :]).then_inc(cat_st, 16)
            stores(NG - 1, NG - 1)
            sp.wait_ge(u_st, 16 * NG)
            sp.wait_ge(cat_st, 16 * NG)

        @block.gpsimd
        def _(pool):
            pool.memset(S_r[:, :, :], 0.0).then_inc(s_set, 1)
            pool.memset(S_m[:, :, :], 0.0).then_inc(s_set, 1)
            pool.memset(hist[:, :, :], 0.0).then_inc(s_set, 1)
            pool.memset(qz[:, :, :, :], 0.0).then_inc(s_set, 1)
            pool.memset(eps[:, :], EPS).then_inc(s_set, 1)
            pool.wait_ge(s_set, 5)
            pool.wait_ge(c_ld, 16 * 14)

            def rstd_of(g):
                pool.wait_ge(ms_done, g + 1)
                pool.tensor_tensor(rstd[:, :], ms[:, :], nhalf[:, 0:GC], ALU.pow).then_inc(rs_done, 1)

            rstd_of(0)
            with pool.Fori(0, NG) as g:
                with pool.If(g < NG - 1):
                    rstd_of(g + 1)
                for c in range(GC):
                    cc = slice(5 * c, 5 * c + 5)
                    steps = Chain(pool, pool_s, g * GC + c, 5)
                    pool.wait_ge(ch_done, g * GC + c + 1)
                    steps.post(pool.tensor_tensor(mso[:, cc], sso[:, cc], eps[:, :], ALU.add))
                    steps.wait()
                    pool.tensor_tensor(rso[:, cc], mso[:, cc], nhalf[:, 0:5], ALU.pow).then_inc(ro_done, 1)
                    pool.wait_ge(ro_done, g * GC + c + 1)
                    yr, ym = Y[:, c, 0:RW], Y[:, c, RW:]
                    yh = yr.rearrange("p (h e) -> p h e", h=RH)
                    steps.post(pool.tensor_tensor(yh, yh, bc(rso[:, 5 * c + 1:5 * c + 5], 2, RD), ALU.mult))
                    steps.post(pool.tensor_scalar(ym, ym, rso[:, 5 * c:5 * c + 1], None, ALU.mult))
                    steps.wait()
                    steps.post(pool.tensor_tensor(yr, yr, gn_bc[:, :], ALU.mult))
                    steps.post(pool.tensor_tensor(ym, ym, ng_bc[:, :], ALU.mult))
                    steps.wait()
                    pool.tensor_tensor(yr, yr, gs[:, c, :], ALU.mult).then_inc(out_done, 1)

        @block.scalar
        def _(act):
            act.wait_ge(c_ld, 16 * 14)
            act.wait_ge(s_set, 5)
            act.activation(a_bc[:, :], a_bc[:, :], ACT.Exp).then_inc(a_set, 1)

            def squares(g):
                act.wait_ge(x_ld, g * 16 + 16)
                act.wait_ge(ms_done, g)
                for c in range(GC):
                    act.wait_ge(sq_done, g * GC + c)
                    act.activation(junk, xg[:, c, :], ACT.Square, accum_out=ss[:, c:c + 1]).then_inc(sq_done, 1)

            squares(0)
            for kt, cols, room, before in pieces:
                act.wait_ge(w_ld[room], before * 16 + 16)
                act.activation(wi[:, 0, kt, cols], stage[room], ACT.Copy, scale=W_SCALE).then_inc(w_hi, 1)
            act.wait_ge(w_lo, len(pieces))
            act.wait_ge(a_set, 3)
            with act.Fori(0, NG) as g:
                act.wait_ge(ch_done, g * GC)
                n = 0
                for kt in range(KT):
                    act.wait_ge(big, g * BIG + n + 1)
                    act.activation(hn_s[0][:, kt, :], bank[n % 4][:, :], ACT.Copy, scale=gmix_s[:, kt:kt + 1]).then_inc(taken, 1)
                    n += 1
                for ct in range(KT):
                    if ct == 0:
                        act.wait_ge(hist_done, g * KT)
                    if ct >= 2:
                        act.wait_ge(hist_done, g * KT + ct - 1)
                    act.wait_ge(big, g * BIG + n + 1)
                    act.activation(xbcT[:, ct % 2, 3:], bank[n % 4][:, :], ACT.Copy, scale=UNSCALE).then_inc(taken, 1)
                    n += 1
                for ct in range(KT):
                    act.wait_ge(conv_done, g * KT + ct + 1)
                    act.activation(xc[:, ct, :], xc[:, ct, :], ACT.Silu).then_inc(silu_done, 1)
                with act.If(g < NG - 1):
                    squares(g + 1)
                for c in range(GC):
                    if c == 0:
                        act.wait_ge(out_done, g * GC)
                    act.wait_ge(big, g * BIG + n + 1)
                    act.activation(gs[:, c, :], bank[n % 4][:, RW:], ACT.Silu, scale=UNSCALE)
                    act.activation(vb[:, c, :], bank[n % 4][:, 0:RW], ACT.Copy, scale=UNSCALE).then_inc(taken, 1)
                    n += 1
                    if c == 0:
                        act.wait_ge(cat_st, g * 16)
                    act.wait_ge(big, g * BIG + n + 1)
                    act.activation(Y[:, c, RW:], bank[n % 4][:, :], ACT.Silu, scale=UNSCALE).then_inc(taken, 1)
                    n += 1
                    if c == 0:
                        act.wait_ge(u_st, g * 16)
                    act.wait_ge(big, g * BIG + n + 1)
                    act.activation(dtu[:, c, SH:], bank[n % 4][:, SH:SH + S5W], ACT.Copy, scale=UNSCALE).then_inc(u_ready, 1)
                    act.activation(dtu[:, c, 0:SH], bank[n % 4][:, 0:SH], ACT.Copy, scale=UNSCALE).then_inc(taken, 1)
                    n += 1
                act.wait_ge(ax_ready, g + 1)
                act.activation(dts[:, 2, :, :], dts[:, 1, :, :], ACT.Exp, scale=-1.0).then_inc(e_ready, 1)
                act.wait_ge(w_ready, g + 1)
                act.activation(dts[:, 4, :, :], dts[:, 3, :, :], ACT.Ln).then_inc(ln_ready, 1)
                for c in range(GC):
                    s0 = g * GC * SML + c * SML
                    act.wait_ge(small, s0 + 1)
                    qk = bank[SB0][:, :].rearrange("p (a b) -> p a b", a=4)
                    act.activation(qz[0:RD, :, 0, :], qk[0:RD, 0:2, :], ACT.Copy)
                    act.activation(qz[RD:, :, 1, :], qk[RD:, 0:2, :], ACT.Copy)
                    act.activation(kT, qk[:, 2:4, :], ACT.Copy).then_inc(s_act, 1)
                    if c == 0:
                        act.wait_ge(ch_done, g * GC)
                    else:
                        act.wait_ge(ch_done, g * GC + c)
                    act.wait_ge(small, s0 + 2)
                    act.activation(xtok[:, :, :], bank[SB0 + 1][:, :].rearrange("p (a b) -> p a b", a=SH), ACT.Copy).then_inc(s_act, 1)
                    act.wait_ge(small, s0 + 3)
                    act.activation(dec[:, :, :], bank[SB0 + 2][:, 2 * SN:2 * SN + 3 * SH].rearrange("p (a b) -> p a b", a=3), ACT.Exp)
                    act.activation(btok[:, :, :], bank[SB0 + 2][:, 0:2 * SN].rearrange("p (a b) -> p a b", a=2), ACT.Copy).then_inc(s_act, 1)
                    for h in range(2):
                        act.wait_ge(small, s0 + 4 + h)
                        act.activation(AB[:, h, :], bank[SB0 + h][:, :], ACT.Exp).then_inc(s_act, 1)

        @block.vector
        def _(dve):
            def norm(g):
                dve.wait_ge(sq_done, g * GC + GC)
                dve.tensor_scalar(ms[:, :], ss[:, :], 1.0 / D, EPS, ALU.mult, ALU.add).then_inc(ms_done, 1)
                dve.wait_ge(rs_done, g + 1)
                for c in range(GC):
                    dve.tensor_scalar(xg[:, c, :], xg[:, c, :], rstd[:, c:c + 1], None, ALU.mult).then_inc(xs_done, 1)

            norm(0)
            for n, (kt, cols, room, before) in enumerate(pieces):
                dve.wait_ge(w_hi, n + 1)
                dve.scalar_tensor_tensor(wi[:, 1, kt, cols], stage[room], W_SCALE, wi[:, 0, kt, cols], ALU.mult, ALU.subtract).then_inc(w_lo, 1)
            dve.wait_ge(a_set, 1)
            dve.wait_ge(c_ld, 16 * 14)
            dve.tensor_scalar(a_bc[:, :], a_bc[:, :], -1.0, None, ALU.mult).then_inc(a_set, 1)
            dve.tensor_scalar(gmix_s[:, :], gmix[:, :], N_SCALE, None, ALU.mult).then_inc(a_set, 1)
            dve.wait_ge(a_set, 3)
            dve.wait_ge(w_lo, len(pieces))
            dve.wait_ge(s_set, 5)
            with dve.Fori(0, NG) as g:
                ch = Chain(dve, dve_s, g, DVE_TURN)
                for kt in range(KT):
                    dve.wait_ge(taken, g * BIG + kt + 1)
                    dve.scalar_tensor_tensor(hn_s[1][:, kt, :], bank[kt % 4][:, :], gmix_s[:, kt:kt + 1], hn_s[0][:, kt, :], ALU.mult, ALU.subtract).then_inc(hn_lo, 1)
                for ct in range(KT):
                    b = xbcT[:, ct % 2, :]
                    ch.post(dve.tensor_copy(b[:, 0:3], hist[:, ct, :]))
                    ch.wait()
                    dve.wait_ge(taken, g * BIG + KT + ct + 1)
                    ch.post(dve.tensor_scalar(xc[:, ct, :], b[:, 0:GT], cw[:, 0, ct:ct + 1], cb[:, ct:ct + 1], ALU.mult, ALU.add))
                    for j in range(1, 4):
                        ch.wait()
                        ins = dve.scalar_tensor_tensor(xc[:, ct, :], b[:, j:GT + j], cw[:, j, ct:ct + 1], xc[:, ct, :], ALU.mult, ALU.add)
                        if j < 3:
                            ch.post(ins)
                        else:
                            ins.then_inc(conv_done, 1)
                    dve.tensor_copy(hist[:, ct, :], b[:, GT:]).then_inc(hist_done, 1)
                dve.wait_ge(r_ld, g * 16 + 16)
                for c in range(GC):
                    dve.wait_ge(qk_done, g * GC + c + 1)
                    t = bank[4][:, :].rearrange("p (h a r) -> p h a r", a=2, r=RD // 2)
                    for j in range(2):
                        tab = rope[:, c, j * RW:(j + 1) * RW].rearrange("p (h r) -> p h r", r=RD // 2)
                        o = AB[:, j, :].rearrange("p (h a r) -> p h a r", a=2, r=RD // 2)
                        ch.post(dve.tensor_tensor(o, t, bc(tab, 2, 2), ALU.mult))
                    ch.wait()
                    A = AB[:, 0, :].rearrange("p (h a r) -> p h a r", a=2, r=RD // 2)
                    B = AB[:, 1, :].rearrange("p (h a r) -> p h a r", a=2, r=RD // 2)
                    o = qr[:, c, :].rearrange("p (h a r) -> p h a r", a=2, r=RD // 2)
                    ch.post(dve.tensor_tensor(o[:, :, 0, :], A[:, :, 0, :], B[:, :, 1, :], ALU.subtract))
                    dve.tensor_tensor(o[:, :, 1, :], A[:, :, 1, :], B[:, :, 0, :], ALU.add).then_inc(qk_free, 1)
                    if c == 1:
                        with dve.If(g < NG - 1):
                            norm(g + 1)
                dve.wait_ge(taken, g * BIG + BIG)
                ch.post(dve.tensor_tensor(dts[:, 0, :, :], dtu[:, :, 0:SH], bc(dtb_bc[:, :], 1, GC), ALU.add))
                ch.wait()
                ch.post(dve.tensor_scalar(dts[:, 5, :, :], dts[:, 0, :, :], -1.0, None, ALU.mult))
                ch.wait()
                dve.tensor_tensor(dts[:, 1, :, :], dts[:, 0, :, :], dts[:, 5, :, :], ALU.max).then_inc(ax_ready, 1)
                dve.wait_ge(e_ready, g + 1)
                dve.tensor_scalar(dts[:, 3, :, :], dts[:, 2, :, :], 1.0, None, ALU.add).then_inc(w_ready, 1)
                dve.wait_ge(w_ready, g + 1)
                ch.post(dve.tensor_scalar(dts[:, 5, :, :], dts[:, 3, :, :], -1.0, 1e-30, ALU.add, ALU.add))
                ch.wait()
                ch.post(dve.reciprocal(dts[:, 5, :, :], dts[:, 5, :, :]))
                ch.wait()
                ch.post(dve.tensor_tensor(dts[:, 5, :, :], dts[:, 5, :, :], dts[:, 2, :, :], ALU.mult))
                ch.wait()
                dve.wait_ge(ln_ready, g + 1)
                ch.post(dve.scalar_tensor_tensor(dts[:, 5, :, :], dts[:, 4, :, :], 1e-30, dts[:, 5, :, :], ALU.add, ALU.mult))
                ch.wait()
                ch.post(dve.scalar_tensor_tensor(dt_, dts[:, 0, :, :], 0.0, dts[:, 5, :, :], ALU.max, ALU.add))
                ch.wait()
                dve.tensor_tensor(dtA, dt_, bc(a_bc[:, :], 1, GC), ALU.mult).then_inc(dt_ready, 1)
                dve.wait_ge(dt_ready, g + 1)
                for c in range(GC):
                    s0 = g * GC * SML + c * SML
                    a0 = g * GC * N_ACT + c * N_ACT
                    if c:
                        dve.wait_ge(small, s0)
                        dve.wait_ge(ch_done, g * GC + c)
                    dve.tensor_tensor(segin[:, :, :], bc(le, 1, SH), bc(dtA[:, c, :], 2, P), ALU.mult).then_inc(seg_ready, 1)
                    dve.wait_ge(s_act, a0 + 2)
                    ch.post(dve.tensor_tensor(xdt[:, :, :], xtok[:, :, :], bc(dt_[:, c, :], 2, SP_), ALU.mult))
                    ch.wait()
                    dve.wait_ge(s_act, a0 + 5)
                    ch.post(dve.tensor_tensor(xdec.rearrange("p (h e) -> p h e", h=SH), xdt[:, :, :], bc(dec[:, 1, :], 2, SP_), ALU.mult))
                    ch.wait()
                    dve.wait_ge(small, s0 + 6)
                    dve.tensor_tensor(cbm[:, :, :], bank[SB0 + 2][:, 0:2 * P].rearrange("p (a b) -> p a b", a=2), bc(le, 1, 2), ALU.mult).then_inc(s_dve, 1)
                    dve.wait_ge(s_dve, (g * GC + c) * N_DVE + 1)
                    Ev = E[:, :, :].rearrange("p (a h) l -> p a h l", a=2)
                    ch.post(dve.tensor_tensor(Ev, Ev, bc(cbm[:, :, :], 2, SH // 2), ALU.mult))
                    ch.wait()
                    dve.wait_ge(small, s0 + 7)
                    dve.tensor_tensor(PT[:, :, :], bank[SB0][:, :].rearrange("p (a b) -> p a b", a=RH), bc(le, 1, RH), ALU.mult).then_inc(s_dve, 1)
                    dve.wait_ge(s_dve, (g * GC + c) * N_DVE + 2)
                    dve.wait_ge(small, s0 + 8)
                    dve.tensor_tensor(yo.rearrange("p (h e) -> p h e", h=SH), bank[SB0 + 1][:, :].rearrange("p (h e) -> p h e", h=SH),
                                      bc(dec[:, 0, :], 2, SP_), ALU.mult).then_inc(s_dve, 1)
                    dve.wait_ge(small, s0 + 9)
                    ch.post(dve.tensor_tensor(S_m[:, :, :], S_m[:, :, :], bc(dec[:, 2, :], 2, SP_), ALU.mult))
                    ch.wait()
                    dve.tensor_tensor(S_m[:, :, :], S_m[:, :, :], bank[SB0 + 2][:, :].rearrange("p (h e) -> p h e", h=SH), ALU.add).then_inc(s_dve, 1)
                    dve.wait_ge(small, s0 + 10)
                    dve.tensor_copy(Y[:, c, 0:RW], bank[SB0][:, 0:RW]).then_inc(s_dve, 1)
                    dve.wait_ge(small, s0 + 11)
                    ch.post(dve.tensor_tensor(S_r[:, :, :], S_r[:, :, :], bank[SB0 + 1][:, 0:2 * RD].rearrange("p (a b) -> p a b", a=2), ALU.add))
                    ch.wait()
                    dve.tensor_tensor(S_r[:, :, :], S_r[:, :, :], gam[:, :].rearrange("p (a b) -> p a b", a=2), ALU.mult).then_inc(s_dve, 1)
                    dve.wait_ge(small, s0 + 12)
                    ch.post(dve.tensor_tensor(yo, yo, bank[SB0 + 2][:, :], ALU.add))
                    ch.post(dve.tensor_tensor(xdt[:, :, :], xtok[:, :, :], bc(d_bc[:, :], 2, SP_), ALU.mult))
                    ch.wait()
                    ch.post(dve.tensor_tensor(yo, yo, xdt[:, :, :].rearrange("p h e -> p (h e)"), ALU.add))
                    ch.wait()
                    dve.tensor_tensor(Y[:, c, RW:], yo, Y[:, c, RW:], ALU.mult).then_inc(s_dve, 1)
                    dve.wait_ge(s_dve, (g * GC + c) * N_DVE + N_DVE)
                    if c == 0:
                        dve.wait_ge(ro_done, g * GC)
                    ch.post(dve.scalar_tensor_tensor(xdt[:, :, :].rearrange("p h e -> p (h e)"), Y[:, c, RW:], 1.0 / SW, Y[:, c, RW:], ALU.mult, ALU.mult, accum_out=sso[:, 5 * c:5 * c + 1]))
                    ch.post(dve.scalar_tensor_tensor(yo[:, 0:RW], Y[:, c, 0:RW], 1.0 / RD, Y[:, c, 0:RW], ALU.mult, ALU.mult))
                    ch.wait()
                    dve.tensor_reduce(sso[:, 5 * c + 1:5 * c + 5], yo[:, 0:RW].rearrange("p (h e) -> p h e", h=RH), AX.X, ALU.add).then_inc(ch_done, 1)
                assert ch.n == DVE_TURN, ch.n

        @block.tensor
        def _(pe):
            pe.wait_ge(c_ld, 16 * 14)
            with pe.Fori(0, NG) as g:
                n = 0

                def slot(n):
                    pe.wait_ge(taken, g * BIG + max(0, n - 3))
                    if 4 <= n < KT + 4:
                        pe.wait_ge(hn_lo, g * KT + n - 3)
                    return bank[n % 4]

                for kt in range(KT):
                    o = slot(n)
                    if kt == 0:
                        pe.wait_ge(xs_done, g * GC + GC)
                    for c in range(GC):
                        ins = pe.transpose(o[:, c * P:(c + 1) * P], xg[:, c, kt * P:(kt + 1) * P], ident)
                    ins.then_inc(big, 1)
                    n += 1
                pe.wait_ge(w_lo, len(pieces))
                pe.wait_ge(taken, g * BIG + KT)
                pe.wait_ge(hn_lo, g * KT + KT)
                for ct in range(KT):
                    o = slot(n)
                    w = [[wi[:, h, kt, C_XBC + ct * P:C_XBC + (ct + 1) * P] for kt in range(KT)] for h in range(2)]
                    hn = [[hn_s[h][:, kt, :] for kt in range(KT)] for h in range(2)]
                    products(pe, o[:, :], w, hn).then_inc(big, 1)
                    n += 1
                for c in range(GC):
                    def project(o, a, w):
                        return products(pe, o[:, 0:w], [[hn_s[h][:, kt, c * P:(c + 1) * P] for kt in range(KT)] for h in range(2)],
                                        [[wi[:, h, kt, a:a + w] for kt in range(KT)] for h in range(2)])

                    pe.wait_ge(qk_free, g * GC + c)
                    project(bank[4], 0, 2 * RW).then_inc(qk_done, 1)
                    project(slot(n), C_VG, 2 * RW).then_inc(big, 1)
                    project(slot(n + 1), C_Z, SW).then_inc(big, 1)
                    project(slot(n + 2), C_DT, SH + S5W).then_inc(big, 1)
                    n += 3
                assert n == BIG
                pe.wait_ge(taken, g * BIG + BIG)
                pe.wait_ge(silu_done, g * KT + KT)
                pe.wait_ge(qk_free, g * GC + GC)
                pe.wait_ge(dt_ready, g + 1)
                for c in range(GC):
                    tok = slice(c * P, (c + 1) * P)

                    def room(j):
                        t = j - 3
                        if t < 0:
                            pe.wait_ge(s_dve, (g * GC + c) * N_DVE)
                        elif BY[t] == "act":
                            pe.wait_ge(s_act, (g * GC + c) * N_ACT + BY[:t + 1].count("act"))
                        else:
                            pe.wait_ge(s_dve, (g * GC + c) * N_DVE + BY[:t + 1].count("dve"))
                        return bank[SB0 + j % 3]

                    o = room(0)
                    for k in range(4):
                        ins = pe.transpose(o[:, k * P:(k + 1) * P], qr[:, c, k * P:(k + 1) * P], ident)
                    ins.then_inc(small, 1)
                    o = room(1)
                    for k in range(4):
                        ins = pe.transpose(o[:, k * P:(k + 1) * P], xc[:, k, tok], ident)
                    ins.then_inc(small, 1)
                    o = room(2)
                    for k in range(2):
                        pe.transpose(o[:, k * P:(k + 1) * P], xc[:, 4 + k, tok], ident)
                    for k, m in enumerate((le, gt, ones)):
                        ins = pe.matmul(o[:, 2 * P + k * SH:2 * P + (k + 1) * SH], m, dtA[:, c, :], start=True, stop=True)
                    ins.then_inc(small, 1)
                    pe.wait_ge(seg_ready, g * GC + c + 1)
                    for h in range(2):
                        pe.matmul(room(3 + h)[:, :], gt, sg2[:, h, :], start=True, stop=True).then_inc(small, 1)
                    o = room(5)
                    for k in range(2):
                        ins = pe.matmul(o[:, k * P:(k + 1) * P], xc[:, 4 + k, tok], xc[:, 6 + k, tok], start=True, stop=True)
                    ins.then_inc(small, 1)
                    pe.wait_ge(s_act, (g * GC + c) * N_ACT + 1)
                    o = room(6)
                    for h in range(RH):
                        ins = pe.matmul(o[:, h * P:(h + 1) * P], kT[:, h // 2, :], qz[:, h // 2, h % 2, :], start=True, stop=True)
                    ins.then_inc(small, 1)
                    o = room(7)
                    for k in range(2):
                        ins = pe.matmul(o[:, k * 256:(k + 1) * 256], xc[:, 6 + k, tok],
                                        S_m[:, 4 * k:4 * k + 4, :].rearrange("p h e -> p (h e)"), start=True, stop=True)
                    ins.then_inc(small, 1)
                    o = room(8)
                    pe.wait_ge(s_dve, (g * GC + c) * N_DVE + 1)
                    for k in range(2):
                        ins = pe.matmul(o[:, k * 256:(k + 1) * 256], btok[:, k, :], xdec[:, k * 256:(k + 1) * 256], start=True, stop=True)
                    ins.then_inc(small, 1)
                    pe.wait_ge(s_dve, (g * GC + c) * N_DVE + 2)
                    o = room(9)
                    for h in range(RH):
                        pe.matmul(o[:, h * RD:(h + 1) * RD], PT[:, h, :], vb[:, c, h * RD:(h + 1) * RD], start=True, stop=False)
                        ins = pe.matmul(o[:, h * RD:(h + 1) * RD], qz[:, h // 2, h % 2, :], S_r[:, h // 2, :], start=False, stop=True)
                    ins.then_inc(small, 1)
                    o = room(10)
                    for h in range(RH):
                        r = slice(h % 2 * RD, h % 2 * RD + RD)
                        ins = pe.matmul(o[r, h // 2 * RD:(h // 2 + 1) * RD], qr[:, c, RW + h * RD:RW + (h + 1) * RD],
                                        vb[:, c, h * RD:(h + 1) * RD], start=True, stop=True)
                    ins.then_inc(small, 1)
                    o = room(11)
                    for h in range(SH):
                        ins = pe.matmul(o[:, h * SP_:(h + 1) * SP_], E[:, h, :], xdt[:, h, :], start=True, stop=True)
                    ins.then_inc(small, 1)
    return held



SBL = 8
SBN = T // SBL
LK = SBL * S5C
GQ = 4
CODY = (6.28125, 0.0019350051879882812, 3.0199159819583e-07)


CH, CD = 4, 256
MT = MEM // P
M_BANKS = 4


def split_rows(pool, room, nearest, rest, steps, before, gain=None):
    for k in range(2):
        scaled = pool.tensor_scalar(room[:, k, :], room[:, k, :], W_SCALE, gain[:, k:k + 1] if gain is not None else None, ALU.mult,
                                    *([ALU.mult] if gain is not None else []))
    scaled.then_inc(steps, 1)
    pool.wait_ge(steps, before + 1)
    pool.tensor_copy(nearest, room).then_inc(steps, 1)
    pool.wait_ge(steps, before + 2)
    pool.tensor_tensor(rest, room, nearest, ALU.subtract).then_inc(steps, 1)


class Memory:

    def __init__(self, dram, sb, sem, bank, keys_t, values, wq, rooms_v):
        self.dram, self.bank, self.keys_t, self.values, self.wq = dram, bank, keys_t, values, wq
        self.wk, self.wv = wq[:, :, :, :].rearrange("p h k n -> p (h k n)").bitcast(F32).rearrange("p (k n) -> p k n", k=KT), rooms_v
        self.mem, self.mT = sb("mem_t", [P, MT, D]), sb("mT", [P, KT, MEM])
        self.ident, self.nhalf, self.mem_gain, self.cross_gain = sb("cst_m", [P, P]), sb("nhalf_m", [P, MT]), sb("gm", [P, KT]), sb("g_cross", [P, KT])
        self.ss, self.ms, self.rs = sb("ss_m", [P, MT]), sb("ms_m", [P, MT]), sb("rs_m", [P, MT])
        self.junk = self.mT[:, :, :].rearrange("p a b -> p (a b)").rearrange("p (m d) -> p m d", m=MT)
        self.stage = [self.mem[:, :, :], self.junk]
        self.ld, self.k_ld, self.v_ld = sem("mem_loaded"), sem("w_ck_loaded"), sem("w_cv_loaded")
        self.sq, self.msd, self.rsd, self.xs = sem("mem_squares"), sem("mem_mean"), sem("mem_rstd"), sem("mem_scaled")
        self.done, self.taken = sem("mem_results"), sem("mem_results_taken")
        self.q_ld, self.q_split = [sem(f"w_cq_loaded{i}") for i in range(2)], sem("w_cq_split")
        self.keys_done, self.all_done = KT, KT + 2 * MT

    def loads(self, sp):
        sp.dma_start(self.mem[:, :, :], self.dram["mem"][0].rearrange("(m p) d -> p m d", p=P)).then_inc(self.ld, 16)
        sp.dma_start(self.ident[:, :], self.dram["cst"][:, K_ID:K_ID + P]).then_inc(self.ld, 16)
        sp.dma_start(self.nhalf[:, :], self.dram["cst"][:, K_HALF:K_HALF + MT]).then_inc(self.ld, 16)
        sp.dma_start(self.mem_gain[:, :], self.dram["mem_norm_g"].rearrange("(k p) -> p k", p=P)).then_inc(self.ld, 16)
        sp.dma_start(self.cross_gain[:, :], self.dram["norm_cross_g"][0].rearrange("(k p) -> p k", p=P)).then_inc(self.ld, 16)

    def weight_loads(self, sp):
        rows = self.dram["w_ck"][0].rearrange("(k p) n -> p k n", p=P)
        for h in range(2):
            hh = slice(4 * h, 4 * h + 4)
            sp.dma_start(self.wk[:, hh, :], rows[:, hh, :]).then_inc(self.k_ld, 16)
        rows = self.dram["w_cv"][0].rearrange("(k p) n -> p k n", p=P)
        for h in range(2):
            sp.dma_start(self.wv[h], rows[:, 4 * h:4 * h + 4, :]).then_inc(self.v_ld, 16)

    def query_loads(self, sp):
        rows = self.dram["w_cq"][0].rearrange("(k p) n -> p k n", p=P)
        sp.wait_ge(self.taken, self.all_done)
        for n in range(KT // 2):
            if n >= 2:
                sp.wait_ge(self.q_split, 3 * (n - 1))
            sp.dma_start(self.stage[n % 2], rows[:, 2 * n:2 * n + 2, :]).then_inc(self.q_ld[n % 2], 16)

    def norm(self, pool):
        pool.wait_ge(self.ld, 80)
        pool.wait_ge(self.sq, MT)
        pool.tensor_scalar(self.ms[:, :], self.ss[:, :], 1.0 / D, EPS, ALU.mult, ALU.add).then_inc(self.msd, 1)
        pool.wait_ge(self.msd, 1)
        pool.tensor_tensor(self.rs[:, :], self.ms[:, :], self.nhalf[:, :], ALU.pow).then_inc(self.rsd, 1)
        pool.wait_ge(self.rsd, 1)
        for m in range(MT):
            pool.tensor_scalar(self.mem[:, m, :], self.mem[:, m, :], self.rs[:, m:m + 1], None, ALU.mult).then_inc(self.xs, 1)

    def split_queries(self, pool):
        for n in range(KT // 2):
            k = slice(2 * n, 2 * n + 2)
            pool.wait_ge(self.q_ld[n % 2], n // 2 * 16 + 16)
            split_rows(pool, self.stage[n % 2], self.wq[:, 0, k, :], self.wq[:, 1, k, :], self.q_split, 3 * n, self.cross_gain[:, k])

    def squares(self, act):
        act.wait_ge(self.ld, 80)
        for m in range(MT):
            act.activation(self.junk[:, m, :], self.mem[:, m, :], ACT.Square, accum_out=self.ss[:, m:m + 1]).then_inc(self.sq, 1)

    def take_results(self, act):
        n = 0
        for kt in range(0, KT, 2):
            act.wait_ge(self.done, n + 1)
            for j in range(2):
                ins = act.activation(self.mT[:, kt + j, :], self.bank[n % M_BANKS][:, j * MEM:(j + 1) * MEM], ACT.Copy, scale=self.mem_gain[:, kt + j:kt + j + 1])
            ins.then_inc(self.taken, 1)
            n += 1
        for e in range(0, KT, 2):
            act.wait_ge(self.done, n + 1)
            act.activation(self.keys_t[:, e:e + 2, :], self.bank[n % M_BANKS][:, :].rearrange("p (a b) -> p a b", a=2), ACT.Copy).then_inc(self.taken, 1)
            n += 1
        for m in range(MT):
            for h in range(2):
                act.wait_ge(self.done, n + 1)
                act.activation(self.values[:, m, h * 512:(h + 1) * 512], self.bank[n % M_BANKS][:, :], ACT.Copy).then_inc(self.taken, 1)
                n += 1
        assert n == self.all_done

    def compute(self, pe):
        def slot(n):
            if n >= M_BANKS:
                pe.wait_ge(self.taken, n - M_BANKS + 1)
            return self.bank[n % M_BANKS]

        n = 0
        pe.wait_ge(self.ld, 80)
        pe.wait_ge(self.xs, MT)
        for kt in range(0, KT, 2):
            o = slot(n)
            for j in range(2):
                for m in range(MT):
                    ins = pe.transpose(o[:, j * MEM + m * P:j * MEM + (m + 1) * P], self.mem[:, m, (kt + j) * P:(kt + j + 1) * P], self.ident[:, :])
            ins.then_inc(self.done, 1)
            n += 1
        pe.wait_ge(self.taken, KT // 2)
        pe.wait_ge(self.k_ld, 32)
        for e in range(0, KT, 2):
            o = slot(n)
            for j in range(2):
                for kt in range(KT):
                    ins = pe.matmul(o[:, j * MEM:(j + 1) * MEM], self.wk[:, kt, (e + j) * P:(e + j + 1) * P], self.mT[:, kt, :], start=(kt == 0), stop=(kt == KT - 1))
            ins.then_inc(self.done, 1)
            n += 1
        pe.wait_ge(self.v_ld, 32)
        for m in range(MT):
            for h in range(2):
                o = slot(n)
                for kt in range(KT):
                    ins = pe.matmul(o[:, :], self.mT[:, kt, m * P:(m + 1) * P], self.wv[kt // 4][:, kt % 4, h * 512:(h + 1) * 512], start=(kt == 0), stop=(kt == KT - 1))
                ins.then_inc(self.done, 1)
                n += 1


def s5_mixer(nc, env, dram, held, keys_t, values, wq):
    DT2 = env["s5_turn"]
    with ExitStack() as ctx:
        def sb(name, shape, dt=F32):
            return ctx.enter_context(nc.sbuf_tensor(name, shape, dt))

        def sem(name):
            return nc.alloc_semaphore(name)

        cst = sb("cst_b", [P, P])
        anat = sb("anat", [S5G, 2, 2, S5P])
        cnat = sb("cnat", [P, 2, 2, 2, S5P])
        bnat = sb("bnat", [P, 2, S5G, S5C])
        step = sb("step", [P, S5G])
        d_bc = sb("d5_bc", [P, S5W])
        b_bc = sb("b5_bc", [P, S5W])
        wglu = sb("wglu", [P, 2, S5W])
        w = sb("s5_work", [P, 16, S5G])
        pw = sb("powers", [P, 2, SBL + 1, S5G])
        pv = sb("powers_back", [P, 2, SBL, S5G])
        Ba, Bb, Bt = (sb(n, [P, S5G, S5C]) for n in ("Ba", "Bb", "Bt"))
        Ca, Cb, Cc, Cd = (sb(n, [P, S5G, S5C]) for n in ("Ca", "Cb", "Cc", "Cd"))
        Cr, Ci = sb("Cr", [P, S5G, S5C]), sb("Ci", [P, S5G, S5C])
        u8 = sb("u8", [P, 2, S5G])
        r8 = sb("r8", [P, S5G])
        TC, TS = sb("TC", [P, S5G, SBN + 1]), sb("TS", [P, S5G, SBN + 1])
        U = sb("U5", [P, 2, SBL, S5W])
        Y5 = sb("Y5", [P, 2, SBL, S5W])
        big = sb("s5_big", [P, 8 * 1024])
        tmp = [big[:, i * 2048:(i + 1) * 2048].rearrange("p (g b) -> p g b", g=S5G) for i in range(2)]
        Uc = big[:, 0:1024].rearrange("p (h g k) -> p h g k", h=2, g=GQ)
        UT = big[:, 1024:2048].rearrange("p (g b) -> p g b", g=GQ)
        z1 = big[:, 2048:3072].rearrange("p (g b) -> p g b", g=GQ)
        z2 = big[:, 3072:4096].rearrange("p (g b) -> p g b", g=GQ)
        W1 = big[:, 4096:5120].rearrange("p (g b) -> p g b", g=GQ)
        W2 = big[:, 5120:6144].rearrange("p (g b) -> p g b", g=GQ)
        z = big[:, 6144:7168].rearrange("p (g b) -> p g b", g=GQ)
        t5 = big[:, 7168:8192]
        MB = sb("MB", [P, GQ, LK])
        BmT = sb("BmT", [P, 2, GQ, P])
        BZ = sb("BZ", [P, GQ, (2 * SBL - 1) * S5C])
        CZ = sb("CZ", [P, GQ, 2 * SBL * S5C])
        CM = sb("CM", [P, GQ, LK])
        Tm = sb("Tm", [P, GQ, LK])
        bank = [ctx.enter_context(nc.psum_tensor(f"bankB{i}", [P, 512], F32)) for i in range(4)]
        vbank = ctx.enter_context(nc.psum_tensor("vbank", [P, GQ, 2, SBN], F32))
        ident = cst[:, :]
        rooms_v = [t.rearrange("p (k n) -> p k n", k=4) for t in (Y5[:, :, :, :].rearrange("p h s c -> p (h s c)"), big[:, 4096:])]
        no_rows = sb("no_rows", [P, D])

        memory = Memory(dram, sb, sem, [vbank[:, i, :, :].rearrange("p k b -> p (k b)") for i in range(M_BANKS)], keys_t, values, wq, rooms_v)

        ld, u_ld = sem("s5_params_loaded"), sem("s5_u_loaded")
        tr0, s1, s2, act0 = sem("s5_params_transposed"), sem("s5_setup_dve"), sem("s5_setup_act"), sem("s5_C_taken")
        dve_t = sem("s5_turn_dve")
        zeroed, uc_ready, mb_ready, z_ready, y_taken = (sem("s5_zeroed"), sem("s5_u_sorted"), sem("s5_matrices"),
                                                        sem("s5_states"), sem("s5_y_taken"))
        ut_done, mb_done, tm_done, v_done, y_done = (sem("s5_uT_done"), sem("s5_BT_done"), sem("s5_T_done"),
                                                     sem("s5_V_done"), sem("s5_y_done"))
        ut_taken, mb_taken, tm_taken = sem("s5_uT_taken"), sem("s5_BT_taken"), sem("s5_T_taken")
        pre, gelu, gt_done, gt_taken, glu_done, glu_b, sig, s5_out, st = (
            sem("s5_plus_Du"), sem("s5_gelu"), sem("s5_gT_done"), sem("s5_gT_taken"), sem("s5_glu_done"),
            sem("s5_glu_bias"), sem("s5_sigmoid"), sem("s5_out"), sem("s5_stored"))
        y_clear = sem("ybuf_cleared")
        ctx.enter_context(nc.allow_non_contiguous_dma(reason="gains by rows, loaded once"))
        block = ctx.enter_context(nc.Block())

        @block.sync
        def _(sp):
            memory.loads(sp)
            for j in range(2):
                for r, a in enumerate(("s5_A_re", "s5_A_im")):
                    sp.dma_start(anat[:, r, j, :], dram[a][0]).then_inc(ld, 16)
                for r, a in enumerate(("s5_C_re", "s5_C_im")):
                    sp.dma_start(cnat[:, r, :, j, :], dram[a][0].rearrange("(a g) c p -> (g c) a p", a=2)).then_inc(ld, 16)
                for r, a in enumerate(("s5_B_re", "s5_B_im")):
                    sp.dma_start(bnat[j * S5P:(j + 1) * S5P, r, :, :], dram[a][0].rearrange("g p c -> p g c")).then_inc(ld, 16)
            sp.dma_start(step[:, :], dram["s5_log_step"][0].partition_broadcast(P)).then_inc(ld, 16)
            sp.dma_start(cst[:, :], dram["cst"][:, K_ID:K_ID + P]).then_inc(ld, 16)
            sp.dma_start(d_bc[:, :], dram["s5_D"][0].partition_broadcast(P)).then_inc(ld, 16)
            sp.dma_start(b_bc[:, :], dram["s5_b_glu"][0].partition_broadcast(P)).then_inc(ld, 16)
            sp.dma_start(wglu[:, :, :], dram["s5_w_glu"][0].rearrange("(k p) n -> p k n", p=P)).then_inc(ld, 16)
            memory.weight_loads(sp)
            for h in range(2):
                sp.dma_start(U[:, h, :, :], dram["u_scr"].rearrange("(h b t) c -> h b t c", h=2, t=SBL)[h]).then_inc(u_ld, 16)
            memory.query_loads(sp)
            sp.wait_ge(zeroed, 3)
            spare = dram["ybuf"].rearrange("(b p) d -> p b d", p=P)[:, USED_MIN:, :]
            sp.dma_start(spare, bc(no_rows[:, :], 1, NB - USED_MIN)).then_inc(y_clear, 16)
            for h in range(2):
                sp.wait_ge(s5_out, 4 * h + 4)
                sp.dma_start(dram["cat"].rearrange("(h b t) d -> h b t d", h=2, t=SBL)[h, :, :, RW + SW:], Y5[:, h, :, :]).then_inc(st, 16)
            sp.wait_ge(st, 32)
            sp.wait_ge(y_clear, 16)

        @block.gpsimd
        def _(pool):
            for h in held:
                pool.sem_clear(h)
            pool.memset(no_rows[:, :], 0.0).then_inc(zeroed, 1)
            pool.memset(BZ[:, :, :], 0.0).then_inc(zeroed, 1)
            pool.memset(CZ[:, :, :], 0.0).then_inc(zeroed, 1)
            memory.norm(pool)
            memory.split_queries(pool)

        @block.vector
        def _(dve):
            ch = Chain(dve, s1)
            tt, ts, stt = dve.tensor_tensor, dve.tensor_scalar, dve.scalar_tensor_tensor

            def do(f, *a):
                ch.post(f(*a))
                ch.wait()

            def W(i):
                return w[:, i, :]

            DELTA, MAG, ANG, K_, SIN, COS, X, LR, LI, DEN, CR, CI, X2 = range(13)
            dve.wait_ge(ld, 16 * 17)
            dve.wait_ge(tr0, 1)
            AR, AI = w[:, 13, :], w[:, 14, :]
            do(dve.tensor_copy, AR, bank[0][:, 0:S5G])
            do(dve.tensor_copy, AI, bank[0][:, S5G:2 * S5G])
            dve.wait_ge(s2, 1)
            do(tt, W(MAG), AR, W(DELTA), ALU.mult)
            do(tt, W(ANG), AI, W(DELTA), ALU.mult)
            mag_at = ch.n
            do(ts, W(K_), W(ANG), 1.0 / (2 * np.pi), 12582912.0, ALU.mult, ALU.add)
            do(ts, W(K_), W(K_), -12582912.0, None, ALU.add)
            for c in CODY:
                do(stt, W(ANG), W(K_), -c, W(ANG), ALU.mult, ALU.add)
            do(ts, W(ANG), W(ANG), 3.1415925, -3.1415925, ALU.min, ALU.max)
            do(ts, W(X), W(ANG), -1.0, None, ALU.mult)
            do(tt, W(X), W(X), W(ANG), ALU.max)
            do(ts, W(X), W(X), -1.0, np.pi / 2, ALU.mult, ALU.add)
            ang_at = ch.n
            assert (mag_at, ang_at) == env["s5_marks"], (mag_at, ang_at)
            dve.wait_ge(s2, 5)
            do(tt, W(LR), W(MAG), W(COS), ALU.mult)
            do(tt, W(LI), W(MAG), W(SIN), ALU.mult)
            do(tt, W(DEN), AR, AR, ALU.mult)
            do(tt, W(X), AI, AI, ALU.mult)
            do(tt, W(DEN), W(DEN), W(X), ALU.add)
            do(dve.reciprocal, W(DEN), W(DEN))
            do(ts, W(K_), W(LR), -1.0, None, ALU.add)
            do(tt, W(CR), W(K_), AR, ALU.mult)
            do(tt, W(X), W(LI), AI, ALU.mult)
            do(tt, W(CR), W(CR), W(X), ALU.add)
            do(tt, W(CR), W(CR), W(DEN), ALU.mult)
            do(tt, W(CI), W(LI), AR, ALU.mult)
            do(tt, W(X), W(K_), AI, ALU.mult)
            do(tt, W(CI), W(CI), W(X), ALU.subtract)
            do(tt, W(CI), W(CI), W(DEN), ALU.mult)
            cr, ci = bc(W(CR), 2, S5C), bc(W(CI), 2, S5C)
            br, bi = bnat[:, 0, :, :], bnat[:, 1, :, :]
            lo, hi = slice(0, S5P), slice(S5P, P)
            do(tt, Ba[:, :, :], cr, br, ALU.mult)
            do(tt, Bt[:, :, :], ci, bi, ALU.mult)
            do(tt, Ba[:, :, :], Ba[:, :, :], Bt[:, :, :], ALU.subtract)
            do(tt, Bb[:, :, :], cr, bi, ALU.mult)
            do(tt, Bt[:, :, :], ci, br, ALU.mult)
            do(tt, Bb[:, :, :], Bb[:, :, :], Bt[:, :, :], ALU.add)
            do(dve.tensor_copy, Bt[hi], Ba[hi])
            do(dve.tensor_copy, Ba[hi], Bb[hi])
            do(dve.tensor_copy, Bb[hi], Bt[hi])
            do(ts, Bb[lo], Bb[lo], -1.0, None, ALU.mult)
            dve.wait_ge(act0, 2)
            do(dve.tensor_copy, Ca[lo], Cr[lo])
            do(ts, Ca[hi], Ci[hi], -1.0, None, ALU.mult)
            do(ts, Cb[lo], Ci[lo], -1.0, None, ALU.mult)
            do(ts, Cb[hi], Cr[hi], -1.0, None, ALU.mult)
            do(ts, Cc[lo], Ci[lo], -1.0, None, ALU.mult)
            do(dve.tensor_copy, Cc[hi], Cr[hi])
            do(ts, Cd[lo], Cr[lo], -1.0, None, ALU.mult)
            do(ts, Cd[hi], Ci[hi], -1.0, None, ALU.mult)

            def cmul(o_r, o_i, a_r, a_i, b_r, b_i, x, y):
                do(tt, x, a_r, b_r, ALU.mult)
                do(tt, y, a_i, b_i, ALU.mult)
                do(tt, o_r, x, y, ALU.subtract)
                do(tt, x, a_r, b_i, ALU.mult)
                do(tt, y, a_i, b_r, ALU.mult)
                do(tt, o_i, x, y, ALU.add)

            do(dve.memset, pw[:, 0, 0, :], 1.0)
            do(dve.memset, pw[:, 1, 0, :], 0.0)
            do(dve.tensor_copy, pw[:, 0, 1, :], W(LR))
            do(dve.tensor_copy, pw[:, 1, 1, :], W(LI))
            n = 1
            while n < SBL:
                a = [pw[:, r, 1:n + 1, :] for r in range(2)]
                b = [bc(pw[:, r, n, :], 1, n) for r in range(2)]
                x, y = (tmp[i][:, 0:n, 0:S5G] for i in range(2))
                cmul(pw[:, 0, n + 1:2 * n + 1, :], pw[:, 1, n + 1:2 * n + 1, :], a[0], a[1], b[0], b[1], x, y)
                n *= 2
            for s in range(SBL):
                do(dve.tensor_copy, pv[:, :, s, :], pw[:, :, SBL - 1 - s, :])
            do(dve.tensor_copy, u8[:, 0, :], W(COS))
            do(dve.tensor_copy, u8[:, 1, :], W(SIN))
            n = 1
            while n < SBL:
                do(tt, W(X), u8[:, 0, :], u8[:, 0, :], ALU.mult)
                do(tt, W(X2), u8[:, 1, :], u8[:, 1, :], ALU.mult)
                do(stt, W(K_), u8[:, 0, :], 2.0, u8[:, 1, :], ALU.mult, ALU.mult)
                do(tt, u8[:, 0, :], W(X), W(X2), ALU.subtract)
                do(dve.tensor_copy, u8[:, 1, :], W(K_))
                n *= 2
            do(dve.memset, TC[:, :, 0:1], 1.0)
            do(dve.memset, TS[:, :, 0:1], 0.0)
            do(dve.tensor_copy, TC[:, :, 1:2], u8[:, 0, :].unsqueeze(2))
            do(dve.tensor_copy, TS[:, :, 1:2], u8[:, 1, :].unsqueeze(2))
            n = 1
            while n < SBN:
                b_r, b_i = (bc(t[:, :, n], 2, n) for t in (TC, TS))
                x, y = (tmp[i][:, :, 0:n] for i in range(2))
                cmul(TC[:, :, n + 1:2 * n + 1], TS[:, :, n + 1:2 * n + 1], TC[:, :, 1:n + 1], TS[:, :, 1:n + 1], b_r, b_i, x, y)
                n *= 2
            do(ts, TS[hi], TS[hi], -1.0, None, ALU.mult)
            dve.wait_ge(memory.done, memory.all_done)
            do(dve.memset, W1[:, :, 0:1], 0.0)
            do(dve.memset, W2[:, :, 0:1], 0.0)
            dve.wait_ge(zeroed, 3)
            dve.wait_ge(u_ld, 32)
            with dve.Fori(0, S5G // GQ) as q:
                c2 = Chain(dve, dve_t, q, DT2)
                gr = bass.ds(q * GQ, GQ)
                dve.wait_ge(y_done, q)
                for h in range(2):
                    src = U[:, h, :, bass.ds(q * GQ * S5C, GQ * S5C)].rearrange("p s (g c) -> p g s c", g=GQ)
                    ins = ts(Uc[:, h, :, :].rearrange("p g (s c) -> p g s c", s=SBL), src, 1.0, None, ALU.mult)
                    ins.then_inc(uc_ready, 1)

                def powers(o, pp, A, B, k):
                    oo = o.rearrange("p g (s c) -> p g s c", c=S5C)
                    for s, M in ((0, A), (1, B)):
                        dst = oo if s == 0 else t5[:, 0:GQ * k * S5C].rearrange("p (g s c) -> p g s c", g=GQ, s=k)
                        for gg in range(GQ):
                            mr = bc(M[:, bass.ds(q * GQ + gg, 1), :].squeeze(1), 1, k)
                            pr = bc(pp[:, s, :, bass.ds(q * GQ + gg, 1)].squeeze(2), 2, S5C)
                            c2.post(tt(dst[:, gg, :, :], pr, mr, ALU.mult))
                    c2.wait()
                    return tt(o, o, t5[:, 0:GQ * k * S5C].rearrange("p (g k) -> p g k", g=GQ), ALU.add)

                powers(MB[:, :, :], pv, Ba, Bb, SBL).then_inc(mb_ready, 1)
                dve.wait_ge(mb_ready, q * 4 + 1)
                ts(BZ[:, :, (SBL - 1) * S5C:SBL * S5C], Ba[:, gr, :], 1.0, None, ALU.mult).then_inc(mb_ready, 1)
                powers(CZ[:, :, (SBL - 1) * S5C:], pw, Ca, Cb, SBL + 1).then_inc(mb_ready, 1)
                dve.wait_ge(mb_ready, q * 4 + 3)
                powers(CM[:, :, :], pw[:, :, 1:, :], Cc, Cd, SBL).then_inc(mb_ready, 1)
                dve.wait_ge(v_done, q + 1)
                c2.post(tt(z1, TC[:, gr, 0:SBN], vbank[:, :, 0, :], ALU.mult))
                c2.post(tt(z2, TS[:, gr, 0:SBN], vbank[:, :, 1, :], ALU.mult))
                c2.wait()
                c2.post(tt(z1, z1, z2, ALU.add))
                c2.wait()
                for gg in range(GQ):
                    rr = bc(r8[:, bass.ds(q * GQ + gg, 1)].squeeze(1), 1, SBN)
                    c2.post(dve.tensor_tensor_scan(z[:, gg, :], rr, z1[:, gg, :], 0.0, ALU.mult, ALU.add))
                c2.wait()
                c2.post(tt(W1[:, :, 1:], TC[:, gr, 0:SBN - 1], z[:, :, 0:SBN - 1], ALU.mult))
                tt(W2[:, :, 1:], TS[:, gr, 0:SBN - 1], z[:, :, 0:SBN - 1], ALU.mult).then_inc(z_ready, 1)
                dve.wait_ge(y_done, q + 1)
                for h in range(2):
                    dst = Y5[:, h, :, bass.ds(q * GQ * S5C, GQ * S5C)].rearrange("p s (g c) -> p g s c", g=GQ)
                    ts(dst, bank[2 + h][:, :].rearrange("p (g s c) -> p g s c", g=GQ, s=SBL), 1.0, None, ALU.mult).then_inc(y_taken, 1)
                assert c2.n == DT2, c2.n
            dve.wait_ge(y_taken, 2 * (S5G // GQ))
            Uf, Yf = (t[:, :, :, :].rearrange("p h s c -> p (h s) c") for t in (U, Y5))
            for h in range(2):
                hh = slice(h * SBL, (h + 1) * SBL)
                tt(Uf[:, hh, :], Uf[:, hh, :], bc(d_bc[:, :], 1, SBL), ALU.mult).then_inc(pre, 1)
                dve.wait_ge(pre, 2 * h + 1)
                tt(Yf[:, hh, :], Yf[:, hh, :], Uf[:, hh, :], ALU.add).then_inc(pre, 1)
            for j in range(SBL):
                jj = slice(2 * j, 2 * j + 2)
                dve.wait_ge(glu_done, j + 1)
                tt(Uf[:, jj, :], bank[j % 2][:, :].rearrange("p (a n) -> p a n", a=2), bc(b_bc[:, :], 1, 2), ALU.add).then_inc(glu_b, 1)
                if j:
                    k = slice(2 * j - 2, 2 * j)
                    dve.wait_ge(sig, j)
                    tt(Yf[:, k, :], Yf[:, k, :], Uf[:, k, :], ALU.mult).then_inc(s5_out, 1)
            k = slice(2 * SBL - 2, 2 * SBL)
            dve.wait_ge(sig, SBL)
            tt(Yf[:, k, :], Yf[:, k, :], Uf[:, k, :], ALU.mult).then_inc(s5_out, 1)

        @block.scalar
        def _(act):
            memory.squares(act)
            act.wait_ge(ld, 16 * 17)
            act.activation(w[:, 0, :], step[:, :], ACT.Exp).then_inc(s2, 1)
            act.wait_ge(tr0, 2)
            for r, C in enumerate((Cr, Ci)):
                act.activation(C[:, :, :].rearrange("p g c -> p (g c)"), bank[1][:, r * 256:(r + 1) * 256], ACT.Copy).then_inc(act0, 1)
            act.wait_ge(s1, env["s5_marks"][0])
            act.activation(r8[:, :], w[:, 1, :], ACT.Exp, scale=float(SBL)).then_inc(s2, 1)
            act.wait_ge(s2, 2)
            act.activation(w[:, 1, :], w[:, 1, :], ACT.Exp).then_inc(s2, 1)
            act.wait_ge(s1, env["s5_marks"][1])
            act.activation(w[:, 4, :], w[:, 2, :], ACT.Sin).then_inc(s2, 1)
            act.activation(w[:, 5, :], w[:, 6, :], ACT.Sin).then_inc(s2, 1)
            memory.take_results(act)
            with act.Fori(0, S5G // GQ) as q:
                for h in range(2):
                    act.wait_ge(ut_done, q * 2 + h + 1)
                    act.activation(UT[:, :, h * P:(h + 1) * P], bank[h][:, :].rearrange("p (g b) -> p g b", g=GQ), ACT.Copy).then_inc(ut_taken, 1)
                act.wait_ge(mb_done, q + 1)
                b = bank[2][:, :].rearrange("p (g a k) -> p g a k", g=GQ, a=2)
                o = BmT[:, :, :, :].rearrange("p s g (a k) -> p s g a k", a=2)
                act.activation(o[:, 0], b, ACT.Copy)
                act.activation(o[:, 1, :, 0, :], b[:, :, 1, :], ACT.Copy)
                act.activation(o[:, 1, :, 1, :], b[:, :, 0, :], ACT.Copy).then_inc(mb_taken, 1)
                act.wait_ge(tm_done, q + 1)
                act.activation(Tm[:, :, :], bank[3][:, :].rearrange("p (g k) -> p g k", g=GQ), ACT.Copy).then_inc(tm_taken, 1)
            Yf = Y5[:, :, :, :].rearrange("p h s c -> p (h s) c")
            Uf = U[:, :, :, :].rearrange("p h s c -> p (h s) c")
            for h in range(2):
                hh = slice(h * SBL, (h + 1) * SBL)
                act.wait_ge(pre, 2 * h + 2)
                act.activation(Yf[:, hh, :], Yf[:, hh, :], ACT.Gelu_apprx_tanh).then_inc(gelu, 1)
            for j in range(SBL + 1):
                if j < SBL:
                    act.wait_ge(gt_done, j + 1)
                    if j >= 2:
                        act.wait_ge(glu_done, j - 1)
                    act.activation(BmT[:, j % 2, :, :], bank[2 + j % 2][:, :].rearrange("p (a b) -> p a b", a=4), ACT.Copy).then_inc(gt_taken, 1)
                if j:
                    jj = slice(2 * j - 2, 2 * j)
                    act.wait_ge(glu_b, j)
                    act.activation(Uf[:, jj, :], Uf[:, jj, :], ACT.Sigmoid).then_inc(sig, 1)

        @block.tensor
        def _(pe):
            pe.wait_ge(ld, 16 * 17)
            for r in range(2):
                ins = pe.transpose(bank[0][:, r * S5G:(r + 1) * S5G], anat[:, r, :, :].rearrange("g a p -> g (a p)"), ident[0:S5G, 0:S5G])
            ins.then_inc(tr0, 1)
            for r in range(2):
                for a in range(2):
                    ins = pe.transpose(bank[1][:, (2 * r + a) * P:(2 * r + a + 1) * P], cnat[:, r, a, :, :].rearrange("q j p -> q (j p)"), ident)
            ins.then_inc(tr0, 1)
            memory.compute(pe)
            pe.wait_ge(memory.taken, memory.all_done)
            pe.wait_ge(act0, 2)
            pe.wait_ge(s1, 2)
            with pe.Fori(0, S5G // GQ) as q:
                for h in range(2):
                    pe.wait_ge(uc_ready, q * 2 + h + 1)
                    for gg in range(GQ):
                        ins = pe.transpose(bank[h][:, gg * P:(gg + 1) * P], Uc[:, h, gg, :], ident)
                    ins.then_inc(ut_done, 1)
                pe.wait_ge(mb_ready, q * 4 + 1)
                pe.wait_ge(y_taken, q * 2)
                for gg in range(GQ):
                    ins = pe.transpose(bank[2][:, gg * P:(gg + 1) * P], MB[:, gg, :], ident)
                ins.then_inc(mb_done, 1)
                pe.wait_ge(mb_ready, q * 4 + 3)
                for gg in range(GQ):
                    for s in range(SBL):
                        a = (SBL - 1 - s) * S5C
                        ins = pe.matmul(bank[3][:, gg * P:(gg + 1) * P], BZ[:, gg, a:a + LK], CZ[:, gg, a:a + LK],
                                        start=(s == 0), stop=(s == SBL - 1))
                ins.then_inc(tm_done, 1)
                pe.wait_ge(ut_taken, q * 2 + 2)
                pe.wait_ge(mb_taken, q + 1)
                for gg in range(GQ):
                    for k in range(2):
                        ins = pe.matmul(vbank[:, gg, k, :], BmT[:, k, gg, :], UT[:, gg, :], start=True, stop=True)
                ins.then_inc(v_done, 1)
                pe.wait_ge(tm_taken, q + 1)
                pe.wait_ge(mb_ready, q * 4 + 4)
                pe.wait_ge(z_ready, q + 1)
                for h in range(2):
                    for gg in range(GQ):
                        o = bank[2 + h][:, gg * P:(gg + 1) * P]
                        b = slice(h * P, (h + 1) * P)
                        pe.matmul(o, UT[:, gg, b], Tm[:, gg, :], start=True, stop=False)
                        pe.matmul(o, W1[:, gg, b], CZ[:, gg, SBL * S5C:], start=False, stop=False)
                        ins = pe.matmul(o, W2[:, gg, b], CM[:, gg, :], start=False, stop=True)
                ins.then_inc(y_done, 1)
            Yf = Y5[:, :, :, :].rearrange("p h s c -> p (h s) c")
            pe.wait_ge(y_taken, 2 * (S5G // GQ))
            for j in range(SBL + 1):
                if j < SBL:
                    pe.wait_ge(gelu, j // 4 + 1)
                    if j >= 2:
                        pe.wait_ge(gt_taken, j - 1)
                    for a in range(2):
                        for k in range(2):
                            ins = pe.transpose(bank[2 + j % 2][:, (2 * a + k) * P:(2 * a + k + 1) * P], Yf[:, 2 * j + a, k * P:(k + 1) * P], ident)
                    ins.then_inc(gt_done, 1)
                if j:
                    i = j - 1
                    pe.wait_ge(gt_taken, i + 1)
                    if i >= 2:
                        pe.wait_ge(glu_b, i - 1)
                    for a in range(2):
                        for k in range(2):
                            ins = pe.matmul(bank[i % 2][:, a * S5W:(a + 1) * S5W], BmT[:, i % 2, 2 * a + k, :], wglu[:, k, :], start=(k == 0), stop=(k == 1))
                    ins.then_inc(glu_done, 1)



O_SCALE = 2.0 ** 3
KS = (RW + SW) // P


def cross_and_router(nc, env, dram, KT_, V_, wq, logits):
    with ExitStack() as ctx:
        def sb(name, shape, dt=F32):
            return ctx.enter_context(nc.sbuf_tensor(name, shape, dt))

        sem = nc.alloc_semaphore
        wo_s, wo_f = sb("w_out_s", [P, 2, KS, D], F16), sb("w_out_f", [P, KT - KS, D])
        wc = sb("w_co_t", [P, 2, KT, D], F16)
        wr = sb("w_route", [P, KT, NGR + NE])
        br = sb("b_route", [P, NGR + NE])
        ident = sb("cst_c", [P, P])
        nhalf = sb("nhalf_c", [P, GC])
        gf = sb("g_ffn", [P, KT])
        C = sb("cat_t", [P, GC, D])
        X = sb("Xc", [P, GC, D])
        H = sb("Hc", [P, GC, D])
        A1 = sb("A1", [P, KT, GT])
        A2 = sb("A2", [P, KT, GT])
        A1s, A2s = halves(A1), halves(A2)
        stage = [C[:, 2 * i:2 * i + 2, :] for i in range(2)]
        o_rooms = [X[:, 2 * i:2 * i + 2, :] for i in range(2)]
        pieces = [slice(2 * k, 2 * k + 2) for k in range(KT // 2)]
        Pm = sb("Pm", [P, 2, CH, MEM])
        ss, ms, rs = sb("ss_c", [P, 2, GC]), sb("ms_c", [P, 2, GC]), sb("rs_c", [P, 2, GC])
        mx, nm, sm, rc = (sb(n, [P, GC, CH]) for n in ("mx", "nm", "sm", "rc"))
        bank = [ctx.enter_context(nc.psum_tensor(f"bankC{i}", [P, 512], F32)) for i in range(8)]

        ld, w_ld, cat_ld, h_ld = sem("c_consts_loaded"), sem("w_out_rest_loaded"), sem("cat_loaded"), sem("x_res_loaded")
        tr, tr_taken = sem("transposes_done"), sem("transposes_taken")
        res, res_taken = sem("residual_products"), sem("residual_added")
        sq, msd, rsd, xs = sem("c_squares"), sem("c_mean"), sem("c_rstd"), sem("c_scaled")
        qd, q_taken = sem("q_done"), sem("q_taken")
        sc, p_exp, p_max, p_ready = sem("scores_done"), sem("scores_exp"), sem("scores_max"), sem("probs_ready")
        pt, pt_taken = sem("probsT_done"), sem("probsT_taken")
        od, o_taken = sem("o_done"), sem("o_taken")
        rt, rt_taken = sem("router_done"), sem("logits_taken")
        h_st, x_st = sem("h_stored"), sem("xn_stored")
        dve_c = sem("dve_steps_c")
        in_room, w_split, gain_s = [sem(f"w_c_loaded{i}") for i in range(2)], sem("w_c_split"), sem("router_rows_scaled")
        wo_ld, wo_hi, wo_lo, cat_lo = [sem(f"w_out_loaded{i}") for i in range(2)], sem("w_out_nearest"), sem("w_out_left"), sem("cat_left")
        hn_lo, o_lo = sem("hn_rest_c"), sem("o_rest")
        DVE_TURN = env["dve_c"]
        ctx.enter_context(nc.allow_non_contiguous_dma(reason="gains by rows, loaded once"))

        def turned(A, n):
            return A[:, 4 * (n % 2):4 * (n % 2) + 4, n // 2 * P:(n // 2 + 1) * P]

        def quarters(b):
            return b[:, :].rearrange("p (a n) -> p a n", a=4)

        def scores(c, j):
            return bank[4 * (1 - c % 2) + j]

        block = ctx.enter_context(nc.Block())

        @block.sync
        def _(sp):
            xv, cv, hv, nv = (dram[k].rearrange("(g c p) d -> g p c d", c=GC, p=P) if k != "x" else
                              dram[k][0].rearrange("(g c p) d -> g p c d", c=GC, p=P) for k in ("x", "cat", "h_scr", "xn_scr"))
            sp.dma_start(C[:, :, :], cv[0]).then_inc(cat_ld, 16)
            sp.dma_start(ident[:, :], dram["cst"][:, K_ID:K_ID + P]).then_inc(ld, 16)
            sp.dma_start(nhalf[:, :], dram["cst"][:, K_HALF:K_HALF + GC]).then_inc(ld, 16)
            sp.dma_start(gf[:, :], dram["norm_ffn_g"][0].rearrange("(k p) -> p k", p=P)).then_inc(ld, 16)
            sp.dma_start(wr[:, :, 0:NGR], dram["w_route_group"][0].rearrange("(k p) n -> p k n", p=P)).then_inc(ld, 16)
            sp.dma_start(wr[:, :, NGR:], dram["w_route_expert"][0].rearrange("(k p) n -> p k n", p=P)).then_inc(ld, 16)
            sp.dma_start(br[:, 0:NGR], dram["b_route_group"][0].partition_broadcast(P)).then_inc(ld, 16)
            sp.dma_start(br[:, NGR:], dram["b_route_expert"][0].partition_broadcast(P)).then_inc(ld, 16)
            rows = dram["w_out"][0].rearrange("(k p) n -> p k n", p=P)
            for n in range(KS // 2):
                if n >= 2:
                    sp.wait_ge(wo_lo, n - 1)
                sp.dma_start(o_rooms[n % 2], rows[:, 2 * n:2 * n + 2, :]).then_inc(wo_ld[n % 2], 16)
            sp.dma_start(wo_f[:, :, :], rows[:, KS:, :]).then_inc(w_ld, 16)
            sp.dma_start(H[:, :, :], xv[0]).then_inc(h_ld, 16)
            sp.wait_ge(tr, KT)
            for n, k in enumerate(pieces):
                if n >= 2:
                    sp.wait_ge(w_split, 3 * (n - 1))
                sp.dma_start(stage[n % 2], dram["w_co"][0].rearrange("(k p) n -> p k n", p=P)[:, k, :]).then_inc(in_room[n % 2], 16)
            sp.wait_ge(w_split, 3 * len(pieces))
            with sp.Fori(0, NG - 1) as g:
                sp.wait_ge(tr, g * 3 * KT + KT)
                sp.dma_start(C[:, :, :], cv[bass.ds(g + 1, 1)].squeeze(0)).then_inc(cat_ld, 16)
                sp.wait_ge(xs, g * 2 * GC + 2 * GC)
                sp.dma_start(nv[bass.ds(g, 1)].squeeze(0), X[:, :, :]).then_inc(x_st, 16)
                sp.dma_start(hv[bass.ds(g, 1)].squeeze(0), H[:, :, :]).then_inc(h_st, 16)
                sp.wait_ge(h_st, g * 16 + 16)
                sp.dma_start(H[:, :, :], xv[bass.ds(g + 1, 1)].squeeze(0)).then_inc(h_ld, 16)
            sp.wait_ge(xs, NG * 2 * GC)
            sp.dma_start(nv[NG - 1], X[:, :, :]).then_inc(x_st, 16)
            sp.dma_start(hv[NG - 1], H[:, :, :]).then_inc(h_st, 16)
            sp.wait_ge(x_st, 16 * NG)
            sp.wait_ge(h_st, 16 * NG)

        @block.gpsimd
        def _(pool):
            pool.wait_ge(ld, 16 * 7)
            pool.tensor_tensor(wr[:, :, :], wr[:, :, :], bc(gf[:, :], 2, NGR + NE), ALU.mult).then_inc(gain_s, 1)

            def rstd(g, i):
                for c in range(GC):
                    pool.wait_ge(msd, g * 2 * GC + i * GC + c + 1)
                    pool.tensor_tensor(rs[:, i, c:c + 1], ms[:, i, c:c + 1], nhalf[:, 0:1], ALU.pow).then_inc(rsd, 1)

            rstd(0, 0)
            for n, k in enumerate(pieces):
                pool.wait_ge(in_room[n % 2], n // 2 * 16 + 16)
                split_rows(pool, stage[n % 2], wc[:, 0, k, :], wc[:, 1, k, :], w_split, 3 * n)
            rstd(0, 1)
            with pool.Fori(1, NG) as g:
                rstd(g, 0)
                rstd(g, 1)

        @block.scalar
        def _(act):
            act.wait_ge(ld, 16 * 7)
            for n in range(KS // 2):
                act.wait_ge(wo_ld[n % 2], n // 2 * 16 + 16)
                act.activation(wo_s[:, 0, 2 * n:2 * n + 2, :], o_rooms[n % 2], ACT.Copy, scale=W_SCALE).then_inc(wo_hi, 1)
            with act.Fori(0, NG) as g:
                n = 0
                for m in range(2 * GC):
                    act.wait_ge(tr, g * 3 * KT + m + 1)
                    q = quarters(bank[n % 4])
                    a = KS - 4 if m % 2 else 4
                    ins = act.activation(turned(A1s[0], m)[:, 0:a, :], q[:, 0:a, :], ACT.Copy, scale=O_SCALE)
                    if m % 2:
                        ins = act.activation(A2[:, 0:4 - a, m // 2 * P:(m // 2 + 1) * P], q[:, a:, :], ACT.Copy, scale=W_SCALE * O_SCALE)
                    ins.then_inc(tr_taken, 1)
                    n += 1
                for i, (A, scale) in enumerate(((A1s[0], N_SCALE), (A1, 1.0))):
                    for c in range(GC):
                        act.wait_ge(res_taken, g * 4 * GC + i * 2 * GC + 2 * c + 2)
                        if i == 0 and c == 0:
                            act.wait_ge(pt, g * 2 * GC)
                        act.wait_ge(sq, g * 2 * GC + i * GC + c)
                        act.activation(Pm[:, 0, :, :].rearrange("p h m -> p (h m)"), H[:, c, :], ACT.Square, accum_out=ss[:, i, c:c + 1]).then_inc(sq, 1)
                    for m in range(2 * GC):
                        act.wait_ge(tr, g * 3 * KT + (i + 1) * KT + m + 1)
                        act.activation(turned(A, m), quarters(bank[n % 4]), ACT.Copy, scale=scale).then_inc(tr_taken, 1)
                        n += 1
                    if i:
                        break
                    for e in range(KT):
                        act.wait_ge(qd, g * KT + e + 1)
                        act.activation(A2[:, e, :], bank[n % 4][:, :], ACT.Copy, scale=UNSCALE).then_inc(q_taken, 1)
                        n += 1
                    def take_pt(c):
                        for j in range(2):
                            act.wait_ge(pt, g * 2 * GC + 2 * c + j + 1)
                            act.activation(A1[:, 4 * j:4 * j + 4, c * P:(c + 1) * P], bank[6 + j][:, :].rearrange("p (a b) -> p a b", a=4), ACT.Copy).then_inc(pt_taken, 1)

                    for c in range(GC):
                        for j in range(2):
                            act.wait_ge(p_max, g * 2 * GC + 2 * c + j + 1)
                            if c >= 2:
                                act.wait_ge(pt, g * 2 * GC + 2 * (c - 2) + 2)
                            for k in range(2):
                                h = 2 * j + k
                                act.activation(Pm[:, c % 2, h, :], scores(c, j)[:, k * MEM:(k + 1) * MEM], ACT.Exp,
                                               bias=nm[:, c, h:h + 1], scale=CD ** -0.5, accum_out=sm[:, c, h:h + 1]).then_inc(p_exp, 1)
                        if c:
                            take_pt(c - 1)
                    take_pt(GC - 1)
                    for e in range(KT):
                        act.wait_ge(od, g * KT + e + 1)
                        act.activation(A2s[0][:, e, :], bank[n % 4][:, :], ACT.Copy, scale=O_SCALE).then_inc(o_taken, 1)
                        n += 1

        @block.vector
        def _(dve):
            dve.wait_ge(ld, 16 * 7)
            for n in range(KS // 2):
                dve.wait_ge(wo_hi, n + 1)
                dve.scalar_tensor_tensor(wo_s[:, 1, 2 * n:2 * n + 2, :], o_rooms[n % 2], W_SCALE, wo_s[:, 0, 2 * n:2 * n + 2, :], ALU.mult, ALU.subtract).then_inc(wo_lo, 1)
            with dve.Fori(0, NG) as g:
                ch = Chain(dve, dve_c, g, DVE_TURN)

                def residual(i):
                    for c in range(GC):
                        for j in range(2):
                            dve.wait_ge(res, g * 4 * GC + i * 2 * GC + 2 * c + j + 1)
                            hh = H[:, c, j * 512:(j + 1) * 512]
                            dve.scalar_tensor_tensor(hh, bank[4 + j][:, :], 1.0 / (W_SCALE * O_SCALE), hh, ALU.mult, ALU.add).then_inc(res_taken, 1)
                        if c:
                            scale(i, c - 1)
                        mean(i, c)
                    if i == 0:
                        rest(0)
                        rest(1)
                    scale(i, GC - 1)

                def mean(i, c):
                    dve.wait_ge(sq, g * 2 * GC + i * GC + c + 1)
                    dve.tensor_scalar(ms[:, i, c:c + 1], ss[:, i, c:c + 1], 1.0 / D, EPS, ALU.mult, ALU.add).then_inc(msd, 1)

                def scale(i, c):
                    dve.wait_ge(rsd, g * 2 * GC + i * GC + c + 1)
                    dve.tensor_scalar(X[:, c, :], H[:, c, :], rs[:, i, c:c + 1], None, ALU.mult).then_inc(xs, 1)

                def rest(m):
                    dve.wait_ge(tr_taken, g * 3 * KT + KT + m + 1)
                    dve.scalar_tensor_tensor(turned(A1s[1], m), quarters(bank[m % 4]), N_SCALE, turned(A1s[0], m), ALU.mult, ALU.subtract).then_inc(hn_lo, 1)

                for m in range(2 * GC):
                    a = KS - 4 if m % 2 else 4
                    dve.wait_ge(tr_taken, g * 3 * KT + m + 1)
                    dve.scalar_tensor_tensor(turned(A1s[1], m)[:, 0:a, :], quarters(bank[m % 4])[:, 0:a, :], O_SCALE, turned(A1s[0], m)[:, 0:a, :], ALU.mult, ALU.subtract).then_inc(cat_lo, 1)
                dve.wait_ge(h_ld, g * 16 + 16)
                dve.wait_ge(tr, g * 3 * KT)
                dve.wait_ge(x_st, g * 16)
                residual(0)
                for m in range(2, 2 * GC):
                    rest(m)

                def probs(c):
                    dve.wait_ge(p_exp, g * CH * GC + CH * c + CH)
                    ch.post(dve.reciprocal(rc[:, c, :], sm[:, c, :]))
                    ch.wait()
                    dve.tensor_tensor(Pm[:, c % 2, :, :], Pm[:, c % 2, :, :], bc(rc[:, c, :], 2, MEM), ALU.mult).then_inc(p_ready, 1)

                for c in range(GC):
                    for j in range(2):
                        dve.wait_ge(sc, g * 2 * GC + 2 * c + j + 1)
                        hh = slice(2 * j, 2 * j + 2)
                        ch.post(dve.tensor_reduce(mx[:, c, hh], scores(c, j)[:, :].rearrange("p (a b) -> p a b", a=2), AX.X, ALU.max))
                        ch.wait()
                        dve.tensor_scalar(nm[:, c, hh], mx[:, c, hh], -CD ** -0.5, None, ALU.mult).then_inc(p_max, 1)
                    if c:
                        probs(c - 1)
                probs(GC - 1)
                for e in range(KT):
                    dve.wait_ge(o_taken, g * KT + e + 1)
                    dve.scalar_tensor_tensor(A2s[1][:, e, :], bank[e % 4][:, :], O_SCALE, A2s[0][:, e, :], ALU.mult, ALU.subtract).then_inc(o_lo, 1)
                residual(1)
                dve.wait_ge(rt, g + 1)
                o = logits[:, bass.ds(g * GC, GC), :]
                dve.tensor_tensor(o, bank[6][:, 0:GC * (NGR + NE)].rearrange("p (c n) -> p c n", c=GC), bc(br[:, :], 1, GC), ALU.add).then_inc(rt_taken, 1)
                assert ch.n == DVE_TURN, ch.n

        @block.tensor
        def _(pe):
            pe.wait_ge(ld, 16 * 7)
            pe.wait_ge(gain_s, 1)
            with pe.Fori(0, NG) as g:
                def transposes(i):
                    for n in range(2 * GC):
                        c, j = n // 2, n % 2
                        pe.wait_ge(tr_taken, g * 3 * KT + i * KT + (n - 3 if i or n > 3 else 0))
                        if i < 2 and n >= 4:
                            pe.wait_ge(hn_lo if i else cat_lo, g * KT + n - 3)
                        if i and j == 0:
                            pe.wait_ge(xs, g * 2 * GC + (i - 1) * GC + c + 1)
                        for k in range(4):
                            kt = 4 * j + k
                            ins = pe.transpose(bank[n % 4][:, k * P:(k + 1) * P], (X if i else C)[:, c, kt * P:(kt + 1) * P], ident[:, :])
                        ins.then_inc(tr, 1)

                def add_products(i, A, w):
                    for c in range(GC):
                        for j in range(2):
                            if c == 0:
                                if i == 0:
                                    pe.wait_ge(res_taken, g * 4 * GC)
                                else:
                                    pe.wait_ge(p_exp, g * CH * GC + CH * GC)
                            else:
                                pe.wait_ge(res_taken, g * 4 * GC + i * 2 * GC + 2 * c + j - 1)
                            n = KT if i else KS
                            ins = products(pe, bank[4 + j][:, :], [[a[:, kt, c * P:(c + 1) * P] for kt in range(n)] for a in A],
                                           [[w[:, h, kt, j * 512:(j + 1) * 512] for kt in range(n)] for h in range(2)], stop=bool(i))
                            for kt in range(n, KT):
                                ins = pe.matmul(bank[4 + j][:, :], A2[:, kt - n, c * P:(c + 1) * P], wo_f[:, kt - n, j * 512:(j + 1) * 512], start=False, stop=(kt == KT - 1))
                            ins.then_inc(res, 1)

                pe.wait_ge(cat_ld, g * 16 + 16)
                transposes(0)
                pe.wait_ge(tr_taken, g * 3 * KT + KT)
                pe.wait_ge(cat_lo, g * KT + KT)
                pe.wait_ge(w_ld, 16)
                pe.wait_ge(wo_lo, KS // 2)
                pe.wait_ge(rt_taken, g)
                add_products(0, A1s, wo_s)
                transposes(1)
                pe.wait_ge(tr_taken, g * 3 * KT + 2 * KT)
                pe.wait_ge(hn_lo, g * KT + KT)
                for e in range(KT):
                    if e >= 4:
                        pe.wait_ge(q_taken, g * KT + e - 3)
                    w = [[wq[:, h, kt, e * P:(e + 1) * P] for kt in range(KT)] for h in range(2)]
                    products(pe, bank[e % 4][:, :], w, [[A1s[h][:, kt, :] for kt in range(KT)] for h in range(2)]).then_inc(qd, 1)
                pe.wait_ge(q_taken, g * KT + KT)

                def turn_probs(c):
                    pe.wait_ge(p_ready, g * GC + c + 1)
                    for j in range(2):
                        if c:
                            pe.wait_ge(pt_taken, g * 2 * GC + 2 * (c - 1) + j + 1)
                        for k in range(4):
                            h, m = 2 * j + k // 2, k % 2
                            ins = pe.transpose(bank[6 + j][:, k * P:(k + 1) * P], Pm[:, c % 2, h, m * P:(m + 1) * P], ident[:, :])
                        ins.then_inc(pt, 1)

                for c in range(GC):
                    for j in range(2):
                        if c >= 2:
                            pe.wait_ge(p_exp, g * CH * GC + CH * (c - 2) + 2 * j + 2)
                        for k in range(2):
                            h = 2 * j + k
                            for e in range(2):
                                ins = pe.matmul(scores(c, j)[:, k * MEM:(k + 1) * MEM], A2[:, 2 * h + e, c * P:(c + 1) * P], KT_[:, 2 * h + e, :], start=(e == 0), stop=(e == 1))
                        ins.then_inc(sc, 1)
                    if c:
                        turn_probs(c - 1)
                turn_probs(GC - 1)
                pe.wait_ge(pt_taken, g * 2 * GC + 2 * GC)
                for e in range(KT):
                    if e >= 4:
                        pe.wait_ge(o_taken, g * KT + e - 3)
                        pe.wait_ge(o_lo, g * KT + e - 3)
                    h = e // 2
                    for m in range(MT):
                        ins = pe.matmul(bank[e % 4][:, :], V_[:, m, e * P:(e + 1) * P], A1[:, 2 * h + m, :], start=(m == 0), stop=(m == MT - 1))
                    ins.then_inc(od, 1)
                pe.wait_ge(o_taken, g * KT + KT)
                pe.wait_ge(o_lo, g * KT + KT)
                pe.wait_ge(w_split, 3 * len(pieces))
                add_products(1, A2s, wc)
                transposes(2)
                for c in range(GC):
                    pe.wait_ge(tr_taken, g * 3 * KT + 2 * KT + 2 * c + 2)
                    for kt in range(KT):
                        a = c * (NGR + NE)
                        ins = pe.matmul(bank[6][:, a:a + NGR + NE], A1[:, kt, c * P:(c + 1) * P], wr[:, kt, :], start=(kt == 0), stop=(kt == KT - 1))
                ins.then_inc(rt, 1)



HB = 2
SLOTS = 3
ROWS = NB * P
WHOLE = 12582912.0
MAX_TURNS = NB // HB - 1
MIN_TURNS = (USED_MIN - 1) // HB
PL_BLOCK, PL_EXPERT, PL_FREE, PL_TURNS, PL_USED, PL_END = np.cumsum([0, NB, NE, NE, 1, 1]).tolist()


def route(nc, env, dram, logits, gates, dest, destf, plan):
    with ExitStack() as ctx:
        def sb(name, shape, dt=F32):
            return ctx.enter_context(nc.sbuf_tensor(name, shape, dt))

        sem = nc.alloc_semaphore
        cst = sb("cst_r", [P, K_GAM])
        G4, O4 = sb("G4", [P, NCH, NGR]), sb("O4", [P, NCH, NGR])
        t4 = sb("t4", [P, NCH, NGR])
        e32 = sb("e32", [P, NCH, NGR, EPG])
        E8, t8, m8, O8 = (sb(n, [P, NCH, EPG]) for n in ("E8", "t8", "m8", "O8"))
        c1 = sb("c1", [P, 8, NCH])
        oh = sb("oh", [P, 2, NCH, NE])
        pos = sb("pos", [P, NCH, NE])
        both, before, cum, again = (sb(n, [P, NE, NCH]) for n in ("both", "before", "cum", "again"))
        nblk, start, end, used, rank, eq, t32 = (sb(n, [P, NE]) for n in ("nblk", "start", "end", "used", "rank", "eq", "t32"))
        cols, turns = sb("cols", [P, 4]), sb("turns_f", [P, 1])
        bank = [ctx.enter_context(nc.psum_tensor(f"bankR{i}", [P, 512], F32)) for i in range(2)]
        ld, s, a_s, cnt, marks = sem("r_consts"), sem("route_steps"), sem("route_exp"), sem("counts_done"), sem("pairs_marked_r")
        ready = sem("again_ready")
        lt, ones, one = cst[:, K_LT:K_LT + P], cst[:, K_ONE:K_ONE + P], cst[:, K_ONE:K_ONE + NE]

        def flat(t):
            return t[:, :, :].rearrange("p e c -> p (e c)")

        def by_c(t):
            return t[:, :, :].rearrange("p e c -> p c e")

        block = ctx.enter_context(nc.Block())

        @block.sync
        def _(sp):
            sp.dma_start(cst[:, :], dram["cst"][:, 0:K_GAM]).then_inc(ld, 16)

        @block.scalar
        def _(act):
            act.wait_ge(s, env["r_marks"][0])
            act.activation(t4[:, :, :], G4[:, :, :], ACT.Exp).then_inc(a_s, 1)
            act.wait_ge(s, env["r_marks"][1])
            act.activation(E8[:, :, :], t8[:, :, :], ACT.Exp).then_inc(a_s, 1)

        @block.vector
        def _(dve):
            ch = Chain(dve, s)
            tt, ts, stt, red = dve.tensor_tensor, dve.tensor_scalar, dve.scalar_tensor_tensor, dve.tensor_reduce
            seen = []
            dve.memset(again[:, :, :], 1.0).then_inc(ready, 1)
            dve.wait_ge(ready, 1)
            dve.memset(again[:, :, 0:1], 0.0).then_inc(ready, 1)
            dve.wait_ge(ready, 2)

            def do(f, *a):
                ch.post(f(*a))
                ch.wait()

            def first(o, x, m, n, idx, t):
                iota = bc(cst[:, K_IOTA:K_IOTA + n], 1, NCH)
                do(tt, t, x, bc(m, 2, n), ALU.is_lt)
                do(stt, t, t, 1000.0, iota, ALU.mult, ALU.add)
                do(red, idx, t, AX.X, ALU.min)
                do(tt, o, iota, bc(idx, 2, n), ALU.is_equal)

            GM, GS, GI, M1, I1, M2, I2, X = (c1[:, i, :] for i in range(8))
            gl = logits[:, :, 0:NGR]
            dve.wait_ge(ld, 16)
            do(red, GM, gl, AX.X, ALU.max)
            first(O4[:, :, :], gl, GM, NGR, GI, t4[:, :, :])
            do(tt, G4[:, :, :], gl, bc(GM, 2, NGR), ALU.subtract)
            seen.append(ch.n)
            el = logits[:, :, NGR:].rearrange("p c (g e) -> p c g e", g=NGR)
            for g in range(NGR):
                ch.post(tt(e32[:, :, g, :], el[:, :, g, :], bc(O4[:, :, g], 2, EPG), ALU.mult))
            ch.wait()
            do(red, m8[:, :, :], e32[:, :, :, :].rearrange("p c g e -> p c e g"), AX.X, ALU.add)
            do(red, M1, m8[:, :, :], AX.X, ALU.max)
            do(tt, t8[:, :, :], m8[:, :, :], bc(M1, 2, EPG), ALU.subtract)
            seen.append(ch.n)
            dve.wait_ge(a_s, 2)
            do(red, GS, t4[:, :, :], AX.X, ALU.add)
            do(red, M1, E8[:, :, :], AX.X, ALU.max)
            first(O8[:, :, :], E8[:, :, :], M1, EPG, I1, t8[:, :, :])
            do(stt, m8[:, :, :], O8[:, :, :], -4.0, E8[:, :, :], ALU.mult, ALU.add)
            do(red, M2, m8[:, :, :], AX.X, ALU.max)
            first(O8[:, :, :], m8[:, :, :], M2, EPG, I2, t8[:, :, :])
            do(tt, X, M1, M2, ALU.add)
            do(tt, X, X, GS, ALU.mult)
            do(dve.reciprocal, X, X)
            do(tt, gates[:, 0, :], M1, X, ALU.mult)
            do(tt, gates[:, 1, :], M2, X, ALU.mult)
            iota = bc(cst[:, K_IOTA:K_IOTA + NE], 1, NCH)
            for k, I in enumerate((I1, I2)):
                do(stt, I, GI, float(EPG), I, ALU.mult, ALU.add)
                do(tt, oh[:, k, :, :], iota, bc(I, 2, NE), ALU.is_equal)
            tt(by_c(both), oh[:, 0, :, :], oh[:, 1, :, :], ALU.add).then_inc(marks, 1)
            dve.wait_ge(marks, 1)
            do(dve.tensor_tensor_scan, flat(cum), flat(again), flat(both), 0.0, ALU.mult, ALU.add)
            tt(before[:, :, :], cum[:, :, :], both[:, :, :], ALU.subtract).then_inc(marks, 1)
            dve.wait_ge(cnt, 1)
            do(ts, nblk[:, :], bank[1][:, 0:NE], 1.0 / P, 0.5 - 0.5 / P, ALU.mult, ALU.add)
            do(ts, nblk[:, :], nblk[:, :], WHOLE, None, ALU.add)
            do(ts, nblk[:, :], nblk[:, :], -WHOLE, None, ALU.add)
            do(dve.tensor_tensor_scan, end[:, :], one, nblk[:, :], 0.0, ALU.mult, ALU.add)
            do(ts, used[:, :], nblk[:, :], 0.0, None, ALU.is_gt)
            do(dve.tensor_tensor_scan, rank[:, :], one, used[:, :], 0.0, ALU.mult, ALU.add)
            here = cst[:, K_TOK:K_TOK + 1]
            do(ts, eq[:, :], rank[:, :], -1.0, here, ALU.add, ALU.is_equal)
            do(tt, eq[:, :], eq[:, :], used[:, :], ALU.mult)
            do(tt, t32[:, :], eq[:, :], cst[:, K_IOTA:K_IOTA + NE], ALU.mult)
            do(red, cols[:, 0:1], t32[:, :], AX.X, ALU.add)
            do(tt, t32[:, :], eq[:, :], end[:, :], ALU.mult)
            do(red, cols[:, 1:2], t32[:, :], AX.X, ALU.add)
            do(stt, t32[:, :], end[:, :], here, used[:, :], ALU.is_le, ALU.mult)
            do(red, cols[:, 3:4], t32[:, :], AX.X, ALU.add)
            do(ts, cols[:, 2:3], rank[:, NE - 1:NE], -1.0, None, ALU.add)
            tt(cols[:, 2:3], cols[:, 2:3], cols[:, 3:4], ALU.min).then_inc(marks, 1)
            do(ts, turns[:, :], end[:, NE - 1:NE], 1.0 / HB, -0.5 - 0.25, ALU.mult, ALU.add)
            do(ts, turns[:, :], turns[:, :], WHOLE, None, ALU.add)
            do(ts, turns[:, :], turns[:, :], -WHOLE, float(MAX_TURNS), ALU.add, ALU.min)
            do(dve.tensor_copy, plan[:, PL_TURNS:PL_TURNS + 1], turns[0:1, :])
            do(dve.tensor_copy, plan[:, PL_USED:PL_USED + 1], rank[0:1, NE - 1:NE])
            dve.wait_ge(cnt, 2)
            do(dve.memset, plan[:, PL_FREE:PL_FREE + SLOTS], 0)
            do(dve.tensor_copy, plan[:, 0:PL_FREE], bank[1][0:1, 2 * NE:2 * NE + PL_FREE])
            do(dve.tensor_copy, plan[:, PL_FREE + SLOTS:PL_TURNS], bank[1][0:1, 2 * NE + PL_FREE:2 * NE + PL_TURNS - SLOTS])
            tt(start[:, :], end[:, :], nblk[:, :], ALU.subtract).then_inc(marks, 1)
            dve.wait_ge(marks, 4)
            do(ts, start[:, :], start[:, :], float(P), None, ALU.mult)
            do(tt, pos[:, :, :], bank[0][:, :].rearrange("p (e c) -> p c e", c=NCH), bc(start[:, :], 1, NCH), ALU.add)
            for k in range(2):
                do(tt, oh[:, k, :, :], pos[:, :, :], oh[:, k, :, :], ALU.mult)
                do(red, destf[:, k, :], oh[:, k, :, :], AX.X, ALU.add)
            do(dve.tensor_copy, dest[:, :, :], destf[:, :, :])
            assert tuple(seen) == env["r_marks"], seen

        @block.tensor
        def _(pe):
            pe.wait_ge(ld, 16)
            pe.wait_ge(marks, 1)
            pe.matmul(bank[0][:, :], lt, flat(both), start=True, stop=False)
            pe.wait_ge(marks, 2)
            pe.matmul(bank[0][:, :], ones, flat(before), start=False, stop=True)
            pe.matmul(bank[1][:, 0:NE], ones, cum[:, :, NCH - 1], start=True, stop=True).then_inc(cnt, 1)
            pe.wait_ge(marks, 3)
            for c, n, at in ((2, NB, 0), (0, NE, PL_EXPERT), (1, NE, PL_FREE)):
                ins = pe.transpose(bank[1][0:1, 2 * NE + at:2 * NE + at + n], cols[0:n, c:c + 1], cst[0:n, K_ID:K_ID + n])
            ins.then_inc(cnt, 1)


def experts(nc, env, dram, destf, plan):
    FT = DE // P
    with ExitStack() as ctx:
        def sb(name, shape, dt=F32):
            return ctx.enter_context(nc.sbuf_tensor(name, shape, dt))

        sem = nc.alloc_semaphore
        wg, wu, wd = sb("wg", [P, SLOTS, KT, DE]), sb("wu", [P, SLOTS, KT, DE]), sb("wd", [P, SLOTS, FT, D])
        xr = [sb(f"xr{i}", [P, D]) for i in range(HB)]
        xT = [sb(f"xT{i}", [P, KT, P]) for i in range(HB)]
        sg = [sb(f"sg{i}", [P, DE]) for i in range(HB)]
        hT = [sb(f"hT{i}", [P, FT, P]) for i in range(HB)]
        y = [sb(f"y{i}", [P, D]) for i in range(HB)]
        ident, iota, tok = sb("cst_e", [P, P]), sb("iota_e", [P, P]), sb("tok_e", [P, NCH])
        in_blk, at_row = sb("in_block", [P, 2 * NCH, NB]), sb("at_row", [P, 2 * NCH, P])
        blk, off = sb("blk", [P, 2 * NCH]), sb("off", [P, 2 * NCH])
        rows_of = sb("rows_of", [P, NB], U32)
        gf = sb("g_ffn_e", [P, KT])
        bank = [ctx.enter_context(nc.psum_tensor(f"bankE{i}", [P, 512], F32)) for i in range(8)]
        ld = sem("e_consts")
        first_ld = [sem(f"first_{n}_loaded") for n in ("wg", "wu", "wd")]
        w_ld = [sem(f"weights_loaded{j}") for j in range(SLOTS)]
        x_ld = [sem(f"rows_gathered{i}") for i in range(HB)]
        lists, marked, listed, rows_ok = sem("list_steps"), sem("pairs_marked"), sem("rows_listed"), sem("rows_known")
        xt, xt_t, gd, ud, sil, hr, ht, ht_t, yd, y_t = (sem(n) for n in (
            "xT_done", "xT_taken", "gate_done", "up_done", "silu_done_e", "h_ready", "hT_done", "hT_taken", "down_done", "y_taken"))
        y_st = [sem(f"y_stored{i}") for i in range(HB)]
        y_end = sem("last_y_stored")
        NT = NB // HB
        ctx.enter_context(nc.allow_non_contiguous_dma(reason="gains by rows, loaded once"))
        block = ctx.enter_context(nc.Block())

        def turns_used(eng):
            return eng.value_load(plan[0:1, PL_TURNS:PL_TURNS + 1], min_val=MIN_TURNS, max_val=MAX_TURNS)

        @block.sync
        def _(sp):
            wv = [dram[n][0].rearrange("e (k p) f -> e p k f", p=P) for n in ("w_gate", "w_up", "w_down")]
            here = (wg, wu, wd)

            def expert(u):
                return sp.value_load(plan[0:1, bass.ds(PL_EXPERT + u, 1)], min_val=0, max_val=NE - 1)

            def weights(u, j):
                e = expert(u)
                free = sp.value_load(plan[0:1, bass.ds(PL_FREE + u, 1)], min_val=0, max_val=NB)
                for w, src, used in zip(here, wv, (gd, ud, yd)):
                    sp.wait_ge(used, free * 2 if used is yd else free)
                    sp.dma_start(w[:, j, :, :], src[bass.ds(e, 1)].squeeze(0)).then_inc(w_ld[j], 16)

            e0 = expert(0)

            def first_weights(i):
                sp.dma_start(here[i][:, 0, :, :], wv[i][bass.ds(e0, 1)].squeeze(0)).then_inc(first_ld[i], 16)

            sp.dma_start(iota[:, :], dram["cst"][:, K_IOTA:K_IOTA + P]).then_inc(ld, 16)
            sp.dma_start(tok[:, :], dram["cst"][:, K_TOK:K_TOK + NCH]).then_inc(ld, 16)
            sp.dma_start(gf[:, :], dram["norm_ffn_g"][0].rearrange("(k p) -> p k", p=P)).then_inc(ld, 16)
            sp.dma_start(ident[:, :], dram["cst"][:, K_ID:K_ID + P]).then_inc(ld, 16)
            first_weights(0)
            first_weights(1)
            e1 = expert(1)
            for i in range(HB):
                sp.wait_ge(x_ld[i], 16)
            first_weights(2)
            for w, src in zip(here, wv):
                sp.dma_start(w[:, 1, :, :], src[bass.ds(e1, 1)].squeeze(0)).then_inc(w_ld[1], 16)
            n_used = sp.value_load(plan[0:1, PL_USED:PL_USED + 1], min_val=2, max_val=NE)
            with sp.Fori(0, NE // SLOTS) as t:
                for i in range(SLOTS):
                    u = t * SLOTS + 2 + i
                    with sp.If(u < n_used):
                        weights(u, (2 + i) % SLOTS)

        @block.gpsimd
        def _(pool):
            used = turns_used(pool)
            pool.wait_ge(rows_ok, 1)

            def gather(b):
                if b >= HB:
                    pool.wait_ge(xt, 2 * (b - HB) + 2)
                pool.indirect_dma_start(xr[b % HB][:, :], None, dram["xn_scr"], bass.IndirectOffsetOnAxis(ap=rows_of[:, b:b + 1], axis=0)).then_inc(x_ld[b % HB], 16)

            for b in range(USED_MIN):
                gather(b)
            for t in range(USED_MIN // HB, NT):
                with pool.If(used + 1 > t):
                    for i in range(HB):
                        gather(HB * t + i)

        def steps(eng, first, step, last):
            used = turns_used(eng)
            first()
            with eng.Fori(0, MAX_TURNS) as t, eng.If(t < used):
                step(t * HB + 1, 1, t)
                step(t * HB + 2, 0, t + 1)
            last(used * HB + 1, used)

        @block.scalar
        def _(act):
            act.wait_ge(ld, 64)
            yb = dram["ybuf"].rearrange("(b p) d -> b p d", p=P)

            def silu(b, i):
                act.wait_ge(hr, b)
                act.wait_ge(gd, b + 1)
                act.activation(sg[i][:, :], bank[2][:, :], ACT.Silu).then_inc(sil, 1)

            def outputs(b, i, k, stored=None):
                act.wait_ge(ht, b + 1)
                act.activation(hT[i][:, :, :], bank[4][:, :].rearrange("p (k n) -> p k n", k=FT), ACT.Copy).then_inc(ht_t, 1)
                act.wait_ge(y_st[i], k * 16)
                for j in range(2):
                    act.wait_ge(yd, b * 2 + j + 1)
                    act.activation(y[i][:, j * 512:(j + 1) * 512], bank[5 + j][:, :], ACT.Copy).then_inc(y_t, 1)
                dst = yb[b] if isinstance(b, int) else yb[bass.ds(b, 1)].squeeze(0)
                act.wait_ge(y_t, b * 2 + 2)
                act.dma_start(dst, y[i][:, :]).then_inc(stored or y_st[i], 16)

            def step(b, i, k):
                silu(b, i)
                outputs(b - 1, 1 - i, k if i else k - 1)

            def last(b, k):
                silu(b, 1)
                outputs(b - 1, 0, k, y_end)
                outputs(b, 1, k, y_end)
                act.wait_ge(y_end, 32)

            steps(act, lambda: silu(0, 0), step, last)

        @block.vector
        def _(dve):
            dve.wait_ge(ld, 64)
            ch = Chain(dve, lists)

            def do(f, *a):
                ch.post(f(*a))
                ch.wait()

            places = destf[:, :, :].rearrange("p k c -> p (k c)")
            pairs = 2 * NCH
            do(dve.tensor_scalar, blk[:, :], places, 1.0 / P, 0.5 / P - 0.5, ALU.mult, ALU.add)
            do(dve.tensor_scalar, blk[:, :], blk[:, :], WHOLE, None, ALU.add)
            do(dve.tensor_scalar, blk[:, :], blk[:, :], -WHOLE, None, ALU.add)
            do(dve.scalar_tensor_tensor, off[:, :], blk[:, :], -float(P), places, ALU.mult, ALU.add)
            do(dve.tensor_tensor, in_blk[:, :, :], bc(iota[:, 0:NB], 1, pairs), bc(blk[:, :], 2, NB), ALU.is_equal)
            for k in range(2):
                kk = slice(k * NCH, (k + 1) * NCH)
                do(dve.tensor_tensor, in_blk[:, kk, :], in_blk[:, kk, :], bc(tok[:, :], 2, NB), ALU.mult)
            for q in range(0, pairs, 8):
                dve.tensor_tensor(at_row[:, q:q + 8, :], bc(iota[:, :], 1, 8), bc(off[:, q:q + 8], 2, P), ALU.is_equal).then_inc(marked, 1)
            dve.wait_ge(listed, 1)
            dve.tensor_copy(rows_of[:, :], bank[7][:, 0:NB]).then_inc(rows_ok, 1)

            def product(b, i):
                dve.wait_ge(sil, b + 1)
                dve.wait_ge(ud, b + 1)
                dve.tensor_tensor(sg[i][:, :], sg[i][:, :], bank[3][:, :], ALU.mult).then_inc(hr, 1)

            def turn_x(b, i):
                for j in range(2):
                    dve.wait_ge(xt, b * 2 + j + 1)
                    dve.tensor_tensor(xT[i][:, 4 * j:4 * j + 4, :], bank[j][:, :].rearrange("p (k n) -> p k n", k=4),
                                      bc(gf[:, 4 * j:4 * j + 4], 2, P), ALU.mult).then_inc(xt_t, 1)

            def step(b, i, k):
                product(b, i)
                turn_x(b + 1, 1 - i)

            def first():
                turn_x(0, 0)
                step(0, 0, 0)

            steps(dve, first, step, lambda b, k: product(b, 1))

        @block.tensor
        def _(pe):
            pe.wait_ge(ld, 64)
            for q in range(2 * NCH):
                if q % 8 == 0:
                    pe.wait_ge(marked, q // 8 + 1)
                ins = pe.matmul(bank[7][:, 0:NB], at_row[:, q, :], in_blk[:, q, :], start=(q == 0), stop=(q == 2 * NCH - 1))
            ins.then_inc(listed, 1)

            def turn_x(b, i, k):
                pe.wait_ge(x_ld[i], k * 16 + 16)
                pe.wait_ge(xt_t, b * 2)
                for j in range(2):
                    for n in range(4):
                        kt = 4 * j + n
                        ins = pe.transpose(bank[j][:, n * P:(n + 1) * P], xr[i][:, kt * P:(kt + 1) * P], ident[:, :])
                    ins.then_inc(xt, 1)

            def expert_of(b):
                u = pe.value_load(plan[0:1, bass.ds(b, 1)], min_val=0, max_val=NE - 1)
                for j in range(SLOTS):
                    pe.wait_ge(w_ld[j], (u + (SLOTS - j) % SLOTS) // SLOTS * 48)
                return u % SLOTS

            def gate_up(b, i):
                pe.wait_ge(xt_t, b * 2 + 2)
                at = expert_of(b)
                for w, used, o, done in ((wg, sil, 2, gd), (wu, hr, 3, ud)):
                    pe.wait_ge(used, b)
                    for kt in range(KT):
                        ins = pe.matmul(bank[o][:, :], xT[i][:, kt, :], w[:, bass.ds(at, 1), kt, :].squeeze(1), start=(kt == 0), stop=(kt == KT - 1))
                    ins.then_inc(done, 1)

            def turn_h(b, i):
                pe.wait_ge(hr, b + 1)
                pe.wait_ge(ht_t, b)
                for n in range(FT):
                    ins = pe.transpose(bank[4][:, n * P:(n + 1) * P], sg[i][:, n * P:(n + 1) * P], ident[:, :])
                ins.then_inc(ht, 1)

            def down(b, i, at):
                pe.wait_ge(ht_t, b + 1)
                pe.wait_ge(y_t, b * 2)
                for j in range(2):
                    for n in range(FT):
                        ins = pe.matmul(bank[5 + j][:, :], hT[i][:, n, :], wd[:, bass.ds(at, 1), n, j * 512:(j + 1) * 512].squeeze(1), start=(n == 0), stop=(n == FT - 1))
                    ins.then_inc(yd, 1)

            def slot_of(b):
                return pe.value_load(plan[0:1, bass.ds(b, 1)], min_val=0, max_val=NE - 1) % SLOTS

            def step(b, i, k):
                gate_up(b, i)
                turn_h(b - 1, 1 - i)
                turn_x(b + 1, 1 - i, k + 1 if i else k)
                down(b - 1, 1 - i, slot_of(b - 1))

            def first():
                turn_x(0, 0, 0)
                pe.wait_ge(xt_t, 2)
                for w, loaded, o, done in ((wg, first_ld[0], 2, gd), (wu, first_ld[1], 3, ud)):
                    pe.wait_ge(loaded, 16)
                    for kt in range(KT):
                        ins = pe.matmul(bank[o][:, :], xT[0][:, kt, :], w[:, 0, kt, :], start=(kt == 0), stop=(kt == KT - 1))
                    ins.then_inc(done, 1)
                turn_x(1, 1, 0)
                pe.wait_ge(first_ld[2], 16)

            def last(b, k):
                gate_up(b, 1)
                turn_h(b - 1, 0)
                down(b - 1, 0, slot_of(b - 1))
                turn_h(b, 1)
                down(b, 1, slot_of(b))

            steps(pe, first, step, last)


def combine(nc, env, dram, gates, dest):
    with ExitStack() as ctx:
        def sb(name, shape, dt=F32):
            return ctx.enter_context(nc.sbuf_tensor(name, shape, dt))

        sem = nc.alloc_semaphore
        R = 4
        NTR = NCH // R
        H = [sb(f"hf{i}", [P, D]) for i in range(R)]
        Y = [[sb(f"yf{k}{i}", [P, D]) for i in range(R)] for k in range(2)]
        junk = sb("junk_f", [P, D])
        gb = sb("g_final", [P, D])
        nhalf = sb("nhalf_f", [P, 2])
        ss, ms, rs = (sb(n, [P, R]) for n in ("ss_f", "ms_f", "rs_f"))
        ld = sem("f_consts")
        h_ld, y_ld, st = ([sem(f"{n}{i}") for i in range(R)] for n in ("h_in", "y_in", "out_stored"))
        add1, add2, sq, msd, rsd, fin = (sem(n) for n in ("added_one", "added_two", "f_squares", "f_mean", "f_rstd", "f_ready"))
        block = ctx.enter_context(nc.Block())

        @block.sync
        def _(sp):
            hv = dram["h_scr"].rearrange("(t i p) d -> t i p d", i=R, p=P)
            ov = dram["out"][0].rearrange("(t i p) d -> t i p d", i=R, p=P)
            sp.dma_start(nhalf[:, :], dram["cst"][:, K_HALF:K_HALF + 2]).then_inc(ld, 16)
            sp.dma_start(gb[:, :], dram["norm_final_g"].partition_broadcast(P)).then_inc(ld, 16)
            for i in range(R):
                sp.dma_start(H[i][:, :], hv[0, i]).then_inc(h_ld[i], 16)
            with sp.Fori(0, NTR - 1) as t:
                for i in range(R):
                    sp.wait_ge(fin, t * R + i + 1)
                    sp.dma_start(ov[bass.ds(t, 1)].squeeze(0)[i], H[i][:, :]).then_inc(st[i], 16)
                for i in range(R):
                    sp.wait_ge(st[i], t * 16 + 16)
                    sp.dma_start(H[i][:, :], hv[bass.ds(t + 1, 1)].squeeze(0)[i]).then_inc(h_ld[i], 16)
            for i in range(R):
                sp.wait_ge(fin, (NTR - 1) * R + i + 1)
                sp.dma_start(ov[NTR - 1, i], H[i][:, :]).then_inc(st[i], 16)
            for i in range(R):
                sp.wait_ge(st[i], 16 * NTR)

        @block.gpsimd
        def _(pool):
            pool.wait_ge(ld, 32)

            def rstd(c):
                pool.wait_ge(msd, c + 1)
                pool.tensor_tensor(rs[:, c % R:c % R + 1], ms[:, c % R:c % R + 1], nhalf[:, 0:1], ALU.pow).then_inc(rsd, 1)

            for c in range(NCH):
                if c >= R:
                    rstd(c - R)
                    pool.wait_ge(add2, c - R + 1)
                for k in range(2):
                    pool.indirect_dma_start(Y[k][c % R][:, :], None, dram["ybuf"], bass.IndirectOffsetOnAxis(ap=dest[:, k, c:c + 1], axis=0)).then_inc(y_ld[c % R], 16)
            for c in range(NCH - R, NCH):
                rstd(c)

        @block.scalar
        def _(act):
            with act.Fori(0, NTR) as t:
                for i in range(R):
                    act.wait_ge(add2, t * R + i + 1)
                    act.wait_ge(sq, t * R + i)
                    act.activation(junk[:, :], H[i][:, :], ACT.Square, accum_out=ss[:, i:i + 1]).then_inc(sq, 1)

        @block.vector
        def _(dve):
            dve.wait_ge(ld, 32)
            with dve.Fori(0, NTR) as t:
                def norm(i):
                    dve.wait_ge(sq, t * R + i + 1)
                    dve.tensor_scalar(ms[:, i:i + 1], ss[:, i:i + 1], 1.0 / D, EPS, ALU.mult, ALU.add).then_inc(msd, 1)
                    dve.wait_ge(rsd, t * R + i + 1)
                    dve.scalar_tensor_tensor(H[i][:, :], H[i][:, :], rs[:, i:i + 1], gb[:, :], ALU.mult, ALU.mult).then_inc(fin, 1)

                for i in range(R):
                    dve.wait_ge(h_ld[i], t * 16 + 16)
                    dve.wait_ge(y_ld[i], t * 32 + 32)
                    g = [gates[:, k, bass.ds(t * R + i, 1)] for k in range(2)]
                    dve.scalar_tensor_tensor(H[i][:, :], Y[0][i][:, :], g[0], H[i][:, :], ALU.mult, ALU.add).then_inc(add1, 1)
                    dve.wait_ge(add1, t * R + i + 1)
                    dve.scalar_tensor_tensor(H[i][:, :], Y[1][i][:, :], g[1], H[i][:, :], ALU.mult, ALU.add).then_inc(add2, 1)
                    if i:
                        norm(i - 1)
                norm(R - 1)


def program(nc, dram):
    env = {"dve_a": 91, "s5_turn": 32, "s5_marks": (4, 13), "dve_c": 12, "r_marks": (6, 13)}
    held = mixer_projections(nc, env, dram)
    with ExitStack() as ctx:
        def sb(name, shape, dt=F32):
            return ctx.enter_context(nc.sbuf_tensor(name, shape, dt))

        logits, gates = sb("logits", [P, NCH, NGR + NE]), sb("gates", [P, 2, NCH])
        dest, destf = sb("dest", [P, 2, NCH], U32), sb("destf", [P, 2, NCH])
        plan = sb("plan", [1, PL_END], I32)
        with ExitStack() as kept:
            keys_t = kept.enter_context(nc.sbuf_tensor("keysT", [P, KT, MEM], F32))
            values = kept.enter_context(nc.sbuf_tensor("values", [P, MT, D], F32))
            wq = kept.enter_context(nc.sbuf_tensor("w_cq_t", [P, 2, KT, D], F16))
            s5_mixer(nc, env, dram, held, keys_t, values, wq)
            nc.extend_free_semaphores([s.num for s in held])
            cross_and_router(nc, env, dram, keys_t, values, wq, logits)
        route(nc, env, dram, logits, gates, dest, destf, plan)
        experts(nc, env, dram, destf, plan)
        combine(nc, env, dram, gates, dest)


_INS = ["x", "mem", "norm_mix_g", "w_in", "ret_gn_g", "ssd_conv_w", "ssd_conv_b", "ssd_dt_bias", "ssd_A_log", "ssd_D",
        "ssd_norm_g", "s5_A_re", "s5_A_im", "s5_B_re", "s5_B_im", "s5_C_re", "s5_C_im", "s5_log_step", "s5_D", "s5_w_glu",
        "s5_b_glu", "w_out", "norm_cross_g", "mem_norm_g", "w_cq", "w_ck", "w_cv", "w_co", "norm_ffn_g", "w_route_group",
        "b_route_group", "w_route_expert", "b_route_expert", "w_gate", "w_up", "w_down", "norm_final_g"]
_SCRATCH = {"cat": (T, D), "u_scr": (T, S5W), "h_scr": (T, D), "xn_scr": (T, D), "ybuf": (ROWS, D)}


def kernel(**inputs):
    import concourse.bacc as _bacc
    from concourse.bass_utils import run_bass_kernel_spmd as _run

    nc = _bacc.Bacc("TRN2", target_bir_lowering=False, num_devices=1)
    table, rope = constants()
    sent = {name: inputs[name] for name in _INS} | {"cst": table, "rope": rope}
    arrays, dram = {}, {}
    for name, a in sent.items():
        a = np.ascontiguousarray(a)
        arrays[f"in_{name}"] = a
        dram[name] = nc.dram_tensor(f"in_{name}", a.shape, mybir.dt.from_np(a.dtype), kind="ExternalInput").ap()
    for name, shape in _SCRATCH.items():
        dram[name] = nc.dram_tensor(f"scratch_{name}", shape, F32, kind="Internal").ap()
    dram["out"] = nc.dram_tensor("out_0", (1, T, D), F32, kind="ExternalOutput").ap()
    program(nc, dram)
    r = _run(nc, [arrays], core_ids=[0])
    return r.results[0]["out_0"]
```
